# Optimizing a Trainium2 kernel written in Bass

```python
import math
import jax, jax.numpy as jnp
from jax import lax
import numpy as np

D_MODEL = 1024
BATCH = 1
SEQ = 256
DEPTH = 2

CTX_LEN = 256
GRID_W = 64
EPS = 1e-6

BR_WIDTH = D_MODEL // 2
N_BRANCH = 3

DA_SUB = 64
DA_VDIM = 2 * DA_SUB
DA_HEADS = BR_WIDTH // DA_VDIM
DA_QK = DA_HEADS * 2 * DA_SUB
BLOCK_Q = 128
ROPE_BASE = 10000.0
ROPE_NF = DA_SUB // 4

HY_WIDTH = BR_WIDTH
HY_SHORT = 3
HY_BANDS = 16
HY_EMB = 1 + 2 * HY_BANDS
HY_HIDDEN = 64
HY_TARGET = 1e-2
HY_FAST_DECAY = 0.3
HY_SLOW_DECAY = 1.5
HY_MIN_DECAY = math.log(HY_TARGET) / HY_SLOW_DECAY
HY_MAX_DECAY = math.log(HY_TARGET) / HY_FAST_DECAY

GM_WIDTH = BR_WIDTH
GM_GROUPS = 8
GM_CHUNK = 128

COL_K = 0
COL_V = COL_K + DA_QK
COL_Q = COL_V + BR_WIDTH
COL_GA = COL_Q + DA_QK
COL_HY = COL_GA + BR_WIDTH
COL_GB = COL_HY + 3 * HY_WIDTH
COL_GM = COL_GB + BR_WIDTH
COL_GC = COL_GM + 2 * GM_WIDTH
COL_MG = COL_GC + BR_WIDTH
COL_END = COL_MG + N_BRANCH * D_MODEL


def rms_norm(x, g):
    xf = x.astype(jnp.float32)
    y = xf * lax.rsqrt(jnp.mean(xf * xf, axis=-1, keepdims=True) + EPS)
    return (y * g.astype(jnp.float32)).astype(x.dtype)

def layer_norm(x, g, b):
    xf = x.astype(jnp.float32)
    mu = jnp.mean(xf, axis=-1, keepdims=True)
    var = jnp.mean(jnp.square(xf - mu), axis=-1, keepdims=True)
    y = (xf - mu) * lax.rsqrt(var + EPS)
    return (y * g.astype(jnp.float32) + b.astype(jnp.float32)).astype(x.dtype)

def modulation(cond, w, b):
    m = jax.nn.silu(cond) @ w + b
    return jnp.split(m, 3, axis=-1)

def axial_rope(row, col):
    inv = ROPE_BASE ** (-jnp.arange(ROPE_NF, dtype=jnp.float32) / ROPE_NF)
    ang = jnp.stack([row[:, None] * inv, col[:, None] * inv], axis=1)
    return jnp.cos(ang), jnp.sin(ang)

def apply_rope(x, cos, sin):
    xr = x.reshape(*x.shape[:-1], 2, 2, ROPE_NF)
    x1, x2 = xr[..., 0, :], xr[..., 1, :]
    cs, sn = cos.astype(x.dtype), sin.astype(x.dtype)
    out = jnp.stack([x1 * cs - x2 * sn, x2 * cs + x1 * sn], axis=-2)
    return out.reshape(x.shape)

def qk_heads(zs):
    b, n, _ = zs.shape
    return zs.reshape(b, n, DA_HEADS, 2, DA_SUB).transpose(0, 2, 3, 1, 4)

def v_heads(zs):
    b, n, _ = zs.shape
    return zs.reshape(b, n, DA_HEADS, DA_VDIM).transpose(0, 2, 1, 3)

def diff_attend(q, k, v, lam):
    b, h, _, n, _ = q.shape
    nb = n // BLOCK_Q
    qb = q.reshape(b, h, 2, nb, BLOCK_Q, DA_SUB).transpose(3, 0, 1, 2, 4, 5)
    scale = DA_SUB ** -0.5

    def one(qi):
        s = jnp.einsum('bhmqd,bhmkd->bhmqk', qi, k).astype(jnp.float32) * scale
        p = jax.nn.softmax(s, axis=-1)
        w = p[:, :, 0] - lam * p[:, :, 1]
        return jnp.einsum('bhqk,bhkd->bhqd', w.astype(v.dtype), v)

    o = lax.map(one, qb)
    return o.transpose(1, 2, 0, 3, 4).reshape(b, h, n, DA_VDIM)

def diff_head_out(o, g, lam_init):
    o = rms_norm(o, g) * (1.0 - lam_init)
    b, _, n, _ = o.shape
    return o.transpose(0, 2, 1, 3).reshape(b, n, BR_WIDTH)

def hyena_filter(L, w1, b1, w2, b2, w3, freq):
    f32 = jnp.float32
    t = jnp.linspace(0.0, 1.0, L, dtype=f32)[:, None]
    wpos = (2.0 * math.pi / L) * jnp.arange(L, dtype=f32)[:, None]
    bands = jnp.linspace(1e-4, HY_BANDS - 1, HY_BANDS, dtype=f32)[None, :]
    z = jnp.concatenate([t, jnp.cos(bands * wpos), -jnp.sin(bands * wpos)], axis=-1)
    hid = jnp.sin(freq[0].astype(f32) * (z @ w1.astype(f32) + b1.astype(f32)))
    hid = jnp.sin(freq[1].astype(f32) * (hid @ w2.astype(f32) + b2.astype(f32)))
    h = (hid @ w3.astype(f32)).reshape(L, 2, HY_WIDTH)
    deltas = jnp.abs(jnp.linspace(HY_MIN_DECAY, HY_MAX_DECAY, HY_WIDTH, dtype=f32))
    return h * jnp.exp(-t * deltas)[:, None, :]

def long_conv_bidir(u, h, bias):
    L = u.shape[1]
    f32 = jnp.float32
    k = jnp.concatenate([h[:, 0], jnp.zeros((1, HY_WIDTH), f32), h[:0:-1, 1]], axis=0)
    k = k * lax.rsqrt(jnp.sum(k * k, axis=0, keepdims=True))
    kf = jnp.fft.rfft(k, n=2 * L, axis=0)
    uf = jnp.fft.rfft(u.astype(f32), n=2 * L, axis=1)
    y = jnp.fft.irfft(uf * kf[None], n=2 * L, axis=1)[:, :L]
    return (y + u.astype(f32) * bias.astype(f32)).astype(u.dtype)

def short_conv(z, w, b):
    n = z.shape[1]
    pad = HY_SHORT // 2
    zp = jnp.pad(z, ((0, 0), (pad, pad), (0, 0)))
    return sum(zp[:, j:j + n] * w[j] for j in range(HY_SHORT)) + b

def hyena_branch(zb, sw, sb, filt, bias):
    zb = short_conv(zb, sw, sb)
    x0, x1, v = jnp.split(zb, 3, axis=-1)
    return x0 * long_conv_bidir(x1 * v, filt, bias)

def gmlp_branch(zg, ln_g, ln_b, ws, bs):
    u, v = jnp.split(jax.nn.gelu(zg, approximate=False), 2, axis=-1)
    v = layer_norm(v, ln_g, ln_b)
    b, n, _ = v.shape
    vr = v.reshape(b, n // GM_CHUNK, GM_CHUNK, GM_GROUPS, GM_WIDTH // GM_GROUPS)
    vm = jnp.einsum('gpq,bcqgd->bcpgd', ws, vr) + bs.T[:, :, None]
    return u * vm.reshape(b, n, GM_WIDTH)

def merge_branches(z, ys, wb, wo):
    out = None
    for i, (y, g0) in enumerate(zip(ys, (COL_GA, COL_GB, COL_GC))):
        gated = y * jax.nn.silu(z[..., g0:g0 + BR_WIDTH])
        sel = jax.nn.sigmoid(z[..., COL_MG + i * D_MODEL:COL_MG + (i + 1) * D_MODEL])
        term = sel * (gated @ wb[i])
        out = term if out is None else out + term
    return out @ wo

def first_inputs(seed: int = 0) -> dict:
    key = jax.random.key(seed)
    ks = jax.random.split(key, 26)
    f32 = jnp.float32
    nrm = lambda k, shape, s: jax.random.normal(k, shape, f32) * s
    D = D_MODEL
    return {
        "x": nrm(ks[0], (BATCH, SEQ, D), 1.0),
        "c": nrm(ks[1], (BATCH, D), 1.0),
        "ctx": nrm(ks[2], (BATCH, CTX_LEN, D), 1.0),
        "c_ctx": nrm(ks[3], (D,), 1.0),
        "ada_w": nrm(ks[4], (DEPTH, D, 3 * D), 0.5 * D ** -0.5),
        "ada_b": nrm(ks[5], (DEPTH, 3 * D), 0.01),
        "norm_pre": 1.0 + nrm(ks[6], (DEPTH, D), 0.05),
        "norm_post": 1.0 + nrm(ks[7], (DEPTH, D), 0.05),
        "w_in": nrm(ks[8], (DEPTH, D, COL_END), D ** -0.5),
        "da_lambda": nrm(ks[9], (DEPTH, 4, DA_SUB), 0.1),
        "da_subln": 1.0 + nrm(ks[10], (DEPTH, DA_VDIM), 0.05),
        "hy_short_w": nrm(ks[11], (DEPTH, HY_SHORT, 3 * HY_WIDTH), HY_SHORT ** -0.5),
        "hy_short_b": nrm(ks[12], (DEPTH, 3 * HY_WIDTH), 0.02),
        "hy_f_w1": nrm(ks[13], (DEPTH, HY_EMB, HY_HIDDEN), HY_EMB ** -0.5),
        "hy_f_b1": nrm(ks[14], (DEPTH, HY_HIDDEN), 0.1),
        "hy_f_w2": nrm(ks[15], (DEPTH, HY_HIDDEN, HY_HIDDEN), HY_HIDDEN ** -0.5),
        "hy_f_b2": nrm(ks[16], (DEPTH, HY_HIDDEN), 0.1),
        "hy_f_w3": nrm(ks[17], (DEPTH, HY_HIDDEN, 2 * HY_WIDTH), HY_HIDDEN ** -0.5),
        "hy_f_freq": 1.0 + nrm(ks[18], (DEPTH, 2, HY_HIDDEN), 0.1),
        "hy_bias": nrm(ks[19], (DEPTH, HY_WIDTH), 0.5),
        "gm_ln_g": 1.0 + nrm(ks[20], (DEPTH, GM_WIDTH), 0.05),
        "gm_ln_b": nrm(ks[21], (DEPTH, GM_WIDTH), 0.02),
        "gm_ws": nrm(ks[22], (DEPTH, GM_GROUPS, GM_CHUNK, GM_CHUNK), 0.5 * GM_CHUNK ** -0.5),
        "gm_bs": 1.0 + nrm(ks[23], (DEPTH, GM_GROUPS, GM_CHUNK), 0.1),
        "w_branch": nrm(ks[24], (DEPTH, N_BRANCH, BR_WIDTH, D), BR_WIDTH ** -0.5),
        "w_out": nrm(ks[25], (DEPTH, D, D), D ** -0.5),
    }

def first_block(x, c, ctx, c_ctx, ada_w, ada_b, norm_pre, norm_post, w_in, da_lambda, da_subln,
              hy_short_w, hy_short_b, hy_f_w1, hy_f_b1, hy_f_w2, hy_f_b2, hy_f_w3, hy_f_freq, hy_bias,
              gm_ln_g, gm_ln_b, gm_ws, gm_bs, w_branch, w_out):
    n = x.shape[1]
    n_ctx = ctx.shape[1]
    rows = n // GRID_W
    row = jnp.repeat(jnp.arange(rows, dtype=jnp.float32), GRID_W)
    col = jnp.tile(jnp.arange(GRID_W, dtype=jnp.float32), rows)
    cos, sin = axial_rope(row, col)
    xc = ctx
    for l in range(DEPTH):
        last = l == DEPTH - 1
        lam_init = 0.8 - 0.6 * math.exp(-0.3 * l)
        lp = da_lambda[l].astype(jnp.float32)
        lam = jnp.exp(jnp.sum(lp[0] * lp[1])) - jnp.exp(jnp.sum(lp[2] * lp[3])) + lam_init

        sh, sc, gt = modulation(c, ada_w[l], ada_b[l])
        shc, scc, gtc = modulation(c_ctx, ada_w[l], ada_b[l])
        h = rms_norm(x, norm_pre[l]) * (1.0 + sc[:, None]) + sh[:, None]
        hc = rms_norm(xc, norm_pre[l]) * (1.0 + scc) + shc

        z = h @ w_in[l]
        zc = hc @ (w_in[l][:, :COL_Q] if last else w_in[l])
        kc = qk_heads(zc[..., COL_K:COL_V])
        vc = v_heads(zc[..., COL_V:COL_Q])

        q = apply_rope(qk_heads(z[..., COL_Q:COL_GA]), cos, sin)
        k = apply_rope(qk_heads(z[..., COL_K:COL_V]), cos, sin)
        v = v_heads(z[..., COL_V:COL_Q])
        k_all = jnp.concatenate([k, kc], axis=3)
        v_all = jnp.concatenate([v, vc], axis=2)
        y_a = diff_head_out(diff_attend(q, k_all, v_all, lam), da_subln[l], lam_init)
        filt = hyena_filter(n, hy_f_w1[l], hy_f_b1[l], hy_f_w2[l], hy_f_b2[l], hy_f_w3[l], hy_f_freq[l])
        y_b = hyena_branch(z[..., COL_HY:COL_GB], hy_short_w[l], hy_short_b[l], filt, hy_bias[l])
        y_c = gmlp_branch(z[..., COL_GM:COL_GC], gm_ln_g[l], gm_ln_b[l], gm_ws[l], gm_bs[l])
        out = merge_branches(z, (y_a, y_b, y_c), w_branch[l], w_out[l])
        x_new = x + gt[:, None] * rms_norm(out, norm_post[l])

        if not last:
            qc = qk_heads(zc[..., COL_Q:COL_GA])
            yc_a = diff_head_out(diff_attend(qc, kc, vc, lam), da_subln[l], lam_init)
            filt_c = hyena_filter(n_ctx, hy_f_w1[l], hy_f_b1[l], hy_f_w2[l], hy_f_b2[l], hy_f_w3[l], hy_f_freq[l])
            yc_b = hyena_branch(zc[..., COL_HY:COL_GB], hy_short_w[l], hy_short_b[l], filt_c, hy_bias[l])
            yc_c = gmlp_branch(zc[..., COL_GM:COL_GC], gm_ln_g[l], gm_ln_b[l], gm_ws[l], gm_bs[l])
            outc = merge_branches(zc, (yc_a, yc_b, yc_c), w_branch[l], w_out[l])
            xc = xc + gtc * rms_norm(outc, norm_post[l])
        x = x_new
    return x


DEPTH_2 = 1

HEAD_DIM = 64
ROPE_DIM = HEAD_DIM // 4
ROPE_THETA = 500000.0
NORM_EPS = 1e-6
ATTN_SCALE = HEAD_DIM ** -0.5

NSA_HEADS = 8
NSA_GROUPS = 2
NSA_REP = NSA_HEADS // NSA_GROUPS
CMP_LEN = 32
CMP_STRIDE = 16
CMP_HIDDEN = 256
SEL_BLOCK = 64
SEL_TOPN = 8
WINDOW = 512
WIN_QBLOCK = 128
NSA_QCHUNK = 64

MOBA_HEADS = 8
MOBA_BLOCK = 256
MOBA_TOPK = 3
MOBA_QCHUNK = 16

PAD_MULT = 256
D_FF = ((-(-8 * D_MODEL // 3)) + 255) // 256 * 256
PLE_DIM = 256

IN_SPLITS = ((NSA_HEADS * HEAD_DIM,) + (NSA_GROUPS * HEAD_DIM,) * 6 + (3 * NSA_HEADS,)
             + (MOBA_HEADS * HEAD_DIM,) * 3 + (D_MODEL, D_MODEL))
IN_COLS = sum(IN_SPLITS)
IN_CUTS = tuple(int(c) for c in np.cumsum(IN_SPLITS)[:-1])


def rms_norm_2(x, g):
    xf = x.astype(jnp.float32)
    y = xf * lax.rsqrt(jnp.mean(xf * xf, axis=-1, keepdims=True) + NORM_EPS)
    return (y * g.astype(jnp.float32)).astype(x.dtype)

def partial_rope(t, pos):
    half = ROPE_DIM // 2
    inv_freq = ROPE_THETA ** (-jnp.arange(half, dtype=jnp.float32) / half)
    ang = pos.astype(jnp.float32)[..., None] * inv_freq
    cos, sin = jnp.cos(ang), jnp.sin(ang)
    tr = t[..., :ROPE_DIM].astype(jnp.float32)
    t1, t2 = tr[..., :half], tr[..., half:]
    rot = jnp.concatenate([t1 * cos - t2 * sin, t2 * cos + t1 * sin], axis=-1)
    return jnp.concatenate([rot.astype(t.dtype), t[..., ROPE_DIM:]], axis=-1)

def masked_softmax(scores, mask):
    s = jnp.where(mask, scores.astype(jnp.float32), -jnp.inf)
    m = jnp.max(s, axis=-1, keepdims=True)
    m = jnp.where(jnp.isfinite(m), m, 0.0)
    e = jnp.where(mask, jnp.exp(s - m), 0.0)
    return e / jnp.maximum(jnp.sum(e, axis=-1, keepdims=True), 1e-30)

def to_heads(t, n):
    b, s, _ = t.shape
    return t.reshape(b, s, n, HEAD_DIM).transpose(0, 2, 1, 3)

def from_heads(t):
    b, n, s, d = t.shape
    return t.transpose(0, 2, 1, 3).reshape(b, s, n * d)

def compress_blocks(t, pe, w1, w2):
    b, g, sp, d = t.shape
    n_sub, per = sp // CMP_STRIDE, CMP_LEN // CMP_STRIDE
    sub = t.reshape(b, g, n_sub, CMP_STRIDE, d)
    nc = n_sub - per + 1
    blocks = jnp.concatenate([sub[:, :, i:i + nc] for i in range(per)], axis=3)
    flat = (blocks + pe).reshape(b, g, nc, CMP_LEN * d)
    return jax.nn.silu(flat @ w1) @ w2

def nsa_mixer(q_in, kc_in, vc_in, ks_in, vs_in, kw_in, vw_in, gate_in, pos_pad,
              q_gain, kc_gain, ks_gain, kw_gain, pe_k, pe_v, ck_w1, ck_w2, cv_w1, cv_w2):
    b, sp, _ = q_in.shape
    G, R, dh = NSA_GROUPS, NSA_REP, HEAD_DIM
    pos_h = pos_pad[:, None, :]
    t_idx = jnp.arange(sp)
    q = partial_rope(rms_norm_2(to_heads(q_in, NSA_HEADS), q_gain), pos_h).reshape(b, G, R, sp, dh)

    kc = rms_norm_2(compress_blocks(to_heads(kc_in, G), pe_k, ck_w1, ck_w2), kc_gain)
    vc = compress_blocks(to_heads(vc_in, G), pe_v, cv_w1, cv_w2)
    nc = kc.shape[2]
    cmp_start = jnp.arange(nc) * CMP_STRIDE
    cmp_end = cmp_start + CMP_LEN - 1
    kc = partial_rope(kc, pos_pad[:, cmp_end][:, None, :])
    s_c = jnp.einsum('bgrtd,bgcd->bgrtc', q, kc) * ATTN_SCALE
    p_c = masked_softmax(s_c, cmp_end[None, :] <= t_idx[:, None])
    o_c = jnp.einsum('bgrtc,bgcd->bgrtd', p_c.astype(vc.dtype), vc)

    ns = sp // SEL_BLOCK
    j = jnp.arange(ns)
    overlap = ((cmp_start[:, None] <= j[None, :] * SEL_BLOCK + SEL_BLOCK - 1)
               & (cmp_end[:, None] >= j[None, :] * SEL_BLOCK)).astype(jnp.float32)
    imp = jnp.einsum('bgrtc,cj->bgtj', p_c, overlap)
    cur = (t_idx // SEL_BLOCK)[:, None]
    forced = (j[None, :] == 0) | (j[None, :] == cur) | (j[None, :] == cur - 1)
    imp = jnp.where(forced, jnp.inf, jnp.where(j[None, :] > cur, -jnp.inf, imp))
    n_top = min(SEL_TOPN, ns)
    _, sel_idx = lax.top_k(imp, n_top)

    ks = partial_rope(rms_norm_2(to_heads(ks_in, G), ks_gain), pos_h)
    vs = to_heads(vs_in, G)
    ks_blk = ks.reshape(b, G, ns, SEL_BLOCK, dh)
    vs_blk = vs.reshape(b, G, ns, SEL_BLOCK, dh)
    nq = sp // NSA_QCHUNK
    bi = jnp.arange(b)[:, None, None, None]
    gi = jnp.arange(G)[None, :, None, None]
    m_sel = n_top * SEL_BLOCK

    def sel_chunk(args):
        qc, ic, tc = args
        kg = ks_blk[bi, gi, ic].reshape(b, G, NSA_QCHUNK, m_sel, dh)
        vg = vs_blk[bi, gi, ic].reshape(b, G, NSA_QCHUNK, m_sel, dh)
        kpos = (ic[..., None] * SEL_BLOCK + jnp.arange(SEL_BLOCK)).reshape(b, G, NSA_QCHUNK, m_sel)
        mask = (kpos <= tc[None, None, :, None])[:, :, None]
        s = jnp.einsum('bgrcd,bgcmd->bgrcm', qc, kg) * ATTN_SCALE
        pr = masked_softmax(s, mask)
        return jnp.einsum('bgrcm,bgcmd->bgrcd', pr.astype(vg.dtype), vg)

    q_ch = q.reshape(b, G, R, nq, NSA_QCHUNK, dh).transpose(3, 0, 1, 2, 4, 5)
    idx_ch = sel_idx.reshape(b, G, nq, NSA_QCHUNK, n_top).transpose(2, 0, 1, 3, 4)
    o_s = lax.map(sel_chunk, (q_ch, idx_ch, t_idx.reshape(nq, NSA_QCHUNK)))
    o_s = o_s.transpose(1, 2, 3, 0, 4, 5).reshape(b, G, R, sp, dh)

    kw = partial_rope(rms_norm_2(to_heads(kw_in, G), kw_gain), pos_h)
    vw = to_heads(vw_in, G)
    nw, nprev = sp // WIN_QBLOCK, WINDOW // WIN_QBLOCK
    band = (nprev + 1) * WIN_QBLOCK

    def banded(t):
        tb = jnp.pad(t.reshape(b, G, nw, WIN_QBLOCK, dh), ((0, 0), (0, 0), (nprev, 0), (0, 0), (0, 0)))
        return jnp.concatenate([tb[:, :, i:i + nw] for i in range(nprev + 1)], axis=3).transpose(2, 0, 1, 3, 4)

    def win_block(args):
        qb, kb, vb, w = args
        qpos = w * WIN_QBLOCK + jnp.arange(WIN_QBLOCK)
        kpos = (w - nprev) * WIN_QBLOCK + jnp.arange(band)
        diff = qpos[:, None] - kpos[None, :]
        mask = (diff >= 0) & (diff < WINDOW) & (kpos[None, :] >= 0)
        s = jnp.einsum('bgrqd,bgkd->bgrqk', qb, kb) * ATTN_SCALE
        pr = masked_softmax(s, mask)
        return jnp.einsum('bgrqk,bgkd->bgrqd', pr.astype(vb.dtype), vb)

    q_w = q.reshape(b, G, R, nw, WIN_QBLOCK, dh).transpose(3, 0, 1, 2, 4, 5)
    o_w = lax.map(win_block, (q_w, banded(kw), banded(vw), jnp.arange(nw)))
    o_w = o_w.transpose(1, 2, 3, 0, 4, 5).reshape(b, G, R, sp, dh)

    g = jax.nn.sigmoid(gate_in.reshape(b, sp, NSA_HEADS, 3)).transpose(0, 2, 1, 3).reshape(b, G, R, sp, 3)
    o = g[..., 0:1] * o_c + g[..., 1:2] * o_s + g[..., 2:3] * o_w
    return from_heads(o.reshape(b, NSA_HEADS, sp, dh))

def moba_mixer(q_in, k_in, v_in, pos_pad, q_gain, k_gain):
    b, sp, _ = q_in.shape
    H, dh, BS, C = MOBA_HEADS, HEAD_DIM, MOBA_BLOCK, MOBA_QCHUNK
    pos_h = pos_pad[:, None, :]
    t_idx = jnp.arange(sp)
    q = partial_rope(rms_norm_2(to_heads(q_in, H), q_gain), pos_h)
    k = partial_rope(rms_norm_2(to_heads(k_in, H), k_gain), pos_h)
    v = to_heads(v_in, H)
    nb = sp // BS
    k_blk = k.reshape(b, H, nb, BS, dh)
    v_blk = v.reshape(b, H, nb, BS, dh)
    k_mean = jnp.mean(k_blk.astype(jnp.float32), axis=3)
    score = jnp.einsum('bhtd,bhnd->bhtn', q.astype(jnp.float32), k_mean)
    own = (t_idx // BS)[:, None]
    score = jnp.where(jnp.arange(nb)[None, :] < own, score, -jnp.inf)
    n_top = min(MOBA_TOPK, nb)
    _, sel_idx = lax.top_k(score, n_top)
    bi = jnp.arange(b)[:, None, None, None]
    hi = jnp.arange(H)[None, :, None, None]
    nq = sp // C
    m_sel = n_top * BS

    def chunk(args):
        qc, ic, c = args
        start = c * C
        blk = start // BS
        k_own = lax.dynamic_slice_in_dim(k, blk * BS, BS, axis=2)
        v_own = lax.dynamic_slice_in_dim(v, blk * BS, BS, axis=2)
        qpos = start + jnp.arange(C)
        m_own = jnp.broadcast_to(blk * BS + jnp.arange(BS)[None, :] <= qpos[:, None], (b, H, C, BS))
        m_sel_mask = jnp.broadcast_to((ic < blk)[..., None], (b, H, C, n_top, BS)).reshape(b, H, C, m_sel)
        kg = k_blk[bi, hi, ic].reshape(b, H, C, m_sel, dh)
        vg = v_blk[bi, hi, ic].reshape(b, H, C, m_sel, dh)
        s = jnp.concatenate([jnp.einsum('bhcd,bhpd->bhcp', qc, k_own),
                             jnp.einsum('bhcd,bhcmd->bhcm', qc, kg)], axis=-1) * ATTN_SCALE
        pr = masked_softmax(s, jnp.concatenate([m_own, m_sel_mask], axis=-1)).astype(v.dtype)
        return (jnp.einsum('bhcp,bhpd->bhcd', pr[..., :BS], v_own)
                + jnp.einsum('bhcm,bhcmd->bhcd', pr[..., BS:], vg))

    q_ch = q.reshape(b, H, nq, C, dh).transpose(2, 0, 1, 3, 4)
    idx_ch = sel_idx.reshape(b, H, nq, C, n_top).transpose(2, 0, 1, 3, 4)
    o = lax.map(chunk, (q_ch, idx_ch, jnp.arange(nq)))
    o = o.transpose(1, 2, 0, 3, 4).reshape(b, H, sp, dh)
    return from_heads(o)

def second_inputs(seed: int = 0) -> dict:
    key = jax.random.key(seed)
    ks = jax.random.split(key, 25)

    def normal(k, shape, scale):
        return jax.random.normal(k, shape, jnp.float32) * scale

    def gain(k, n):
        return 1.0 + 0.1 * jax.random.normal(k, (DEPTH_2, n), jnp.float32)

    L, dh = DEPTH_2, HEAD_DIM
    nsa_w, moba_w = NSA_HEADS * dh, MOBA_HEADS * dh
    return {
        'x': normal(ks[0], (BATCH, SEQ, D_MODEL), 1.0),
        'p': normal(ks[1], (DEPTH_2, BATCH, SEQ, PLE_DIM), 1.0),
        'positions': jnp.tile(jnp.arange(SEQ, dtype=jnp.int32)[None, :], (BATCH, 1)),
        'g_mix': gain(ks[2], D_MODEL),
        'w_in': normal(ks[3], (L, D_MODEL, IN_COLS), D_MODEL ** -0.5),
        'nsa_q_gain': gain(ks[4], dh),
        'nsa_kc_gain': gain(ks[5], dh),
        'nsa_ks_gain': gain(ks[6], dh),
        'nsa_kw_gain': gain(ks[7], dh),
        'nsa_pe_k': normal(ks[8], (L, CMP_LEN, dh), 0.1),
        'nsa_pe_v': normal(ks[9], (L, CMP_LEN, dh), 0.1),
        'nsa_ck_w1': normal(ks[10], (L, CMP_LEN * dh, CMP_HIDDEN), (CMP_LEN * dh) ** -0.5),
        'nsa_ck_w2': normal(ks[11], (L, CMP_HIDDEN, dh), CMP_HIDDEN ** -0.5),
        'nsa_cv_w1': normal(ks[12], (L, CMP_LEN * dh, CMP_HIDDEN), (CMP_LEN * dh) ** -0.5),
        'nsa_cv_w2': normal(ks[13], (L, CMP_HIDDEN, dh), CMP_HIDDEN ** -0.5),
        'moba_q_gain': gain(ks[14], dh),
        'moba_k_gain': gain(ks[15], dh),
        'w_up_nsa': normal(ks[16], (L, nsa_w, D_MODEL), nsa_w ** -0.5),
        'w_up_moba': normal(ks[17], (L, moba_w, D_MODEL), moba_w ** -0.5),
        'w_out': normal(ks[18], (L, D_MODEL, D_MODEL), D_MODEL ** -0.5),
        'g_ffn': gain(ks[19], D_MODEL),
        'w_ffn_in': normal(ks[20], (L, D_MODEL, 2 * D_FF), D_MODEL ** -0.5),
        'w_ffn_out': normal(ks[21], (L, D_FF, D_MODEL), D_FF ** -0.5),
        'g_ple': gain(ks[22], D_MODEL),
        'w_ple_gate': normal(ks[23], (L, D_MODEL, D_MODEL), D_MODEL ** -0.5),
        'w_ple_proj': normal(ks[24], (L, PLE_DIM, D_MODEL), PLE_DIM ** -0.5),
    }

def second_block(x, p, positions, g_mix, w_in, nsa_q_gain, nsa_kc_gain, nsa_ks_gain, nsa_kw_gain,
              nsa_pe_k, nsa_pe_v, nsa_ck_w1, nsa_ck_w2, nsa_cv_w1, nsa_cv_w2,
              moba_q_gain, moba_k_gain, w_up_nsa, w_up_moba, w_out,
              g_ffn, w_ffn_in, w_ffn_out, g_ple, w_ple_gate, w_ple_proj):
    b, s, _ = x.shape
    sp = -(-s // PAD_MULT) * PAD_MULT
    extra = jnp.arange(1, sp - s + 1, dtype=positions.dtype)
    pos_pad = jnp.concatenate([positions, positions[:, -1:] + extra[None, :]], axis=1)
    for i in range(DEPTH_2):
        proj = rms_norm_2(x, g_mix[i]) @ w_in[i]
        proj = jnp.pad(proj, ((0, 0), (0, sp - s), (0, 0)))
        (q_n, kc_n, vc_n, ks_n, vs_n, kw_n, vw_n, gate_n,
         q_m, k_m, v_m, gate_a, gate_b) = jnp.split(proj, IN_CUTS, axis=-1)
        y_nsa = nsa_mixer(q_n, kc_n, vc_n, ks_n, vs_n, kw_n, vw_n, gate_n, pos_pad,
                          nsa_q_gain[i], nsa_kc_gain[i], nsa_ks_gain[i], nsa_kw_gain[i],
                          nsa_pe_k[i], nsa_pe_v[i], nsa_ck_w1[i], nsa_ck_w2[i],
                          nsa_cv_w1[i], nsa_cv_w2[i])[:, :s]
        y_moba = moba_mixer(q_m, k_m, v_m, pos_pad, moba_q_gain[i], moba_k_gain[i])[:, :s]
        merged = (jax.nn.sigmoid(gate_a[:, :s]) * (y_nsa @ w_up_nsa[i])
                  + jax.nn.sigmoid(gate_b[:, :s]) * (y_moba @ w_up_moba[i]))
        x = x + merged @ w_out[i]
        gate, up = jnp.split(rms_norm_2(x, g_ffn[i]) @ w_ffn_in[i], 2, axis=-1)
        x = x + (jax.nn.silu(gate) * up) @ w_ffn_out[i]
        ple_gate = jax.nn.sigmoid(rms_norm_2(x, g_ple[i]) @ w_ple_gate[i])
        x = x + ple_gate * (p[i] @ w_ple_proj[i])
    return x


def setup_inputs(seed=0):
    out = dict(first_inputs(seed))
    for name, value in second_inputs(seed + 1).items():
        if name != "x":
            out[name + "_2"] = value
    return out


def reference(
    x, c, ctx, c_ctx, ada_w, ada_b, norm_pre, norm_post, w_in, da_lambda, da_subln, hy_short_w,
    hy_short_b, hy_f_w1, hy_f_b1, hy_f_w2, hy_f_b2, hy_f_w3, hy_f_freq, hy_bias, gm_ln_g,
    gm_ln_b, gm_ws, gm_bs, w_branch, w_out, p_2, positions_2, g_mix_2, w_in_2, nsa_q_gain_2,
    nsa_kc_gain_2, nsa_ks_gain_2, nsa_kw_gain_2, nsa_pe_k_2, nsa_pe_v_2, nsa_ck_w1_2,
    nsa_ck_w2_2, nsa_cv_w1_2, nsa_cv_w2_2, moba_q_gain_2, moba_k_gain_2, w_up_nsa_2,
    w_up_moba_2, w_out_2, g_ffn_2, w_ffn_in_2, w_ffn_out_2, g_ple_2, w_ple_gate_2, w_ple_proj_2,
):
    x = first_block(
        x, c, ctx, c_ctx, ada_w, ada_b, norm_pre, norm_post, w_in, da_lambda, da_subln,
        hy_short_w, hy_short_b, hy_f_w1, hy_f_b1, hy_f_w2, hy_f_b2, hy_f_w3, hy_f_freq, hy_bias,
        gm_ln_g, gm_ln_b, gm_ws, gm_bs, w_branch, w_out,
    )
    return second_block(
        x, p_2, positions_2, g_mix_2, w_in_2, nsa_q_gain_2, nsa_kc_gain_2, nsa_ks_gain_2,
        nsa_kw_gain_2, nsa_pe_k_2, nsa_pe_v_2, nsa_ck_w1_2, nsa_ck_w2_2, nsa_cv_w1_2,
        nsa_cv_w2_2, moba_q_gain_2, moba_k_gain_2, w_up_nsa_2, w_up_moba_2, w_out_2, g_ffn_2,
        w_ffn_in_2, w_ffn_out_2, g_ple_2, w_ple_gate_2, w_ple_proj_2,
    )


_drawn_inputs = setup_inputs


def setup_inputs(seed=0):
    import zlib

    import numpy as np

    out = dict(_drawn_inputs(seed))
    spreads = {}
    factors = {'ada_b': 2.77,
     'da_lambda': 6.628,
     'da_subln': 5.5,
     'hy_short_b': 3.892,
     'gm_ln_g': 8.0,
     'gm_ln_b': 8.0,
     'gm_bs': 3.044,
     'nsa_q_gain_2': 6.534,
     'nsa_kc_gain_2': 8.0,
     'nsa_ks_gain_2': 8.0,
     'nsa_kw_gain_2': 8.0,
     'nsa_pe_k_2': 8.0,
     'nsa_pe_v_2': 3.997,
     'moba_q_gain_2': 6.482,
     'moba_k_gain_2': 7.4,
     'g_ple_2': 3.849}
    for name, (base, spread) in spreads.items():
        noise = np.random.default_rng([zlib.crc32(name.encode()), seed]).standard_normal(out[name].shape)
        drawn = base * np.exp(spread * noise) if base else spread * noise
        out[name] = __import__('jax').numpy.asarray(drawn.astype(out[name].dtype))
    for name, factor in factors.items():
        out[name] = (out[name] * factor).astype(out[name].dtype)
    return out
```

```python
import math
from contextlib import ExitStack, contextmanager

import numpy as np

import concourse.bass as bass
from concourse import mybir

F32 = mybir.dt.float32
F32R = mybir.dt.float32r
I32 = mybir.dt.int32
ACT = mybir.ActivationFunctionType
ALU = mybir.AluOpType
AXX = mybir.AxisListType.X

P = 128
D = 1024
KT = D // P
TOK = 256
ALL = 2 * TOK
BR = 512
BT = BR // P
HEADS = 4
DEPTH = 2
EPS = 1e-6
RAW = 4
SPLIT = 4
AHEAD = 2
D_FF = 2816
FT = D_FF // P
NCMP = 15
NEG = -1e30
TWO_PI = 2.0 * math.pi
MAGIC = 1.5 * 2.0 ** 23
LAYER_TILES = 24 + 4 + 4 + 4 + 12 + 4 + 4 + 12 + 36 + 8
TILES = DEPTH * LAYER_TILES + 8 + 8 + 4 + 4 + 4 + 4 + 24 + 8 + 2 * FT + FT + 8 + 2


def pi_parts():
    parts, rest = [], TWO_PI
    for _ in range(3):
        scale = 2.0 ** (8 - math.ceil(math.log2(rest)))
        part = math.floor(rest * scale) / scale
        parts.append(part)
        rest -= part
    return parts + [float(np.float32(rest))]


class Count:

    def __init__(self, sem):
        self.sem, self.off, self.sym = sem, 0, None

    def value(self, k=0):
        v = self.off + k
        return v if self.sym is None else self.sym + v


class Line:

    def __init__(self, eng, sem):
        self.eng, self.count = eng, Count(sem)

    def mark(self, ins):
        ins.then_inc(self.count.sem, 1)
        self.count.off += 1
        return (self.count, self.count.value())

    def wait(self, *marks):
        for m in marks:
            if m is not None:
                self.eng.wait_ge(m[0].sem, m[1])

    def last(self):
        return (self.count, self.count.value())

    def settle(self):
        self.eng.wait_ge(self.count.sem, self.count.value())


class Program:
    def __init__(self, nc, ctx, ins, out):
        self.nc, self.ctx, self.ins, self.out = nc, ctx, ins, out
        self.act = Line(nc.scalar, self.sem("act"))
        self.dve = Line(nc.vector, self.sem("dve"))
        self.pe = Line(nc.tensor, self.sem("pe"))
        self.hi = Count(self.sem("tile_hi"))
        self.lo = Count(self.sem("tile_lo"))
        self.used = Count(self.sem("tile_used"))
        self.free = Count(self.sem("bank_free"))
        self.arrived = [self.sem(f"tile_arrived{r}") for r in range(RAW)]
        self.split_at = 0
        self.sym_tile = None
        self.loads = {}
        self.G = [ctx.enter_context(nc.psum_tensor(f"gemm_bank{i}", [P, 512], F32)) for i in range(4)]
        self.M = [ctx.enter_context(nc.psum_tensor(f"misc_bank{i}", [P, 512], F32)) for i in range(4)]
        sb = self.sb
        self.raw = sb("raw", [P, RAW, 1024])
        self.whi = sb("whi", [P, SPLIT, 1024], F32R)
        self.wlo = sb("wlo", [P, SPLIT, 1024], F32R)
        self.x = sb("x", [P, KT, ALL])
        self.hhi = sb("hhi", [P, KT, ALL], F32R)
        self.hlo = sb("hlo", [P, KT, ALL], F32R)
        at = nc.sbuf_base
        self.arena = sb("arena", [P, 24, ALL])
        self.arena_r = nc.alloc_sbuf_tensor_at("arena_r", [P, 24, ALL], F32R, offset=at)
        self.y = sb("y", [P, 12, ALL])
        self.tmp = sb("tmp", [P, 5, ALL])
        self.kre, self.kim = self.y[:, 8:10, :], self.y[:, 10:12, :]
        self.wt = self.arena[:, 12:14, :].rearrange("p a (b q) -> p (a b) q", q=TOK)
        self.stat = sb("stat", [P, 40])
        self.hy_rs = sb("hy_rs", [P, BT])

    def sem(self, name):
        return self.ctx.enter_context(self.nc.semaphore(name))

    def sb(self, name, shape, dt=F32):
        return self.ctx.enter_context(self.nc.sbuf_tensor(name, shape, dt))

    def load(self, name, dst=None, src=None, dt=F32, eng=None):
        src = self.ins[name] if src is None else src
        if dst is None:
            dst = self.sb(name + "_sb", list(src.shape), dt)[:]
        s = self.sem("in_" + name)
        (eng or self.nc.scalar).dma_start(dst, src).then_inc(s, 16)
        self.loads[name] = (dst, s)
        return dst

    def need(self, line, *names):
        for n in names:
            line.eng.wait_ge(self.loads[n][1], 16)

    @contextmanager
    def roll(self, n, **step):
        counts = {"act": self.act.count, "dve": self.dve.count, "pe": self.pe.count, "tile": self.used, "bank": self.free}
        start = {k: c.off for k, c in counts.items()}
        hi0, split0 = self.hi.off, self.split_at
        assert step["tile"] % SPLIT == 0 and step.get("bank", 0) % 4 == 0
        eng = (mybir.EngineType.PE, mybir.EngineType.Activation, mybir.EngineType.DVE)
        with self.nc.Fori(0, n, 1, engines=eng) as i:
            for k, c in counts.items():
                c.sym = i * step.get(k, 0) if step.get(k, 0) else None
            self.sym_tile = i * step["tile"]
            self.turns = n
            yield i
        for k, c in counts.items():
            assert c.off == start[k] + step.get(k, 0), (k, c.off - start[k], step.get(k, 0))
            c.off = start[k] + n * step.get(k, 0)
            c.sym = None
        self.split_at = split0 + n * step["tile"]
        self.sym_tile = None

    def plus(self, v):
        return v if self.sym_tile is None else self.sym_tile + v

    def stream(self):
        sp, w, s_lo = self.nc.sync, self.ins["stream"], self.lo.sem
        for r in range(RAW):
            sp.dma_start(self.raw[:, r, :], w[r]).then_inc(self.arrived[r], 16)
        turns, rest = divmod(TILES - RAW, RAW)
        with sp.Fori(0, turns, 1) as i:
            for r in range(RAW):
                sp.wait_ge(s_lo, i * RAW + (r + 1))
                sp.dma_start(self.raw[:, r, :], w[i * RAW + (RAW + r)]).then_inc(self.arrived[r], 16)
        for r in range(rest):
            sp.wait_ge(s_lo, turns * RAW + r + 1)
            sp.dma_start(self.raw[:, r, :], w[turns * RAW + RAW + r]).then_inc(self.arrived[r], 16)

    def split(self):
        if self.sym_tile is None and self.split_at >= TILES:
            return
        t, act, dve = self.split_at, self.nc.scalar, self.nc.vector
        self.split_at += 1
        r, s = t % RAW, t % SPLIT
        turn = self.plus(t - r) if self.sym_tile is not None else t - r
        act.wait_ge(self.arrived[r], turn * (16 // RAW) + 16)
        if t >= SPLIT:
            act.wait_ge(self.used.sem, self.plus(t - SPLIT + 1))
        act.activation(self.whi[:, s, :], self.raw[:, r, :], ACT.Copy).then_inc(self.hi.sem, 1)
        dve.wait_ge(self.hi.sem, self.plus(t + 1))
        dve.tensor_tensor(self.wlo[:, s, :], self.raw[:, r, :], self.whi[:, s, :].bitcast(F32), ALU.subtract).then_inc(self.lo.sem, 1)

    def tile(self, products):
        self.split()
        t = self.used.off
        self.nc.tensor.wait_ge(self.lo.sem, self.plus(t + 1))
        s = t % SPLIT
        last = products(self.whi[:, s, :], self.wlo[:, s, :])
        last.then_inc(self.used.sem, 1)
        self.used.off += 1
        return (self.used, self.used.value())

    def bank(self):
        e = self.free.off
        if e >= 4:
            self.nc.tensor.wait_ge(self.free.sem, self.free.value(-3))
        return self.G[e % 4]

    def release(self, ins):
        ins.then_inc(self.free.sem, 1)
        self.free.off += 1
        return (self.free, self.free.value())

    def three(self, out, w_hi, w_lo, r_hi, r_lo, first, last):
        mm = self.nc.tensor.matmul
        mm(out, w_lo, r_hi, start=first, stop=False)
        mm(out, w_hi, r_lo, start=False, stop=False)
        return mm(out, w_hi, r_hi, start=False, stop=last)

    def feature_tile(self, n, rhs=None, col=0, nk=KT, bank=None):
        r_hi, r_lo = rhs or (self.hhi, self.hlo)

        def products(hi, lo):
            for k in range(nk):
                c = slice(col + k * P, col + (k + 1) * P)
                m = self.three(bank[:, 0:n], hi[:, c], lo[:, c], r_hi[:, k, 0:n], r_lo[:, k, 0:n], k == 0, k == nk - 1)
            return m
        return products

    def token_tiles(self, banks, ntt, width, first_k, last_k, k0):
        def products(hi, lo):
            for kk in range(2):
                k = k0 + kk
                for j in range(ntt):
                    tk = slice(j * P, (j + 1) * P)
                    c = slice(kk * 512, kk * 512 + width)
                    m = self.three(banks[j][:, 0:width], self.hhi[:, k, tk], self.hlo[:, k, tk], hi[:, c], lo[:, c], k == 0, k == KT - 1)
            return m
        return products

    def token_gemm(self, ntt, width=512):
        for g in range(4):
            u = self.tile(self.token_tiles(self.M, ntt, width, 0, 0, 2 * g))
        return u

    def halves(self, hi, lo, src, scale=1.0, waits=()):
        self.act.wait(*waits)
        a = self.act.mark(self.nc.scalar.activation(hi, src, ACT.Copy, scale=scale))
        self.dve.wait(a)
        return self.dve.mark(self.nc.vector.scalar_tensor_tensor(lo, src, scale, hi.bitcast(F32), ALU.mult, ALU.subtract))

    def rms(self, src, n, tiles, dst, waits):
        nc, bank = self.nc, self.M[0]
        self.act.wait(*waits)
        self.pe.wait(*waits)
        self.act.settle()
        done = [None, None]
        for k in range(tiles):
            self.act.wait(done[k % 2])
            a = self.act.mark(nc.scalar.activation(self.tmp[:, k % 2, 0:n], src[:, k, 0:n], ACT.Square))
            self.pe.wait(a)
            done[k % 2] = self.pe.mark(nc.tensor.matmul(bank[:, 0:n], self.mean_all, self.tmp[:, k % 2, 0:n], start=(k == 0), stop=(k == tiles - 1)))
        return self.rsqrt(dst[:, 0:n], bank[:, 0:n], done[(tiles - 1) % 2])

    def rsqrt(self, dst, src, mark, bias=None):
        p = dst.shape[0]
        self.act.wait(mark)
        a = self.act.mark(self.nc.scalar.activation(dst, src, ACT.Sqrt, bias=(self.eps if bias is None else bias)[0:p, :]))
        self.dve.wait(a)
        return self.dve.mark(self.nc.vector.reciprocal(dst, dst))

    def sine(self, dst, arg, tmp, mark, p, big=False, shift=0.0):
        v, dve = self.nc.vector, self.dve
        k = tmp
        parts = pi_parts()
        dve.wait(mark)

        def go(ins):
            dve.mark(ins)
            dve.settle()
        for stage in ([4096.0] if big else []) + [1.0]:
            sh = shift if stage == 1.0 else 0.0
            go(v.tensor_scalar(k, arg, 1.0 / (TWO_PI * stage), sh / TWO_PI, ALU.mult, ALU.add))
            go(v.tensor_scalar(k, k, MAGIC, None, ALU.add))
            go(v.tensor_scalar(k, k, MAGIC, None, ALU.subtract))
            for c in parts:
                go(v.scalar_tensor_tensor(arg, k, -c * stage, arg, ALU.mult, ALU.add))
        if shift:
            go(v.tensor_scalar(arg, arg, shift, None, ALU.add))
        go(v.tensor_scalar(arg, arg, 3.1415925, -3.1415925, ALU.min, ALU.max))
        self.act.wait(dve.last())
        return self.act.mark(self.nc.scalar.activation(dst, arg, ACT.Sin))

    def constants(self):
        nc, dve = self.nc, self.nc.vector
        self.mean_all = self.sb("mean_all", [P, P])[:]
        self.ident = self.loads["ident"][0]
        self.mean_128 = self.sb("mean_128", [P, P])[:]
        self.ones = self.sb("ones", [P, 1])[:]
        self.eps = self.sb("eps", [P, 1])[:]
        self.zero = self.sb("zero", [P, 1])[:]
        for ap, v in ((self.mean_all, 1.0 / D), (self.mean_128, 1.0 / P), (self.ones, 1.0), (self.eps, EPS), (self.zero, 0.0)):
            self.dve.mark(dve.memset(ap, v))
        self.const = self.dve.last()
        for line in (self.act, self.pe, self.dve):
            line.wait(self.const)

    def condition(self):
        nc = self.nc
        self.chi = self.sb("chi", [P, KT, 2], F32R)
        self.clo = self.sb("clo", [P, KT, 2], F32R)
        c = self.loads["cond"][0]
        th = self.sb("c_tanh", [P, KT, 2])[:]
        self.need(self.act, "cond")
        self.need(self.dve, "cond")
        a = self.act.mark(nc.scalar.activation(th, c, ACT.Tanh, scale=0.5))
        self.dve.wait(a)
        d = self.dve.mark(nc.vector.scalar_tensor_tensor(th, th, 1.0, c, ALU.add, ALU.mult))
        self.dve.settle()
        self.cond_mark = self.halves(self.chi[:], self.clo[:], th, 0.5, (d,))
        self.mod = self.sb("mod", [P, 24, 2])
        self.A = self.sb("modA", [P, KT, 2])

    def modulation(self, l):
        nc = self.nc
        self.pe.wait(self.cond_mark)

        def one(m):
            b = self.bank()
            u = self.tile(self.feature_tile(2, (self.chi, self.clo), bank=b))
            self.dve.wait(u)
            self.release(nc.vector.tensor_copy(self.mod[:, m, :], b[:, 0:2]))
        for m in range(8):
            one(m)
        with self.roll(4, tile=4, bank=4) as i:
            for j in range(4):
                one(i * 4 + (8 + j))
        self.need(self.dve, f"ada_b{l}", f"norm_pre{l}", f"norm_post{l}")
        v, dve = nc.vector, self.dve
        self.dve.wait((self.free, self.free.value()))

        def bc(name, n):
            return self.loads[name][0].unsqueeze(2).broadcast_to([P, n, 2])
        dve.mark(v.tensor_tensor(self.mod[:], self.mod[:], bc(f"ada_b{l}", 24), ALU.add))
        dve.settle()
        dve.mark(v.scalar_tensor_tensor(self.A[:], self.mod[:, 8:16, :], 1.0, bc(f"norm_pre{l}", 8), ALU.add, ALU.mult))
        dve.mark(v.tensor_tensor(self.mod[:, 16:24, :], self.mod[:, 16:24, :], bc(f"norm_post{l}", 8), ALU.mult))
        return dve.last()

    def pre_norm(self, mod_mark, x_mark):
        nc = self.nc
        r = self.tmp[:, 2, :]
        m = self.rms(self.x, ALL, KT, self.tmp[:, 2, :], (x_mark,))
        self.dve.wait(m)
        self.act.wait(mod_mark)
        done = [None, None]
        for k in range(KT):
            t = self.tmp[:, 3 + k % 2, :]
            self.dve.wait(done[k % 2])
            d = self.dve.mark(nc.vector.tensor_tensor(t, self.x[:, k, :], r, ALU.mult))
            self.act.wait(d)
            for s in range(2):
                c = slice(s * TOK, (s + 1) * TOK)
                self.act.mark(nc.scalar.activation(t[:, c], t[:, c], ACT.Identity, bias=self.mod[:, k, s:s + 1], scale=self.A[:, k, s:s + 1]))
            self.act.settle()
            done[k % 2] = self.halves(self.hhi[:, k, :], self.hlo[:, k, :], t)
        return self.dve.last()

    def lam(self, l):
        nc, v, dve = self.nc, self.nc.vector, self.dve
        src = self.loads["lambda"][0]
        self.need(dve, "lambda")
        t = self.sb(f"lam_t{l}", [P, 2, 64])[:]
        e = self.sb(f"lam_e{l}", [P, 4])[:]
        for j in range(2):
            dve.mark(v.tensor_tensor(t[:, j, :], src[:, l, 2 * j, :], src[:, l, 2 * j + 1, :], ALU.mult))
        dve.settle()
        d = dve.mark(v.tensor_reduce(e[:, 0:2], t, AXX, ALU.add))
        self.act.wait(d)
        a = self.act.mark(nc.scalar.activation(e[:, 0:2], e[:, 0:2], ACT.Exp))
        dve.wait(a)
        dve.mark(v.tensor_tensor(e[:, 2:3], e[:, 1:2], e[:, 0:1], ALU.subtract))
        dve.settle()
        dve.mark(v.tensor_scalar(e[:, 3:4], e[:, 2:3], -(0.8 - 0.6 * math.exp(-0.3 * l)), None, ALU.add))
        dve.settle()
        return e[:, 3:4]

    def rope(self, ap, n, cos, sin, perm, mark, bank, tmp):
        nc, v, dve = self.nc, self.nc.vector, self.dve
        self.pe.wait(mark)
        p = self.pe.mark(nc.tensor.matmul(bank[:, 0:n], perm, ap, start=True, stop=True))
        dve.wait(p)
        dve.mark(v.tensor_tensor(tmp[:, 0:n], bank[:, 0:n], sin, ALU.mult))
        dve.mark(v.tensor_tensor(ap, ap, cos, ALU.mult))
        dve.settle()
        return dve.mark(v.tensor_tensor(ap, ap, tmp[:, 0:n], ALU.add))

    def diff_attention(self, l, q_off, k_off, nkeys, Kt, Qt, V, neg_lam, marks):
        nc, v, dve, act, pe = self.nc, self.nc.vector, self.dve, self.act, self.pe
        st = self.stat
        nkt = nkeys // P
        j0 = k_off // P
        pe.wait(*marks)
        dve.wait(*marks)
        pv_done = None
        out_done = None
        for h in range(HEADS):
            wt_marks = []
            for i in range(2):
                S = [self.M[0], self.M[1]]
                q = slice(q_off + i * P, q_off + (i + 1) * P)
                for m in range(2):
                    r = slice(m * 64, (m + 1) * 64)
                    pe.mark(nc.tensor.matmul(S[m][:, 0:nkeys], Qt[r, h, q], Kt[r, h, k_off:k_off + nkeys], start=True, stop=True))
                    dve.wait(pe.last())
                    dve.mark(v.tensor_reduce(st[:, m:m + 1], S[m][:, 0:nkeys], AXX, ALU.max, negate=True))
                dve.settle()
                d = dve.mark(v.tensor_scalar(st[:, 2:4], st[:, 0:2], 0.125, None, ALU.mult))
                act.wait(d)
                for m in range(2):
                    a = act.mark(nc.scalar.activation(self.tmp[:, m, 0:nkeys], S[m][:, 0:nkeys], ACT.Exp, bias=st[:, 2 + m:3 + m], scale=0.125, accum_out=st[:, 4 + m:5 + m]))
                dve.wait(a)
                dve.mark(v.reciprocal(st[:, 6:8], st[:, 4:6]))
                dve.settle()
                dve.mark(v.tensor_tensor(st[:, 7:8], st[:, 7:8], neg_lam, ALU.mult))
                dve.mark(v.tensor_scalar(self.tmp[:, 0, 0:nkeys], self.tmp[:, 0, 0:nkeys], st[:, 6:7], None, ALU.mult))
                dve.settle()
                w = self.tmp[:, 2, 0:nkeys]
                d = dve.mark(v.scalar_tensor_tensor(w, self.tmp[:, 1, 0:nkeys], st[:, 7:8], self.tmp[:, 0, 0:nkeys], ALU.mult, ALU.add))
                pe.wait(d)
                if wt_marks:
                    pe.wait(wt_marks[-1])
                for kt in range(nkt):
                    p = nc.tensor.transpose(self.M[2][:, kt * P:(kt + 1) * P], w[:, kt * P:(kt + 1) * P], self.ident)
                p = pe.mark(p)
                act.wait(p)
                if i == 0 and pv_done:
                    act.wait(pv_done)
                wt_marks.append(act.mark(nc.scalar.activation(
                    self.wt[:, 0:nkt, i * P:(i + 1) * P], self.M[2][:, 0:nkeys].rearrange("p (k q) -> p k q", k=nkt), ACT.Copy)))
            pe.wait(*wt_marks)
            pe.wait(out_done)
            for kt in range(nkt):
                p = nc.tensor.matmul(self.M[3][:, 0:TOK], V[:, j0 + kt, h * P:(h + 1) * P], self.wt[:, kt, :], start=(kt == 0), stop=(kt == nkt - 1))
            pv_done = pe.mark(p)
            dve.wait(pv_done)
            out_done = dve.mark(v.tensor_copy(self.y[:, h, q_off:q_off + TOK], self.M[3][:, 0:TOK]))
        self.need(dve, f"subln{l}")
        init = 0.8 - 0.6 * math.exp(-0.3 * l)
        for h in range(HEADS):
            yh = self.y[:, h, q_off:q_off + TOK]
            act.wait(out_done, dve.last())
            a = act.mark(nc.scalar.activation(self.tmp[:, 0, 0:TOK], yh, ACT.Square))
            pe.wait(a)
            p = pe.mark(nc.tensor.matmul(self.M[0][:, 0:TOK], self.mean_128, self.tmp[:, 0, 0:TOK], start=True, stop=True))
            m = self.rsqrt(self.tmp[:, 1, 0:TOK], self.M[0][:, 0:TOK], p)
            dve.wait(m)
            dve.mark(v.tensor_tensor(yh, yh, self.tmp[:, 1, 0:TOK], ALU.mult))
            dve.settle()
            dve.mark(v.tensor_scalar(yh, yh, self.loads[f"subln{l}"][0], 1.0 - init, ALU.mult, ALU.mult))
        return dve.last()

    def hyena_filter(self, l):
        nc, v, dve, act, pe = self.nc, self.nc.vector, self.dve, self.act, self.pe
        names = [f"hy_{n}{l}" for n in ("w1", "b1", "w2", "b2", "w3", "freq")]
        w3_at = self.y[0:64, 4:6, :].rearrange("p a n -> p (a n)")
        self.load(f"hy_w3{l}", w3_at, eng=nc.gpsimd)
        self.load(f"hy_decay{l}", self.y[:, 6:8, :], self.ins["hy_decay"], eng=nc.gpsimd)
        for line in (pe, dve):
            self.need(line, *names, "hy_z", f"hy_decay{l}", "dft")
        w1, b1, w2, b2, w3, fr = (self.loads[n][0] for n in names)
        z, decay, dft = (self.loads[n][0] for n in ("hy_z", f"hy_decay{l}", "dft"))
        hid = self.tmp[0:64, 0, 0:TOK]
        arg = self.tmp[0:64, 0, TOK:ALL]
        k = self.tmp[0:64, 1, 0:TOK]
        src = z
        m = None
        for s, (w, b, kk) in enumerate(((w1, b1, 33), (w2, b2, 64))):
            pe.wait(m)
            p = pe.mark(nc.tensor.matmul(self.M[0][0:64, 0:TOK], w, src, start=True, stop=True))
            dve.wait(p)
            dve.mark(v.tensor_scalar(arg, self.M[0][0:64, 0:TOK], b, fr[:, s:s + 1], ALU.add, ALU.mult))
            m = self.sine(hid, arg, k, dve.last(), 64)
            src = hid
        pe.wait(m)
        f, b = self.arena[:, 0:2, :], self.arena[:, 2:4, :]
        for c, dst in ((0, f), (1, b)):
            for t in range(2):
                p = pe.mark(nc.tensor.matmul(self.M[2 * c + t][:, :], hid[:, t * P:(t + 1) * P], w3[:, c * BR:(c + 1) * BR], start=True, stop=True))
                dve.wait(p)
                dve.mark(v.tensor_tensor(dst[:, t, :], self.M[2 * c + t][:, :], decay[:, t, :], ALU.mult))
        dve.settle()
        dve.mark(v.memset(b[0:1, 0, :], 0.0))
        dve.settle()
        act.wait(dve.last())
        pe.wait(dve.last())
        sq = self.arena[:, 4:8, :]
        for n in range(4):
            a = act.mark(nc.scalar.activation(sq[:, n, :], self.arena[:, n, :], ACT.Square))
        pe.wait(a)
        for c in range(BT):
            for n in range(4):
                p = nc.tensor.matmul(self.M[0][:, c:c + 1], sq[:, n, c * P:(c + 1) * P], self.ones, start=(n == 0), stop=(n == 3))
        p = pe.mark(p)
        m = self.rsqrt(self.hy_rs[:], self.M[0][:, 0:BT], p, self.zero)
        s, d = self.arena[:, 8:10, :], self.arena[:, 10:12, :]
        dve.mark(v.tensor_tensor(s, f, b, ALU.add))
        dve.mark(v.tensor_tensor(d, f, b, ALU.subtract))
        pe.wait(dve.last())
        for part, src, dst in ((0, s, self.kre), (1, d, self.kim)):
            for ft in range(2):
                bank = self.M[(2 * part + ft) % 4]
                for t in range(2):
                    p = nc.tensor.matmul(bank[:, :], dft[:, t, part * TOK + ft * P:part * TOK + (ft + 1) * P], src[:, t, :], start=(t == 0), stop=(t == 1))
                p = pe.mark(p)
                act.wait(p)
                act.mark(nc.scalar.activation(dst[:, ft, :], bank[:, :], ACT.Copy))
        return act.last(), dve.last()

    def hyena_conv(self, l, seqs, marks):
        nc, v, dve, act, pe = self.nc, self.nc.vector, self.dve, self.act, self.pe
        n = seqs * TOK
        hy = self.arena[:, 12:24, :]
        for line in (dve, act, pe):
            line.wait(*marks)
        self.need(dve, f"hy_bias{l}")
        self.need(pe, "idft", "ident")
        idft, dft = self.loads["idft"][0], self.loads["dft"][0]
        for c in range(BT):
            dve.mark(v.tensor_tensor(hy[:, 4 + c, 0:n], hy[:, 4 + c, 0:n], hy[:, 8 + c, 0:n], ALU.mult))
        pe.wait(dve.last())
        ut = self.arena[:, 8:12, :]
        prev = None
        for s in range(seqs):
            for t in range(2):
                b = self.M[(2 * s + t) % 4]
                for c in range(BT):
                    o = s * TOK + t * P
                    p = nc.tensor.transpose(b[:, c * P:(c + 1) * P], hy[:, 4 + c, o:o + P], self.ident)
                p = pe.mark(p)
                act.wait(p)
                act.mark(nc.scalar.activation(ut[:, 2 * s + t, :], b[:, :], ACT.Copy))
        pe.wait(act.last())
        for s in range(seqs):
            spec = self.arena[:, 0:4, :]
            inv_done = None if s == 0 else pe.last()
            dve.wait(inv_done)
            for ft in range(2):
                re, im = self.M[2 * ft], self.M[2 * ft + 1]
                for part, b in ((0, re), (1, im)):
                    for t in range(2):
                        p = nc.tensor.matmul(b[:, :], dft[:, t, part * TOK + ft * P:part * TOK + (ft + 1) * P], ut[:, 2 * s + t, :], start=(t == 0), stop=(t == 1))
                    p = pe.mark(p)
                dve.wait(p)
                t0, t1 = self.tmp[:, 0, :], self.tmp[:, 1, :]
                dve.mark(v.tensor_tensor(t0, im[:, :], self.kim[:, ft, :], ALU.mult))
                dve.mark(v.tensor_tensor(spec[:, ft, :], re[:, :], self.kre[:, ft, :], ALU.mult))
                dve.mark(v.tensor_tensor(t1, im[:, :], self.kre[:, ft, :], ALU.mult))
                dve.mark(v.tensor_tensor(spec[:, 2 + ft, :], re[:, :], self.kim[:, ft, :], ALU.mult))
                dve.settle()
                dve.mark(v.tensor_tensor(spec[:, ft, :], spec[:, ft, :], t0, ALU.subtract))
                dve.mark(v.tensor_tensor(spec[:, 2 + ft, :], spec[:, 2 + ft, :], t1, ALU.add))
                dve.settle()
            pe.wait(dve.last())
            o = slice(s * TOK, (s + 1) * TOK)
            for c in range(BT):
                b = self.M[c]
                for k in range(4):
                    p = nc.tensor.matmul(b[:, 0:TOK], spec[:, k, c * P:(c + 1) * P], idft[:, k, :], start=(k == 0), stop=(k == 3))
                p = pe.mark(p)
                dve.wait(p)
                yb = self.y[:, 4 + c, o]
                dve.mark(v.tensor_scalar(yb, b[:, 0:TOK], self.hy_rs[:, c:c + 1], None, ALU.mult))
                dve.settle()
                dve.mark(v.scalar_tensor_tensor(yb, hy[:, 4 + c, o], self.loads[f"hy_bias{l}"][0][:, c:c + 1], yb, ALU.mult, ALU.add))
                dve.settle()
                dve.mark(v.tensor_tensor(yb, yb, hy[:, c, o], ALU.mult))
            pe.wait(dve.last())
        return dve.last()

    def gmlp(self, l, ntt, marks):
        nc, v, dve, act, pe = self.nc, self.nc.vector, self.dve, self.act, self.pe
        self.need(dve, f"ln_g{l}", f"ln_b{l}", f"gm_bs{l}")
        self.need(pe, f"gm_ws{l}")
        g, b_, ws, bs = (self.loads[f"{n}{l}"][0] for n in ("ln_g", "ln_b", "gm_ws", "gm_bs"))
        dve.wait(*marks)
        u, vt = self.arena[:, 0:4, :], self.arena[:, 4:8, :]
        for t in range(ntt):
            x = vt[:, t, :]
            st = self.stat
            dve.mark(v.bn_stats(st[:, 8:14], x))
            dve.settle()
            dve.mark(v.bn_aggr(st[:, 14:16], st[:, 8:14]))
            m = self.rsqrt(st[:, 16:17], st[:, 15:16], dve.last())
            dve.wait(m)
            dve.mark(v.tensor_scalar(x, x, st[:, 14:15], st[:, 16:17], ALU.subtract, ALU.mult))
            dve.settle()
            dve.mark(v.tensor_tensor(x, x, g, ALU.mult))
            dve.settle()
            dve.mark(v.tensor_tensor(x, x, b_, ALU.add))
            dve.settle()
        pe.wait(dve.last())
        freed = [None] * 4
        tm_read = [None] * 4
        for t in range(ntt):
            for j in range(BT):
                b = self.M[j]
                pe.wait(freed[j])
                p = pe.mark(nc.tensor.matmul(b[:, 0:2 * P], vt[:, t, j * P:(j + 1) * P], ws[:, 2 * j:2 * j + 2, :], start=True, stop=True))
                dve.wait(p)
                tm = self.tmp[:, 0, j * P:(j + 1) * P]
                dve.wait(tm_read[j])
                dve.mark(v.tensor_tensor(tm[0:64, :], b[0:64, 0:P], bs[0:64, j, :], ALU.add))
                freed[j] = dve.mark(v.tensor_tensor(tm[64:P, :], b[64:P, P:2 * P], bs[64:P, j, :], ALU.add))
                dve.settle()
                tm_read[j] = dve.mark(v.tensor_tensor(self.y[:, 8 + j, t * P:(t + 1) * P], tm, u[:, j, t * P:(t + 1) * P], ALU.mult))
        return dve.last()

    def merge(self, branches, n, gated):
        nc, v, dve, act = self.nc, self.nc.vector, self.dve, self.act
        dve.mark(v.memset(self.y[:, 0:KT, 0:n], 0.0))
        dve.settle()
        with self.roll(branches, tile=12, bank=8, act=8, dve=8) as i:
            rhs = gated(i)
            for pair in range(4):
                def terms(hi, lo):
                    for o in range(2):
                        nc.tensor.wait_ge(self.free.sem, self.free.value(o - 3))
                        b = self.G[(self.free.off + o) % 4]
                        for k in range(BT):
                            c = slice((o * BT + k) * P, (o * BT + k + 1) * P)
                            m = self.three(b[:, 0:n], hi[:, c], lo[:, c], rhs[0](k), rhs[1](k), k == 0, k == BT - 1)
                    return m
                self.tile(terms)
                for o in range(2):
                    e = self.free.off % 4
                    sel = self.M[e]
                    u = self.tile(self.feature_tile(n, bank=sel))
                    act.wait(u)
                    th = self.tmp[:, e % 2, 0:n]
                    act.eng.wait_ge(self.free.sem, self.free.value(-1))
                    a = act.mark(nc.scalar.activation(th, sel[:, 0:n], ACT.Tanh, scale=0.5))
                    dve.wait(a)
                    dve.mark(v.scalar_tensor_tensor(th, th, 1.0, self.G[e][:, 0:n], ALU.add, ALU.mult))
                    dve.settle()
                    acc = self.y[:, 2 * pair + o, 0:n]
                    self.release(v.tensor_tensor(acc, acc, th, ALU.add))
        return (self.free, self.free.value())


def block1_layer(p, l, x_mark):
    nc, v, dve, act, pe = p.nc, p.nc.vector, p.dve, p.act, p.pe
    last = l == DEPTH - 1
    n = TOK if last else ALL
    mod_mark = p.modulation(l)
    neg_lam = p.lam(l)
    h_mark = p.pre_norm(mod_mark, x_mark)
    pe.wait(h_mark)

    K, Q, V = p.arena[:, 0:4, :], p.arena[:, 4:8, :], p.arena[:, 8:12, :]
    for dst, width in ((K, ALL), (Q, n)):
        for j in range(4):
            b = p.bank()
            u = p.tile(p.feature_tile(width, bank=b))
            act.wait(u)
            p.release(nc.scalar.activation(dst[:, j, 0:width], b[:, 0:width], ACT.Copy))
    kq = (p.free, p.free.value())
    u = p.token_gemm(4)
    act.wait(u)
    for j in range(4):
        v_mark = act.mark(nc.scalar.activation(V[:, j, :], p.M[j][:, :], ACT.Copy))
    p.need(dve, "rope")
    p.need(pe, "rope", "perm1", "ident")
    dve.wait(kq, v_mark)
    pe.wait(v_mark)
    rope = p.loads["rope"][0]
    bank_read = [None] * 4
    for j in range(8):
        T = (K, Q)[j // 4]
        pe.wait(bank_read[j % 4])
        m = bank_read[j % 4] = p.rope(T[:, j % 4, 0:TOK], TOK, rope[:, 0, :], rope[:, 1, :], p.loads["perm1"][0], kq if j < 4 else kq, p.M[j % 4], p.tmp[:, j % 2, :])
    a = p.diff_attention(l, 0, 0, ALL, K, Q, V, neg_lam, (m,))
    if not last:
        a = p.diff_attention(l, TOK, TOK, TOK, K, Q, V, neg_lam, (a, m))
    pe.wait(a)
    act.wait(a)
    dve.wait(a)

    nc.gpsimd.wait_ge(a[0].sem, a[1])
    f_act, f_dve = p.hyena_filter(l)
    p.need(act, f"hy_sw{l}")
    p.need(dve, f"hy_sw{l}")
    sw = p.loads[f"hy_sw{l}"][0]
    hy = p.arena[:, 12:24, :]
    seqs = n // TOK
    dve_step = 2
    with p.roll(3, tile=4, bank=4, act=4, dve=4) as i:
        for j in range(4):
            m = i * 4 + j
            b = p.bank()
            u = p.tile(p.feature_tile(n, bank=b))
            act.wait(u)
            o = hy[:, m, 0:n]
            a = act.mark(nc.scalar.activation(o, b[:, 0:n], ACT.Identity, bias=sw[:, m, 3:4], scale=sw[:, m, 1:2]))
            dve.wait(a)
            o3 = o.rearrange("p (s t) -> p s t", s=seqs)
            b3 = b[:, 0:n].rearrange("p (s t) -> p s t", s=seqs)
            dve.mark(v.scalar_tensor_tensor(o3[:, :, 1:TOK], b3[:, :, 0:TOK - 1], sw[:, m, 0:1], o3[:, :, 1:TOK], ALU.mult, ALU.add))
            dve.settle()
            p.release(v.scalar_tensor_tensor(o3[:, :, 0:TOK - 1], b3[:, :, 1:TOK], sw[:, m, 2:3], o3[:, :, 0:TOK - 1], ALU.mult, ALU.add))
    b_mark = p.hyena_conv(l, seqs, ((p.free, p.free.value()), f_act, f_dve))
    for line in (pe, act, dve):
        line.wait(b_mark)

    nc.gpsimd.wait_ge(b_mark[0].sem, b_mark[1])
    p.load(f"ln_g{l}", p.arena[:, 12, :], eng=nc.gpsimd)
    p.load(f"ln_b{l}", p.arena[:, 13, :], eng=nc.gpsimd)
    p.load(f"gm_ws{l}", p.arena[:, 14:16, :].rearrange("p a (g q) -> p (a g) q", q=P), eng=nc.gpsimd)
    p.load(f"gm_bs{l}", p.arena[:, 16, :].rearrange("p (j q) -> p j q", q=P), eng=nc.gpsimd)
    gu = p.arena[:, 0:4, :]
    for j in range(4):
        b = p.bank()
        u = p.tile(p.feature_tile(n, bank=b))
        act.wait(u)
        p.release(nc.scalar.activation(gu[:, j, 0:n], b[:, 0:n], ACT.Gelu))
    ntt = n // P
    u = p.token_gemm(ntt)
    act.wait(u)
    for j in range(ntt):
        act.mark(nc.scalar.activation(p.arena[:, 4 + j, :], p.M[j][:, :], ACT.Gelu))
    c_mark = p.gmlp(l, ntt, (act.last(), (p.free, p.free.value())))
    for line in (pe, act, dve):
        line.wait(c_mark)

    arenaR = p.arena_r
    with p.roll(3, tile=4, bank=4, act=8, dve=8) as i:
        for j in range(4):
            b = p.bank()
            u = p.tile(p.feature_tile(n, bank=b))
            act.wait(u)
            th = p.tmp[:, 3 + j % 2, 0:n]
            yt = p.y[:, i * 4 + j, 0:n]
            act.eng.wait_ge(p.free.sem, p.free.value(-1))
            a = act.mark(nc.scalar.activation(th, b[:, 0:n], ACT.Tanh, scale=0.5))
            dve.wait(a)
            dve.mark(v.scalar_tensor_tensor(th, th, 1.0, b[:, 0:n], ALU.add, ALU.mult))
            dve.settle()
            d = dve.mark(v.tensor_tensor(th, th, yt, ALU.mult))
            act.wait(d)
            hi, lo = arenaR[:, i * 8 + j, 0:n], arenaR[:, i * 8 + (4 + j), 0:n]
            a = act.mark(nc.scalar.activation(hi, th, ACT.Copy, scale=0.5))
            dve.wait(a)
            p.release(v.scalar_tensor_tensor(lo, th, 0.5, hi.bitcast(F32), ALU.mult, ALU.subtract))
    pe.wait((p.free, p.free.value()))

    def gated(i):
        return (lambda k: arenaR[:, i * 8 + k, 0:n]), (lambda k: arenaR[:, i * 8 + (4 + k), 0:n])
    return gated, n


def block1_out(p, n, m_mark, x_mark):
    nc, v, dve, act, pe = p.nc, p.nc.vector, p.dve, p.act, p.pe
    act.wait(m_mark)
    dve.wait(m_mark)
    pe.wait(m_mark)
    for k in range(KT):
        m = p.halves(p.hhi[:, k, 0:n], p.hlo[:, k, 0:n], p.y[:, k, 0:n], 0.5)
    pe.wait(m)
    for o in range(KT):
        b = p.bank()
        u = p.tile(p.feature_tile(n, bank=b))
        act.wait(u)
        p.release(nc.scalar.activation(p.arena[:, o, 0:n], b[:, 0:n], ACT.Copy))
    m = p.rms(p.arena[:], n, KT, p.tmp[:, 2, :], ((p.free, p.free.value()),))
    dve.wait(m, (p.free, p.free.value()))
    dve.settle()
    for k in range(KT):
        o = p.arena[:, k, 0:n]
        dve.mark(v.tensor_tensor(o, o, p.tmp[:, 2, 0:n], ALU.mult))
        dve.settle()
        for s in range(n // TOK):
            c = slice(s * TOK, (s + 1) * TOK)
            dve.mark(v.scalar_tensor_tensor(p.x[:, k, c], p.arena[:, k, c], p.mod[:, 16 + k, s:s + 1], p.x[:, k, c], ALU.mult, ALU.add))
    return dve.last()


def second_norm(p, gain, x_mark):
    nc, v, dve = p.nc, p.nc.vector, p.dve
    m = p.rms(p.x, TOK, KT, p.tmp[:, 2, :], (x_mark,))
    p.need(dve, gain)
    g = p.loads[gain][0]
    dve.wait(m)
    dve.settle()
    done = [None, None]
    for k in range(KT):
        t = p.tmp[:, 3 + k % 2, 0:TOK]
        dve.wait(done[k % 2])
        d = dve.mark(v.scalar_tensor_tensor(t, p.x[:, k, 0:TOK], g[:, k:k + 1], p.tmp[:, 2, 0:TOK], ALU.mult, ALU.mult))
        done[k % 2] = p.halves(p.hhi[:, k, 0:TOK], p.hlo[:, k, 0:TOK], t, 1.0, (d,))
    return dve.last()


def compress(p, z, which, X, xh, xl, hid):
    nc, v, dve, act, pe = p.nc, p.nc.vector, p.dve, p.act, p.pe
    pe_t = p.loads[f"pe_{which}"][0]
    p.need(dve, f"pe_{which}")
    pair = p.tmp[:, 0, :].rearrange("p (g t) -> p g t", g=2)[:, :, 0:P]
    for g in range(2):
        for par in range(2):
            a = act.mark(nc.scalar.activation(pair[par * 64:par * 64 + 64, g, :], z[g * 64:g * 64 + 64, par::2], ACT.Copy))
    dve.wait(a)
    for g in range(2):
        for jj in range(16):
            dve.mark(v.tensor_scalar(X[:, jj, g * NCMP:(g + 1) * NCMP], pair[:, g, jj:jj + 8 * (NCMP - 1) + 1:8], pe_t[:, jj:jj + 1], None, ALU.add))
    dve.settle()
    m = p.halves(xh[:], xl[:], X, 1.0, (dve.last(),))
    pe.wait(m)
    banks = [p.M[1], p.M[2]]
    for g in range(4):
        def products(hi, lo):
            for q in range(4):
                jj = 4 * g + q
                for o in range(2):
                    c = slice(q * 256 + o * P, q * 256 + (o + 1) * P)
                    r = p.three(banks[o][:, 0:2 * NCMP], hi[:, c], lo[:, c], xh[:, jj, :], xl[:, jj, :], jj == 0, jj == 15)
            return r
        u = p.tile(products)
    act.wait(u)
    dve.wait(u)
    th = p.tmp[:, 1, 0:4 * NCMP].rearrange("p (o n) -> p o n", o=2)
    for o in range(2):
        a = act.mark(nc.scalar.activation(th[:, o, :], banks[o][:, 0:2 * NCMP], ACT.Tanh, scale=0.5))
        dve.wait(a)
        dve.mark(v.scalar_tensor_tensor(th[:, o, :], th[:, o, :], 1.0, banks[o][:, 0:2 * NCMP], ALU.add, ALU.mult))
    dve.settle()
    return dve.mark(v.tensor_scalar(hid, th, 0.5, None, ALU.mult))


def block2(p, x_mark):
    nc, v, dve, act, pe = p.nc, p.nc.vector, p.dve, p.act, p.pe
    pool = nc.gpsimd
    pool.wait_ge(x_mark[0].sem, x_mark[1])
    p.load("head_spread", p.shared[0:32, 0:1792].rearrange("p (a n) -> p a n", a=14), eng=pool)
    p.load("ck_w2", p.shared[:, 1792:1920].rearrange("p (a n) -> p a n", a=2), eng=pool)
    p.load("cv_w2", p.shared[:, 1920:2048].rearrange("p (a n) -> p a n", a=2), eng=pool)
    p.load("ple", p.y[:, 8, :], eng=pool)
    L = {k: m[0] for k, m in p.loads.items()}

    p.need(dve, "pos", "inv_freq", "head_gain", "causal", "cmp_add", "cmp_keep")
    p.need(pe, "perm2", "head_sum", "head_spread", "block_mean", "ck_w2", "cv_w2")
    dve.wait(x_mark)
    act.wait(x_mark)
    pe.wait(x_mark)
    trig = p.y[:, 9, :].rearrange("p (s t) -> p s t", s=2)
    posf = p.tmp[:, 0, 0:TOK]
    for s, shift in ((0, math.pi / 2), (1, 0.0)):
        act.wait(dve.last())
        dve.mark(v.tensor_copy(posf, L["pos"]))
        dve.settle()
        dve.mark(v.tensor_scalar(p.tmp[:, 1, 0:TOK], posf, L["inv_freq"], None, ALU.mult))
        dve.settle()
        m = p.sine(trig[:, s, :], p.tmp[:, 1, 0:TOK], p.tmp[:, 0, 0:TOK], dve.last(), P, big=True, shift=shift)
        dve.wait(m)
    cos, sin = trig[:, 0, :], trig[:, 1, :]

    h = second_norm(p, "g_mix", dve.last())
    pe.wait(h)
    Z = p.arena[:, 0:8, :].rearrange("p a (b t) -> p (a b) t", t=TOK)
    with p.roll(4, tile=4, bank=4) as i:
        for j in range(4):
            b = p.bank()
            u = p.tile(p.feature_tile(TOK, bank=b))
            act.wait(u)
            p.release(nc.scalar.activation(Z[:, i * 4 + j, :], b[:, 0:TOK], ACT.Copy))
    z_mark = (p.free, p.free.value())
    VM, VS = p.arena[:, 8:10, :], p.arena[:, 10:12, :]
    u = p.token_gemm(2)
    act.wait(u)
    for j in range(2):
        a = act.mark(nc.scalar.activation(VM[:, j, :], p.M[j][:, :], ACT.Copy))
    pe.wait(a)
    u = p.token_gemm(2, 280)
    act.wait(u)
    gate = p.sb("gate2", [P, 2, 24])[:]
    for j in range(2):
        a = act.mark(nc.scalar.activation(VS[:, j, 0:256], p.M[j][:, 0:256], ACT.Copy))
        a = act.mark(nc.scalar.activation(gate[:, j, :], p.M[j][:, 256:280], ACT.Tanh, scale=0.5))
    dve.wait(a, z_mark)
    dve.mark(v.tensor_scalar(gate, gate, 1.0, 0.5, ALU.add, ALU.mult))

    X = p.y[:, 10, 0:32 * NCMP].rearrange("p (a n) -> p a n", a=16)
    xh, xl = p.sb("cmp_xh", [P, 16, 2 * NCMP], F32R), p.sb("cmp_xl", [P, 16, 2 * NCMP], F32R)
    hid = p.sb("cmp_hid", [P, 2, 2 * NCMP])[:]
    act.wait(z_mark)
    act.settle()
    pe.wait(a)
    m = compress(p, Z[:, 4, :], "k", X, xh, xl, hid)
    pe.wait(m)
    kcT = p.sb("kc_t", [P, 2, 16])[:]
    b = p.M[0]
    for g in range(2):
        for o in range(2):
            q = nc.tensor.matmul(b[g * 64:g * 64 + 64, 0:NCMP], L["ck_w2"][:, o, :], hid[:, o, g * NCMP:(g + 1) * NCMP], start=(o == 0), stop=(o == 1))
        q = pe.mark(q)
    act.wait(q)
    a = act.mark(nc.scalar.activation(kcT[:, 0, 0:NCMP], b[:, 0:NCMP], ACT.Copy))
    a = act.mark(nc.scalar.activation(kcT[:, 1, 0:NCMP], b[:, 0:NCMP], ACT.Square))
    pe.wait(a)
    q = pe.mark(nc.tensor.matmul(b[:, 0:NCMP], L["block_mean"], kcT[:, 1, 0:NCMP], start=True, stop=True))
    m = p.rsqrt(kcT[:, 1, 0:NCMP], b[:, 0:NCMP], q)
    dve.settle()
    dve.mark(v.scalar_tensor_tensor(kcT[:, 0, 0:NCMP], kcT[:, 0, 0:NCMP], L["head_gain"][:, 14:15], kcT[:, 1, 0:NCMP], ALU.mult, ALU.mult))
    p.rope(kcT[:, 0, 0:NCMP], NCMP, cos[:, 31::16], sin[:, 31::16], L["perm2"], dve.last(), b, p.tmp[:, 3, :])
    act.wait(dve.last())
    m = compress(p, Z[:, 5, :], "v", X, xh, xl, hid)
    pe.wait(m)
    vc = p.sb("vc", [16, P])[:]
    for g in range(2):
        for o in range(2):
            q = nc.tensor.matmul(b[0:NCMP, g * 64:g * 64 + 64], hid[:, o, g * NCMP:(g + 1) * NCMP], L["cv_w2"][:, o, :], start=(o == 0), stop=(o == 1))
    q = pe.mark(q)
    act.wait(q)
    act.mark(nc.scalar.activation(vc[0:NCMP, :], b[0:NCMP, 0:P], ACT.Copy))

    tiles = [0, 1, 2, 3, 6, 7] + list(range(8, 16))
    pe.wait(act.last())
    done = [None, None]
    for n, zt in enumerate(tiles):
        act.wait(done[n % 2])
        a = act.mark(nc.scalar.activation(p.tmp[:, n % 2, 0:TOK], Z[:, zt, :], ACT.Square))
        pe.wait(a)
        done[n % 2] = pe.mark(nc.tensor.matmul(b[0:32, 0:TOK], L["head_sum"][:, n, :], p.tmp[:, n % 2, 0:TOK], start=(n == 0), stop=(n == 13)))
    hr = p.tmp[0:32, 2, 0:TOK]
    m = p.rsqrt(hr, b[0:32, 0:TOK], done[1])
    pe.wait(m)
    dve.settle()
    last_use = [None] * 4
    for n, zt in enumerate(tiles):
        s, r = p.M[1 + n % 2], p.M[0 if n % 2 else 3]
        pe.wait(last_use[n % 2])
        q = pe.mark(nc.tensor.matmul(s[:, 0:TOK], L["head_spread"][:, n, :], hr, start=True, stop=True))
        dve.wait(q)
        d = dve.mark(v.scalar_tensor_tensor(Z[:, zt, :], Z[:, zt, :], L["head_gain"][:, n:n + 1], s[:, 0:TOK], ALU.mult, ALU.mult))
        dve.settle()
        last_use[n % 2] = p.rope(Z[:, zt, :], TOK, cos, sin, L["perm2"], d, r, p.tmp[:, 3 + n % 2, :])
    qk = dve.last()

    Sm = p.arena[:, 12:15, :].rearrange("p a (b t) -> p (a b) t", t=TOK)
    PT = p.arena[:, 15:18, :].rearrange("p a (b k q) -> p a b k q", b=2, k=2)
    Sc = p.sb("s_cmp", [P, 2, 16])[:]
    PTc = p.y[0:16, 11, 0:2 * P].rearrange("p (b q) -> p b q", b=2)
    YN = p.y[:, 0:2, :].rearrange("p a (b t) -> p (a b) t", t=TOK)
    YM = p.y[:, 2:4, :].rearrange("p a (b t) -> p (a b) t", t=TOK)
    st = p.stat
    banks_read = None
    for i in range(2):
        nk = P * (i + 1)
        q_ = slice(i * P, (i + 1) * P)
        for j in range(4):
            pe.wait(qk, banks_read)
            for ab in range(2):
                r = slice(ab * 64, ab * 64 + 64)
                for kind, (qt, kt) in enumerate(((j, 6), (j, 7), (8 + j, 12 + j))):
                    c = (kind % 2) * nk
                    nc.tensor.matmul(p.M[2 * ab + kind // 2][:, c:c + nk], Z[r, qt, q_], Z[r, kt, 0:nk], start=True, stop=True)
                q = nc.tensor.matmul(p.M[2 * ab + 1][:, TOK:TOK + NCMP], Z[r, j, q_], kcT[r, 0, 0:NCMP], start=True, stop=True)
                q = pe.mark(q)
            dve.wait(q)
            mask = L["causal"][:, TOK - nk:TOK].unsqueeze(1).broadcast_to([P, 2, nk])
            for ab in range(2):
                two, one = p.M[2 * ab], p.M[2 * ab + 1]
                dve.mark(v.scalar_tensor_tensor(Sm[:, 3 * ab:3 * ab + 2, 0:nk], two[:, 0:2 * nk].rearrange("p (b n) -> p b n", b=2), 0.125, mask, ALU.mult, ALU.add))
                dve.mark(v.scalar_tensor_tensor(Sm[:, 3 * ab + 2, 0:nk], one[:, 0:nk], 0.125, L["causal"][:, TOK - nk:TOK], ALU.mult, ALU.add))
                dve.mark(v.scalar_tensor_tensor(Sc[:, ab, 0:NCMP], one[:, TOK:TOK + NCMP], 0.125, L["cmp_add"][:, i, :], ALU.mult, ALU.add))
            ckeep = L["cmp_keep"][:, i:i + 1, :].broadcast_to([P, 2, NCMP])
            dve.settle()
            dve.mark(v.tensor_reduce(st[:, 0:6], Sm[:, :, 0:nk], AXX, ALU.max, negate=True))
            d = dve.mark(v.tensor_reduce(st[:, 6:8], Sc[:, :, 0:NCMP], AXX, ALU.max, negate=True))
            act.wait(d)
            for r in range(6):
                act.mark(nc.scalar.activation(Sm[:, r, 0:nk], Sm[:, r, 0:nk], ACT.Exp, bias=st[:, r:r + 1], accum_out=st[:, 8 + r:9 + r]))
            for ab in range(2):
                a = act.mark(nc.scalar.activation(Sc[:, ab, 0:NCMP], Sc[:, ab, 0:NCMP], ACT.Exp, bias=st[:, 6 + ab:7 + ab]))
            dve.wait(a)
            dve.mark(v.tensor_tensor(Sc[:, :, 0:NCMP], Sc[:, :, 0:NCMP], ckeep, ALU.mult))
            dve.settle()
            dve.mark(v.tensor_reduce(st[:, 14:16], Sc[:, :, 0:NCMP], AXX, ALU.add))
            dve.settle()
            dve.mark(v.tensor_scalar(st[:, 8:16], st[:, 8:16], 1e-30, None, ALU.max))
            dve.settle()
            dve.mark(v.reciprocal(st[:, 16:24], st[:, 8:16]))
            dve.settle()
            for kind, cols in ((1, slice(16, 20, 3)), (2, slice(17, 21, 3)), (0, slice(22, 24))):
                c0 = j * 3 + kind
                dve.mark(v.tensor_tensor(st[:, cols], st[:, cols], gate[:, i, c0:c0 + 13:12], ALU.mult))
            dve.settle()
            dve.mark(v.tensor_tensor(Sm[:, :, 0:nk], Sm[:, :, 0:nk], st[:, 16:22].unsqueeze(2).broadcast_to([P, 6, nk]), ALU.mult))
            d = dve.mark(v.tensor_tensor(Sc[:, :, 0:NCMP], Sc[:, :, 0:NCMP], st[:, 22:24].unsqueeze(2).broadcast_to([P, 2, NCMP]), ALU.mult))
            pe.wait(d)
            for kind in range(3):
                for ab in range(2):
                    for kt in range(i + 1):
                        c = (ab * 2 + kt) * P
                        nc.tensor.transpose(p.M[kind][:, c:c + P], Sm[:, 3 * ab + kind, kt * P:(kt + 1) * P], p.ident)
            for ab in range(2):
                q = nc.tensor.transpose(p.M[3][0:NCMP, ab * P:(ab + 1) * P], Sc[:, ab, 0:NCMP], p.ident)
            q = pe.mark(q)
            act.wait(q)
            dve.wait(q)
            for kind in range(3):
                a = act.mark(nc.scalar.activation(PT[:, kind, :, 0:i + 1, :], p.M[kind][:, :].rearrange("p (b k q) -> p b k q", b=2, k=2)[:, :, 0:i + 1, :], ACT.Copy))
            d = dve.mark(v.tensor_copy(PTc[0:NCMP, :, :], p.M[3][0:NCMP, 0:2 * P].rearrange("p (b q) -> p b q", b=2)))
            pe.wait(a, d)
            for ab in range(2):
                o = slice(ab * 64, ab * 64 + 64)
                for kind in range(2):
                    for kt in range(i + 1):
                        nc.tensor.matmul(p.M[0][o, 0:P], VS[:, kt, kind * P + ab * 64:kind * P + ab * 64 + 64], PT[:, kind, ab, kt, :], start=(kind == 0 and kt == 0), stop=False)
                nc.tensor.matmul(p.M[0][o, 0:P], vc[0:NCMP, o], PTc[0:NCMP, ab, :], start=False, stop=True)
                for kt in range(i + 1):
                    hd = 2 * j + ab
                    q = nc.tensor.matmul(p.M[1][o, 0:P], VM[:, kt, hd * 64:hd * 64 + 64], PT[:, 2, ab, kt, :], start=(kt == 0), stop=(kt == i))
            q = pe.mark(q)
            dve.wait(q)
            dve.mark(v.tensor_copy(YN[:, j, q_], p.M[0][:, 0:P]))
            banks_read = dve.mark(v.tensor_copy(YM[:, j, q_], p.M[1][:, 0:P]))
    act.wait(banks_read)
    dve.settle()

    R = p.arena_r
    for br, Y in enumerate((YN, YM)):
        for k in range(BT):
            m = p.halves(R[:, br * 8 + k, 0:TOK], R[:, br * 8 + 4 + k, 0:TOK], Y[:, k, :])
    pe.wait(m)
    dve.wait(m)

    def gated(i):
        return (lambda k: R[:, i * 8 + k, 0:TOK]), (lambda k: R[:, i * 8 + (4 + k), 0:TOK])
    m = p.merge(2, TOK, gated)
    act.wait(m)
    dve.wait(m)
    for k in range(KT):
        m = p.halves(p.hhi[:, k, 0:TOK], p.hlo[:, k, 0:TOK], p.y[:, k, 0:TOK], 0.5)
    pe.wait(m)
    for o in range(KT):
        b = p.bank()
        u = p.tile(p.feature_tile(TOK, bank=b))
        dve.wait(u)
        p.release(v.tensor_tensor(p.x[:, o, 0:TOK], p.x[:, o, 0:TOK], b[:, 0:TOK], ALU.add))

    h = second_norm(p, "g_ffn", (p.free, p.free.value()))
    pe.wait(h)
    ah = R[:, 0:11, :].rearrange("p a (b t) -> p (a b) t", t=TOK)
    al = R[:, 11:22, :].rearrange("p a (b t) -> p (a b) t", t=TOK)

    def ffn_pair(f):
        e = p.free.off % 4
        up, gt = p.bank(), p.M[e]
        ug = p.tile(p.feature_tile(TOK, bank=gt))
        uu = p.tile(p.feature_tile(TOK, bank=up))
        act.wait(ug)
        act.eng.wait_ge(p.free.sem, p.free.value(-1))
        th = p.tmp[:, e % 2, 0:TOK]
        a = act.mark(nc.scalar.activation(th, gt[:, 0:TOK], ACT.Tanh, scale=0.5))
        dve.wait(a)
        dve.mark(v.scalar_tensor_tensor(th, th, 1.0, gt[:, 0:TOK], ALU.add, ALU.mult))
        dve.wait(uu)
        dve.settle()
        d = dve.mark(v.tensor_tensor(th, th, up[:, 0:TOK], ALU.mult))
        act.wait(d)
        a = act.mark(nc.scalar.activation(ah[:, f, :], th, ACT.Copy, scale=0.5))
        dve.wait(a)
        p.release(v.scalar_tensor_tensor(al[:, f, :], th, 0.5, ah[:, f, :].bitcast(F32), ALU.mult, ALU.subtract))
    with p.roll(5, tile=8, bank=4, act=8, dve=8) as i:
        for j in range(4):
            ffn_pair(i * 4 + j)
    for f in range(20, FT):
        ffn_pair(f)
    last = (p.free, p.free.value())
    pe.wait(last)
    out_banks = p.G + p.M

    def down(k, first, final):
        def products(hi, lo):
            for o in range(KT):
                c = slice(o * P, (o + 1) * P)
                m = p.three(out_banks[o][:, 0:TOK], hi[:, c], lo[:, c], ah[:, k, :], al[:, k, :], first, final)
            return m
        return p.tile(products)
    for k in range(2):
        down(k, k == 0, False)
    with p.roll(4, tile=4) as i:
        for j in range(4):
            down(i * 4 + (2 + j), False, False)
    for k in range(18, FT):
        u = down(k, False, k == FT - 1)
    dve.wait(u)
    for o in range(KT):
        d = dve.mark(v.tensor_tensor(p.x[:, o, 0:TOK], p.x[:, o, 0:TOK], out_banks[o][:, 0:TOK], ALU.add))
    pe.wait(d)
    dve.settle()

    h = second_norm(p, "g_ple", d)
    p.need(act, "ple")
    p.need(dve, "ple")
    ph, pl = R[:, 22, :], R[:, 23, :]
    m = p.halves(ph, pl, L["ple"])
    pe.wait(h, m)
    for o in range(KT):
        b = p.bank()
        u = p.tile(p.feature_tile(TOK, bank=b))
        act.wait(u)
        p.release(nc.scalar.activation(p.y[:, o, 0:TOK], b[:, 0:TOK], ACT.Tanh, scale=0.5))
    dve.wait((p.free, p.free.value()))
    outs = []
    for g in range(2):
        def products(hi, lo):
            for o in range(4):
                for k in range(2):
                    c = slice((o * 2 + k) * P, (o * 2 + k + 1) * P)
                    t = slice(k * TOK, (k + 1) * TOK)
                    m = p.three(p.M[o][:, 0:TOK], hi[:, c], lo[:, c], ph[:, t], pl[:, t], k == 0, k == 1)
            return m
        u = p.tile(products)
        dve.wait(u)
        for o in range(4):
            k = 4 * g + o
            yk, xk = p.y[:, k, 0:TOK], p.x[:, k, 0:TOK]
            d = dve.mark(v.scalar_tensor_tensor(yk, yk, 1.0, p.M[o][:, 0:TOK], ALU.add, ALU.mult))
            dve.settle()
            outs.append(dve.mark(v.scalar_tensor_tensor(xk, yk, 0.5, xk, ALU.mult, ALU.add)))
        pe.wait(d)
        nc.sync.wait_ge(outs[-1][0].sem, outs[-1][1])
        nc.sync.dma_start(p.out[:, 4 * g:4 * g + 4, :], p.x[:, 4 * g:4 * g + 4, 0:TOK]).then_inc(p.stored, 16)
    nc.sync.wait_ge(p.stored, 32)


SMALL = ["cond", "ident", "norm_pre0", "norm_post0", "ada_b0", "norm_pre1", "norm_post1", "ada_b1", "lambda",
         "rope", "perm1", "subln0", "subln1", "hy_z"] + \
    [f"hy_{n}{l}" for l in range(2) for n in ("w1", "b1", "w2", "b2", "freq", "sw", "bias")] + \
    ["inv_freq", "head_gain", "causal", "cmp_add", "cmp_keep", "perm2", "head_sum",
     "block_mean", "pe_k", "pe_v", "g_mix", "g_ffn", "g_ple"]


def program(nc, ins, out):
    with ExitStack() as ctx:
        p = Program(nc, ctx, ins, out)
        p.stored = p.sem("stored")
        for s in range(2):
            n = ("x", "ctx")[s]
            p.load(n, p.x[:, :, s * TOK:(s + 1) * TOK])
        for n in SMALL:
            p.load(n)
        p.load("pos", dt=I32)
        p.shared = p.sb("shared", [P, 2048])
        p.load("dft", p.shared[:, 0:1024].rearrange("p (a n) -> p a n", a=2))
        p.load("idft", p.shared[:, 1024:2048].rearrange("p (a n) -> p a n", a=4))
        p.stream()
        p.constants()
        for line in (p.act, p.dve, p.pe):
            p.need(line, "x", "ctx")
        p.condition()
        for _ in range(AHEAD):
            p.split()
        x_mark = p.const
        for l in range(DEPTH):
            gated, n = block1_layer(p, l, x_mark)
            m = p.merge(3, n, gated)
            x_mark = block1_out(p, n, m, x_mark)
            for line in (p.act, p.dve, p.pe):
                line.wait(x_mark)
        block2(p, x_mark)
        assert p.used.off == TILES, (p.used.off, TILES)


def _columns(w):
    k, n = w.shape
    return w.reshape(k // P, P, n // P, P).transpose(2, 1, 0, 3).reshape(n // P, P, k)


def _rows(w):
    return w.reshape(4, 2, P, 512).transpose(0, 2, 1, 3).reshape(4, P, 1024)


def _feat(a):
    t, f = a.shape
    return a.T.reshape(f // P, P, t).transpose(1, 0, 2)


def _vec(a):
    return a.reshape(-1, P).T


def _layout(i):
    tiles = []

    def merged(ws, gates):
        for w, g in zip(ws, gates):
            b, s = _columns(w), _columns(g)
            for pair in range(4):
                tiles.append(np.concatenate([b[2 * pair], b[2 * pair + 1]], axis=1)[None])
                tiles.append(s[2 * pair:2 * pair + 2])
    for l in range(DEPTH):
        w = i["w_in"][l]
        tiles.append(_columns(i["ada_w"][l]))
        tiles.append(_columns(w[:, 0:512]))
        tiles.append(_columns(w[:, 1024:1536]))
        tiles.append(_rows(w[:, 512:1024]))
        tiles.append(_columns(w[:, 2048:3584]))
        tiles.append(_columns(w[:, 4096:4608]))
        tiles.append(_rows(w[:, 4608:5120]))
        for g in (1536, 3584, 5120):
            tiles.append(_columns(w[:, g:g + 512]))
        merged(list(i["w_branch"][l]), [w[:, 5632 + b * D:5632 + (b + 1) * D] for b in range(3)])
        tiles.append(_columns(i["w_out"][l]))
    w = i["w_in_2"][0]
    order = [h for j in range(4) for h in (j, 4 + j)]
    heads = np.concatenate([np.arange(h * 64, h * 64 + 64) for h in order])
    tiles.append(_columns(w[:, heads]))
    for c in (512, 640, 768, 1024):
        tiles.append(_columns(w[:, c:c + P]))
    tiles.append(_columns(w[:, 1304:1816]))
    tiles.append(_columns(w[:, 1816:2328]))
    tiles.append(_rows(w[:, 2328:2840]))
    vsg = np.zeros((D, 512), w.dtype)
    vsg[:, 0:128], vsg[:, 128:256], vsg[:, 256:280] = w[:, 896:1024], w[:, 1152:1280], w[:, 1280:1304]
    tiles.append(_rows(vsg))
    for n in ("nsa_ck_w1_2", "nsa_cv_w1_2"):
        tiles.append(i[n][0].reshape(4, 4, P, 256).transpose(0, 2, 1, 3).reshape(4, P, 1024))
    merged([i["w_up_nsa_2"][0][heads], i["w_up_moba_2"][0]], [w[:, 2840:3864], w[:, 3864:4888]])
    tiles.append(_columns(i["w_out_2"][0]))
    f = i["w_ffn_in_2"][0]
    g, u = _columns(f[:, :D_FF]), _columns(f[:, D_FF:])
    tiles.append(np.stack([g, u], axis=1).reshape(2 * FT, P, D))
    tiles.append(i["w_ffn_out_2"][0].reshape(FT, P, D))
    tiles.append(_columns(i["w_ple_gate_2"][0]))
    tiles.append(i["w_ple_proj_2"][0].reshape(2, P, 2, 4, P).transpose(2, 1, 3, 0, 4).reshape(2, P, 1024))
    a = {"stream": np.concatenate(tiles)}
    assert a["stream"].shape == (TILES, P, 1024), a["stream"].shape

    a["x"], a["ctx"] = _feat(i["x"][0]), _feat(i["ctx"][0])
    a["cond"] = np.stack([_vec(i["c"][0]), _vec(i["c_ctx"])], axis=2)
    a["lambda"] = np.broadcast_to(i["da_lambda"], (P,) + i["da_lambda"].shape)
    for l in range(DEPTH):
        a[f"ada_b{l}"], a[f"norm_pre{l}"], a[f"norm_post{l}"] = _vec(i["ada_b"][l]), _vec(i["norm_pre"][l]), _vec(i["norm_post"][l])
        a[f"subln{l}"] = i["da_subln"][l][:, None]
        a[f"hy_w1{l}"], a[f"hy_w2{l}"], a[f"hy_w3{l}"] = i["hy_f_w1"][l], i["hy_f_w2"][l], i["hy_f_w3"][l]
        a[f"hy_b1{l}"], a[f"hy_b2{l}"] = i["hy_f_b1"][l][:, None], i["hy_f_b2"][l][:, None]
        a[f"hy_freq{l}"] = i["hy_f_freq"][l].T
        a[f"hy_sw{l}"] = np.stack([_vec(r) for r in (*i["hy_short_w"][l], i["hy_short_b"][l])], axis=2)
        a[f"hy_bias{l}"] = _vec(i["hy_bias"][l])
        a[f"ln_g{l}"], a[f"ln_b{l}"] = (np.broadcast_to(i[n][l], (P, BR)) for n in ("gm_ln_g", "gm_ln_b"))
        a[f"gm_ws{l}"] = i["gm_ws"][l].transpose(2, 0, 1)
        a[f"gm_bs{l}"] = np.repeat(i["gm_bs"][l], 64, axis=0).reshape(4, P, P).transpose(1, 0, 2)
    a["pos"] = np.broadcast_to(i["positions_2"], (P, TOK))
    a["ple"] = _feat(i["p_2"][0, 0]).reshape(P, 2 * TOK)
    for n in ("g_mix", "g_ffn", "g_ple"):
        a[n] = _vec(i[n + "_2"][0])
    a["ck_w2"], a["cv_w2"] = (i[n][0].reshape(2, P, 64).transpose(1, 0, 2) for n in ("nsa_ck_w2_2", "nsa_cv_w2_2"))
    a["pe_k"], a["pe_v"] = (i[n][0].reshape(16, P).T for n in ("nsa_pe_k_2", "nsa_pe_v_2"))
    gains = ["nsa_q_gain_2"] * 4 + ["nsa_ks_gain_2", "nsa_kw_gain_2"] + ["moba_q_gain_2"] * 4 + ["moba_k_gain_2"] * 4 + ["nsa_kc_gain_2"]
    a["head_gain"] = np.stack([np.tile(i[n][0], 2) for n in gains], axis=1)

    f = np.float32
    a["ident"] = np.eye(P, dtype=f)
    d = np.arange(P)
    inv = (f(10000.0) ** (-np.arange(16, dtype=f) / f(16))).astype(f)
    t = np.arange(TOK)
    coord = np.where((d[:, None] % 64) < 32, t[None, :] // 64, t[None, :] % 64).astype(f)
    ang = (coord * inv[d % 16][:, None]).astype(f).astype(np.float64)
    a["rope"] = np.stack([np.cos(ang), np.sin(ang)], axis=1).astype(f)

    def rotation(half, width, rotated):
        m = np.zeros((P, P), f)
        for x in range(P):
            if x % 64 < rotated:
                if x % width < half:
                    m[x + half, x] = -1.0
                else:
                    m[x - half, x] = 1.0
        return m
    a["perm1"], a["perm2"] = rotation(16, 32, 64), rotation(8, 16, 16)
    inv2 = (f(500000.0) ** (-np.arange(8, dtype=f) / f(8))).astype(f)
    a["inv_freq"] = np.where(d % 64 < 16, inv2[d % 8], f(0.0)).astype(f)[:, None]
    lt = np.linspace(0.0, 1.0, TOK, dtype=f)[:, None]
    wpos = (f(2.0 * math.pi / TOK) * np.arange(TOK, dtype=f))[:, None]
    bands = np.linspace(1e-4, 15, 16, dtype=f)[None, :]
    bw = (bands * wpos).astype(np.float64)
    a["hy_z"] = np.concatenate([lt, np.cos(bw), -np.sin(bw)], axis=1).astype(f).T
    deltas = np.abs(np.linspace(math.log(1e-2) / 1.5, math.log(1e-2) / 0.3, BR, dtype=f))
    a["hy_decay"] = np.exp((-lt * deltas).astype(np.float64)).astype(f).reshape(2, P, BR).transpose(1, 0, 2)
    w = 2.0 * math.pi * (np.arange(TOK) + 0.5) / 512.0
    c, s = np.cos(w[None, :] * t[:, None]), -np.sin(w[None, :] * t[:, None])
    a["dft"] = np.concatenate([c, s], axis=1).astype(f).reshape(2, P, 512).transpose(1, 0, 2)
    a["idft"] = (np.concatenate([c.T, s.T], axis=0) / TOK).astype(f).reshape(4, P, TOK).transpose(1, 0, 2)
    q, k = np.arange(P)[:, None], np.arange(P)[None, :]
    a["causal"] = np.concatenate([np.zeros((P, P), f), np.where(k <= q, 0.0, NEG).astype(f)], axis=1)
    end = np.arange(NCMP) * 16 + 31
    keep = (end[None, None, :] <= (np.arange(P)[:, None, None] + P * np.arange(2)[None, :, None]))
    a["cmp_keep"], a["cmp_add"] = keep.astype(f), np.where(keep, 0.0, NEG).astype(f)
    hs = np.zeros((P, 14, 32), f)
    sp = np.zeros((32, 14, P), f)
    for n in range(14):
        for half in range(2):
            hs[half * 64:half * 64 + 64, n, 2 * n + half] = 1.0 / 64
            sp[2 * n + half, n, half * 64:half * 64 + 64] = 1.0
    a["head_sum"], a["head_spread"] = hs, sp
    a["block_mean"] = np.kron(np.eye(2, dtype=f), np.full((64, 64), 1.0 / 64, f))
    return {n: np.ascontiguousarray(x) for n, x in a.items()}


def kernel(**inputs):
    import concourse.bacc as bacc
    from concourse.bass_utils import run_bass_kernel_spmd

    arrays = _layout({n: np.asarray(x) for n, x in inputs.items()})
    nc = bacc.Bacc("TRN2", target_bir_lowering=False, num_devices=1)
    ins = {n: nc.dram_tensor(f"in_{n}", x.shape, mybir.dt.from_np(x.dtype), kind="ExternalInput").ap() for n, x in arrays.items()}
    out = nc.dram_tensor("out", (P, KT, TOK), F32, kind="ExternalOutput").ap()
    program(nc, ins, out)
    r = run_bass_kernel_spmd(nc, [{f"in_{n}": x for n, x in arrays.items()}], core_ids=[0])
    y = r.results[0]["out"]
    return y.transpose(2, 1, 0).reshape(1, TOK, D)
```

```python
import math
from contextlib import ExitStack, contextmanager

import numpy as np

import concourse.bass as bass
from concourse import mybir

F32 = mybir.dt.float32
F32R = mybir.dt.float32r
I32 = mybir.dt.int32
ACT = mybir.ActivationFunctionType
ALU = mybir.AluOpType
AXX = mybir.AxisListType.X

P = 128
D = 1024
KT = D // P
TOK = 256
ALL = 2 * TOK
BR = 512
BT = BR // P
HEADS = 4
DEPTH = 2
EPS = 1e-6
RAW = 4
SPLIT = 4
AHEAD = 2
D_FF = 2816
FT = D_FF // P
NCMP = 15
NEG = -1e30
TWO_PI = 2.0 * math.pi
MAGIC = 1.5 * 2.0 ** 23
LAYER_TILES = 24 + 4 + 4 + 4 + 12 + 4 + 4 + 12 + 36 + 8
TILES = DEPTH * LAYER_TILES + 8 + 8 + 4 + 4 + 4 + 4 + 24 + 8 + 2 * FT + FT + 8 + 2


def pi_parts():
    parts, rest = [], TWO_PI
    for _ in range(3):
        scale = 2.0 ** (8 - math.ceil(math.log2(rest)))
        part = math.floor(rest * scale) / scale
        parts.append(part)
        rest -= part
    return parts + [float(np.float32(rest))]


class Count:

    def __init__(self, sem):
        self.sem, self.off, self.sym = sem, 0, None

    def value(self, k=0):
        v = self.off + k
        return v if self.sym is None else self.sym + v


class Line:

    def __init__(self, eng, sem):
        self.eng, self.count = eng, Count(sem)

    def mark(self, ins):
        ins.then_inc(self.count.sem, 1)
        self.count.off += 1
        return (self.count, self.count.value())

    def wait(self, *marks):
        for m in marks:
            if m is not None:
                self.eng.wait_ge(m[0].sem, m[1])

    def last(self):
        return (self.count, self.count.value())

    def settle(self):
        self.eng.wait_ge(self.count.sem, self.count.value())


class Program:
    def __init__(self, nc, ctx, ins, out):
        self.nc, self.ctx, self.ins, self.out = nc, ctx, ins, out
        self.act = Line(nc.scalar, self.sem("act"))
        self.dve = Line(nc.vector, self.sem("dve"))
        self.pe = Line(nc.tensor, self.sem("pe"))
        self.hi = Count(self.sem("tile_hi"))
        self.lo = Count(self.sem("tile_lo"))
        self.used = Count(self.sem("tile_used"))
        self.free = Count(self.sem("bank_free"))
        self.arrived = [self.sem(f"tile_arrived{r}") for r in range(RAW)]
        self.split_at = 0
        self.sym_tile = None
        self.loads = {}
        self.fillers = []
        self.G = [ctx.enter_context(nc.psum_tensor(f"gemm_bank{i}", [P, 512], F32)) for i in range(4)]
        self.M = [ctx.enter_context(nc.psum_tensor(f"misc_bank{i}", [P, 512], F32)) for i in range(4)]
        sb = self.sb
        self.raw = sb("raw", [P, RAW, 1024])
        self.whi = sb("whi", [P, SPLIT, 1024], F32R)
        self.wlo = sb("wlo", [P, SPLIT, 1024], F32R)
        self.x = sb("x", [P, KT, ALL])
        self.hhi = sb("hhi", [P, KT, ALL], F32R)
        self.hlo = sb("hlo", [P, KT, ALL], F32R)
        at = nc.sbuf_base
        self.arena = sb("arena", [P, 24, ALL])
        self.arena_r = nc.alloc_sbuf_tensor_at("arena_r", [P, 24, ALL], F32R, offset=at)
        self.y = sb("y", [P, 12, ALL])
        self.tmp = sb("tmp", [P, 5, ALL])
        self.kre, self.kim = self.y[:, 8:10, :], self.y[:, 10:12, :]
        self.wt = self.y[:, 4:6, :].rearrange("p a (b q) -> p (a b) q", q=TOK)
        self.stat = sb("stat", [P, 40])
        self.hy_rs = sb("hy_rs", [P, BT])

    def sem(self, name):
        return self.ctx.enter_context(self.nc.semaphore(name))

    def sb(self, name, shape, dt=F32):
        return self.ctx.enter_context(self.nc.sbuf_tensor(name, shape, dt))

    def load(self, name, dst=None, src=None, dt=F32, eng=None):
        src = self.ins[name] if src is None else src
        if dst is None:
            dst = self.sb(name + "_sb", list(src.shape), dt)[:]
        s = self.sem("in_" + name)
        (eng or self.nc.scalar).dma_start(dst, src).then_inc(s, 16)
        self.loads[name] = (dst, s)
        return dst

    def need(self, line, *names):
        for n in names:
            line.eng.wait_ge(self.loads[n][1], 16)

    @contextmanager
    def roll(self, n, **step):
        counts = {"act": self.act.count, "dve": self.dve.count, "pe": self.pe.count, "tile": self.used, "bank": self.free}
        start = {k: c.off for k, c in counts.items()}
        hi0, split0 = self.hi.off, self.split_at
        assert step["tile"] % SPLIT == 0 and step.get("bank", 0) % 4 == 0
        eng = (mybir.EngineType.PE, mybir.EngineType.Activation, mybir.EngineType.DVE)
        with self.nc.Fori(0, n, 1, engines=eng) as i:
            for k, c in counts.items():
                c.sym = i * step.get(k, 0) if step.get(k, 0) else None
            self.sym_tile = i * step["tile"]
            self.turns = n
            yield i
        for k, c in counts.items():
            assert c.off == start[k] + step.get(k, 0), (k, c.off - start[k], step.get(k, 0))
            c.off = start[k] + n * step.get(k, 0)
            c.sym = None
        self.split_at = split0 + n * step["tile"]
        self.sym_tile = None

    def plus(self, v):
        return v if self.sym_tile is None else self.sym_tile + v

    def fill(self, n=1):
        while n and self.fillers:
            self.fillers.pop(0)()
            n -= 1

    def stream(self):
        sp, w, s_lo = self.nc.sync, self.ins["stream"], self.lo.sem
        for r in range(RAW):
            sp.dma_start(self.raw[:, r, :], w[r]).then_inc(self.arrived[r], 16)
        turns, rest = divmod(TILES - RAW, RAW)
        with sp.Fori(0, turns, 1) as i:
            for r in range(RAW):
                sp.wait_ge(s_lo, i * RAW + (r + 1))
                sp.dma_start(self.raw[:, r, :], w[i * RAW + (RAW + r)]).then_inc(self.arrived[r], 16)
        for r in range(rest):
            sp.wait_ge(s_lo, turns * RAW + r + 1)
            sp.dma_start(self.raw[:, r, :], w[turns * RAW + RAW + r]).then_inc(self.arrived[r], 16)

    def split(self):
        if self.sym_tile is None and self.split_at >= TILES:
            return
        t, act, dve = self.split_at, self.nc.scalar, self.nc.vector
        self.split_at += 1
        r, s = t % RAW, t % SPLIT
        turn = self.plus(t - r) if self.sym_tile is not None else t - r
        act.wait_ge(self.arrived[r], turn * (16 // RAW) + 16)
        if t >= SPLIT:
            act.wait_ge(self.used.sem, self.plus(t - SPLIT + 1))
        act.activation(self.whi[:, s, :], self.raw[:, r, :], ACT.Copy).then_inc(self.hi.sem, 1)
        dve.wait_ge(self.hi.sem, self.plus(t + 1))
        dve.tensor_tensor(self.wlo[:, s, :], self.raw[:, r, :], self.whi[:, s, :].bitcast(F32), ALU.subtract).then_inc(self.lo.sem, 1)

    def tile(self, products):
        self.split()
        t = self.used.off
        self.nc.tensor.wait_ge(self.lo.sem, self.plus(t + 1))
        s = t % SPLIT
        last = products(self.whi[:, s, :], self.wlo[:, s, :])
        last.then_inc(self.used.sem, 1)
        self.used.off += 1
        return (self.used, self.used.value())

    def bank(self):
        e = self.free.off
        if e >= 4:
            self.nc.tensor.wait_ge(self.free.sem, self.free.value(-3))
        return self.G[e % 4]

    def release(self, ins):
        ins.then_inc(self.free.sem, 1)
        self.free.off += 1
        return (self.free, self.free.value())

    def three(self, out, w_hi, w_lo, r_hi, r_lo, first, last):
        mm = self.nc.tensor.matmul
        mm(out, w_lo, r_hi, start=first, stop=False)
        mm(out, w_hi, r_lo, start=False, stop=False)
        return mm(out, w_hi, r_hi, start=False, stop=last)

    def feature_tile(self, n, rhs=None, col=0, nk=KT, bank=None):
        r_hi, r_lo = rhs or (self.hhi, self.hlo)

        def products(hi, lo):
            for k in range(nk):
                c = slice(col + k * P, col + (k + 1) * P)
                m = self.three(bank[:, 0:n], hi[:, c], lo[:, c], r_hi[:, k, 0:n], r_lo[:, k, 0:n], k == 0, k == nk - 1)
            return m
        return products

    def token_gemm(self, ntt, evacuate, width=512):
        banks = []

        def one(g):
            def run():
                if g == 0:
                    for j in range(ntt):
                        self.nc.tensor.wait_ge(self.free.sem, self.free.value(j - 3))
                        banks.append(self.G[(self.free.off + j) % 4])

                def products(hi, lo):
                    for kk in range(2):
                        k = 2 * g + kk
                        c = slice(kk * 512, kk * 512 + width)
                        for j in range(ntt):
                            tk = slice(j * P, (j + 1) * P)
                            m = self.three(banks[j][:, 0:width], self.hhi[:, k, tk], self.hlo[:, k, tk], hi[:, c], lo[:, c], k == 0, k == KT - 1)
                    return m
                u = self.tile(products)
                if g == 3:
                    self.act.wait(u)
                    for j in range(ntt):
                        self.release(evacuate(j, banks[j]))
            return run
        return [one(g) for g in range(4)]

    def feature_gemm(self, tiles, n, evacuate):
        def one(j):
            def run():
                b = self.bank()
                u = self.tile(self.feature_tile(n, bank=b))
                self.release(evacuate(j, b, u))
            return run
        return [one(j) for j in range(tiles)]

    def halves(self, hi, lo, src, scale=1.0, waits=()):
        self.act.wait(*waits)
        a = self.act.mark(self.nc.scalar.activation(hi, src, ACT.Copy, scale=scale))
        self.dve.wait(a)
        return self.dve.mark(self.nc.vector.scalar_tensor_tensor(lo, src, scale, hi.bitcast(F32), ALU.mult, ALU.subtract))

    def rms(self, src, n, tiles, dst, waits):
        nc, bank = self.nc, self.M[0]
        self.act.wait(*waits)
        self.pe.wait(*waits)
        self.act.settle()
        done = [None, None]
        for k in range(tiles):
            self.act.wait(done[k % 2])
            a = self.act.mark(nc.scalar.activation(self.tmp[:, k % 2, 0:n], src[:, k, 0:n], ACT.Square))
            self.pe.wait(a)
            done[k % 2] = self.pe.mark(nc.tensor.matmul(bank[:, 0:n], self.mean_all, self.tmp[:, k % 2, 0:n], start=(k == 0), stop=(k == tiles - 1)))
        return self.rsqrt(dst[:, 0:n], bank[:, 0:n], done[(tiles - 1) % 2])

    def rsqrt(self, dst, src, mark, bias=None):
        p = dst.shape[0]
        self.act.wait(mark)
        a = self.act.mark(self.nc.scalar.activation(dst, src, ACT.Sqrt, bias=(self.eps if bias is None else bias)[0:p, :]))
        self.dve.wait(a)
        return self.dve.mark(self.nc.vector.reciprocal(dst, dst))

    def sine(self, dst, arg, tmp, mark, p, big=False, shift=0.0):
        v, dve = self.nc.vector, self.dve
        k = tmp
        parts = pi_parts()
        dve.wait(mark)

        def go(ins):
            dve.mark(ins)
            dve.settle()
        for stage in ([4096.0] if big else []) + [1.0]:
            sh = shift if stage == 1.0 else 0.0
            go(v.tensor_scalar(k, arg, 1.0 / (TWO_PI * stage), sh / TWO_PI, ALU.mult, ALU.add))
            go(v.tensor_scalar(k, k, MAGIC, None, ALU.add))
            go(v.tensor_scalar(k, k, MAGIC, None, ALU.subtract))
            for c in parts:
                go(v.scalar_tensor_tensor(arg, k, -c * stage, arg, ALU.mult, ALU.add))
        if shift:
            go(v.tensor_scalar(arg, arg, shift, None, ALU.add))
        go(v.tensor_scalar(arg, arg, 3.1415925, -3.1415925, ALU.min, ALU.max))
        self.act.wait(dve.last())
        return self.act.mark(self.nc.scalar.activation(dst, arg, ACT.Sin))

    def constants(self):
        nc, dve = self.nc, self.nc.vector
        self.mean_all = self.sb("mean_all", [P, P])[:]
        self.ident = self.loads["ident"][0]
        self.mean_128 = self.sb("mean_128", [P, P])[:]
        self.ones = self.sb("ones", [P, 1])[:]
        self.eps = self.sb("eps", [P, 1])[:]
        self.zero = self.sb("zero", [P, 1])[:]
        for ap, v in ((self.mean_all, 1.0 / D), (self.mean_128, 1.0 / P), (self.ones, 1.0), (self.eps, EPS), (self.zero, 0.0)):
            self.dve.mark(dve.memset(ap, v))
        self.const = self.dve.last()
        self.need(self.pe, "ident")
        for line in (self.act, self.pe, self.dve):
            line.wait(self.const)

    def condition(self):
        nc = self.nc
        self.chi = self.sb("chi", [P, KT, 2], F32R)
        self.clo = self.sb("clo", [P, KT, 2], F32R)
        c = self.loads["cond"][0]
        th = self.sb("c_tanh", [P, KT, 2])[:]
        self.need(self.act, "cond")
        self.need(self.dve, "cond")
        a = self.act.mark(nc.scalar.activation(th, c, ACT.Tanh, scale=0.5))
        self.dve.wait(a)
        d = self.dve.mark(nc.vector.scalar_tensor_tensor(th, th, 1.0, c, ALU.add, ALU.mult))
        self.dve.settle()
        self.cond_mark = self.halves(self.chi[:], self.clo[:], th, 0.5, (d,))
        self.mods = [self.sb(f"mod{l}", [P, 24, 2]) for l in range(DEPTH)]
        self.A = self.sb("modA", [P, KT, 2])

    def modulation_gemm(self, l, rows):
        nc, act, pe, dve = self.nc, self.act, self.pe, self.dve
        banks = []

        def one(c, k):
            def run():
                if k == 0:
                    if c == 0:
                        pe.wait(self.cond_mark)
                    banks.clear()
                    for j in range(2):
                        if self.free.off + j >= 4:
                            nc.tensor.wait_ge(self.free.sem, self.free.value(j - 3))
                        banks.append(self.G[(self.free.off + j) % 4])

                def products(hi, lo):
                    for j in range(2):
                        m = self.three(banks[j][0:2, :], self.chi[:, k, :], self.clo[:, k, :], hi[:, j * 512:(j + 1) * 512], lo[:, j * 512:(j + 1) * 512], k == 0, k == KT - 1)
                    return m
                u = self.tile(products)
                if k == KT - 1:
                    act.wait(u)
                    if c:
                        act.wait(self.turned)
                    for j in range(2):
                        done = self.release(nc.scalar.activation(rows[:, j, :], banks[j][0:2, :], ACT.Copy))
                    b = self.bank()
                    pe.wait(done)
                    for m in range(8):
                        t = nc.tensor.transpose(b[:, 2 * m:2 * m + 2], rows[:, m // 4, (m % 4) * P:(m % 4 + 1) * P], self.ident[0:2, 0:2])
                    self.turned = pe.mark(t)
                    dve.wait(self.turned)
                    self.release(nc.vector.tensor_copy(self.mods[l][:, 8 * c:8 * c + 8, :], b[:, 0:16].rearrange("p (m s) -> p m s", s=2)))
            return run
        return [one(c, k) for c in range(3) for k in range(KT)]

    def modulation(self, l):
        nc = self.nc
        self.mod = self.mods[l]
        self.need(self.dve, f"ada_b{l}", f"norm_pre{l}", f"norm_post{l}")
        v, dve = nc.vector, self.dve
        self.dve.wait((self.free, self.free.value()))

        def bc(name, n):
            return self.loads[name][0].unsqueeze(2).broadcast_to([P, n, 2])
        dve.mark(v.tensor_tensor(self.mod[:], self.mod[:], bc(f"ada_b{l}", 24), ALU.add))
        dve.settle()
        dve.mark(v.scalar_tensor_tensor(self.A[:], self.mod[:, 8:16, :], 1.0, bc(f"norm_pre{l}", 8), ALU.add, ALU.mult))
        dve.mark(v.tensor_tensor(self.mod[:, 16:24, :], self.mod[:, 16:24, :], bc(f"norm_post{l}", 8), ALU.mult))
        return dve.last()

    def pre_norm(self, mod_mark, x_mark):
        nc = self.nc
        r = self.tmp[:, 2, :]
        m = self.rms(self.x, ALL, KT, self.tmp[:, 2, :], (x_mark,))
        self.dve.wait(m)
        self.act.wait(mod_mark)
        done = [None, None]
        for k in range(KT):
            t = self.tmp[:, 3 + k % 2, :]
            self.dve.wait(done[k % 2])
            d = self.dve.mark(nc.vector.tensor_tensor(t, self.x[:, k, :], r, ALU.mult))
            self.act.wait(d)
            for s in range(2):
                c = slice(s * TOK, (s + 1) * TOK)
                self.act.mark(nc.scalar.activation(t[:, c], t[:, c], ACT.Identity, bias=self.mod[:, k, s:s + 1], scale=self.A[:, k, s:s + 1]))
            self.act.settle()
            done[k % 2] = self.halves(self.hhi[:, k, :], self.hlo[:, k, :], t)
        return self.dve.last()

    def lam(self, l):
        nc, v, dve = self.nc, self.nc.vector, self.dve
        src = self.loads["lambda"][0]
        self.need(dve, "lambda")
        t = self.sb(f"lam_t{l}", [P, 2, 64])[:]
        e = self.sb(f"lam_e{l}", [P, 4])[:]
        for j in range(2):
            dve.mark(v.tensor_tensor(t[:, j, :], src[:, l, 2 * j, :], src[:, l, 2 * j + 1, :], ALU.mult))
        dve.settle()
        d = dve.mark(v.tensor_reduce(e[:, 0:2], t, AXX, ALU.add))
        self.act.wait(d)
        a = self.act.mark(nc.scalar.activation(e[:, 0:2], e[:, 0:2], ACT.Exp))
        dve.wait(a)
        dve.mark(v.tensor_tensor(e[:, 2:3], e[:, 1:2], e[:, 0:1], ALU.subtract))
        dve.settle()
        dve.mark(v.tensor_scalar(e[:, 3:4], e[:, 2:3], -(0.8 - 0.6 * math.exp(-0.3 * l)), None, ALU.add))
        dve.settle()
        return e[:, 3:4]

    def rope(self, ap, n, cos, sin, perm, mark, bank, tmp):
        nc, v, dve = self.nc, self.nc.vector, self.dve
        self.pe.wait(mark)
        p = self.pe.mark(nc.tensor.matmul(bank[:, 0:n], perm, ap, start=True, stop=True))
        dve.wait(p)
        dve.mark(v.tensor_tensor(tmp[:, 0:n], bank[:, 0:n], sin, ALU.mult))
        dve.mark(v.tensor_tensor(ap, ap, cos, ALU.mult))
        dve.settle()
        return dve.mark(v.tensor_tensor(ap, ap, tmp[:, 0:n], ALU.add))

    def diff_attention(self, l, parts, Kt, Qt, V, neg_lam, marks):
        nc, v, dve, act, pe = self.nc, self.nc.vector, self.dve, self.act, self.pe
        st = self.stat
        S = (self.M[0], self.M[1])
        units = [(part, h, i) for part in parts for h in range(HEADS) for i in range(2)]
        pe.wait(*marks)
        dve.wait(*marks)
        w_read = [None, None]
        wt_copied, pv_done, out_done, exp_done = [], [None], [None], [None]

        def scores(u):
            (q_off, k_off, nkeys), h, i = units[u]
            q = slice(q_off + i * P, q_off + (i + 1) * P)
            pe.wait(exp_done[0])
            for m in range(2):
                r = slice(m * 64, (m + 1) * 64)
                p = pe.mark(nc.tensor.matmul(S[m][:, 0:nkeys], Qt[r, h, q], Kt[r, h, k_off:k_off + nkeys], start=True, stop=True))
            return p

        def softmax(u, s_mark):
            nkeys = units[u][0][2]
            c = 10 * (u % 2)
            dve.wait(s_mark)
            for m in range(2):
                dve.mark(v.tensor_reduce(st[:, c + m:c + m + 1], S[m][:, 0:nkeys], AXX, ALU.max, negate=True))
            dve.settle()
            act.wait(dve.mark(v.tensor_scalar(st[:, c + 2:c + 4], st[:, c:c + 2], 0.125, None, ALU.mult)))
            for m in range(2):
                exp_done[0] = act.mark(nc.scalar.activation(self.tmp[:, m, 0:nkeys], S[m][:, 0:nkeys], ACT.Exp, bias=st[:, c + 2 + m:c + 3 + m], scale=0.125, accum_out=st[:, c + 4 + m:c + 5 + m]))

        def weights(u):
            nkeys = units[u][0][2]
            c = 10 * (u % 2)
            dve.wait(exp_done[0])
            dve.mark(v.reciprocal(st[:, c + 6:c + 8], st[:, c + 4:c + 6]))
            dve.settle()
            dve.mark(v.tensor_tensor(st[:, c + 7:c + 8], st[:, c + 7:c + 8], neg_lam, ALU.mult))
            dve.mark(v.tensor_scalar(self.tmp[:, 0, 0:nkeys], self.tmp[:, 0, 0:nkeys], st[:, c + 6:c + 7], None, ALU.mult))
            dve.settle()
            dve.wait(w_read[0])
            return dve.mark(v.scalar_tensor_tensor(self.tmp[:, 2, 0:nkeys], self.tmp[:, 1, 0:nkeys], st[:, c + 7:c + 8], self.tmp[:, 0, 0:nkeys], ALU.mult, ALU.add))

        def values(u, w_mark):
            (q_off, k_off, nkeys), h, i = units[u]
            nkt = nkeys // P
            pe.wait(w_mark, *wt_copied[-1:])
            for kt in range(nkt):
                p = nc.tensor.transpose(self.M[2][:, kt * P:(kt + 1) * P], self.tmp[:, 2, kt * P:(kt + 1) * P], self.ident)
            w_read[0] = pe.mark(p)
            act.wait(w_read[0], pv_done[0])
            wt_copied.append(act.mark(nc.scalar.activation(
                self.wt[:, 0:nkt, i * P:(i + 1) * P], self.M[2][:, 0:nkeys].rearrange("p (k q) -> p k q", k=nkt), ACT.Copy)))
            if i == 0:
                return
            pe.wait(wt_copied[-1], out_done[0])
            for kt in range(nkt):
                p = nc.tensor.matmul(self.M[3][:, 0:TOK], V[:, k_off // P + kt, h * P:(h + 1) * P], self.wt[:, kt, :], start=(kt == 0), stop=(kt == nkt - 1))
            pv_done[0] = pe.mark(p)
            act.wait(pv_done[0])
            out_done[0] = act.mark(nc.scalar.activation(self.y[:, h, q_off:q_off + TOK], self.M[3][:, 0:TOK], ACT.Copy))

        softmax(0, scores(0))
        for u in range(len(units)):
            w = weights(u)
            self.fill()
            if u + 1 < len(units):
                softmax(u + 1, scores(u + 1))
            values(u, w)
        self.fill(2)
        self.need(dve, f"subln{l}")
        init = 0.8 - 0.6 * math.exp(-0.3 * l)
        n = len(parts) * TOK
        scratch = [None, None]
        act.settle()
        act.wait(dve.last())
        for h in range(HEADS):
            yh, sq, r, b = self.y[:, h, 0:n], self.tmp[:, h % 2, 0:n], self.tmp[:, 2 + h % 2, 0:n], self.M[h % 2]
            act.wait(scratch[h % 2])
            a = act.mark(nc.scalar.activation(sq, yh, ACT.Square))
            pe.wait(a)
            p = pe.mark(nc.tensor.matmul(b[:, 0:n], self.mean_128, sq, start=True, stop=True))
            m = self.rsqrt(r, b[:, 0:n], p)
            dve.settle()
            dve.mark(v.scalar_tensor_tensor(yh, yh, self.loads[f"subln{l}"][0], r, ALU.mult, ALU.mult))
            dve.settle()
            scratch[h % 2] = dve.mark(v.tensor_scalar(yh, yh, 1.0 - init, None, ALU.mult))
        return dve.last()

    def hyena_filter(self, l):
        nc, v, dve, act, pe = self.nc, self.nc.vector, self.dve, self.act, self.pe
        names = [f"hy_{n}{l}" for n in ("w1", "b1", "w2", "b2", "w3", "freq")]
        w3_at = self.y[0:64, 4:6, :].rearrange("p a n -> p (a n)")
        self.load(f"hy_w3{l}", w3_at, eng=nc.gpsimd)
        self.load(f"hy_decay{l}", self.y[:, 6:8, :], self.ins["hy_decay"], eng=nc.gpsimd)
        for line in (pe, dve):
            self.need(line, *names, "hy_z", f"hy_decay{l}", "dft")
        w1, b1, w2, b2, w3, fr = (self.loads[n][0] for n in names)
        z, decay, dft = (self.loads[n][0] for n in ("hy_z", f"hy_decay{l}", "dft"))
        hid = self.tmp[0:64, 0, 0:TOK]
        arg = self.tmp[0:64, 0, TOK:ALL]
        k = self.tmp[0:64, 1, 0:TOK]
        src = z
        m = None
        for s, (w, b, kk) in enumerate(((w1, b1, 33), (w2, b2, 64))):
            pe.wait(m)
            p = pe.mark(nc.tensor.matmul(self.M[0][0:64, 0:TOK], w, src, start=True, stop=True))
            dve.wait(p)
            dve.mark(v.tensor_scalar(arg, self.M[0][0:64, 0:TOK], b, fr[:, s:s + 1], ALU.add, ALU.mult))
            m = self.sine(hid, arg, k, dve.last(), 64)
            self.fill(2)
            src = hid
        pe.wait(m)
        f, b = self.arena[:, 0:2, :], self.arena[:, 2:4, :]
        for c, dst in ((0, f), (1, b)):
            for t in range(2):
                p = pe.mark(nc.tensor.matmul(self.M[2 * c + t][:, :], hid[:, t * P:(t + 1) * P], w3[:, c * BR:(c + 1) * BR], start=True, stop=True))
                dve.wait(p)
                dve.mark(v.tensor_tensor(dst[:, t, :], self.M[2 * c + t][:, :], decay[:, t, :], ALU.mult))
        self.fill(2)
        dve.settle()
        dve.mark(v.memset(b[0:1, 0, :], 0.0))
        dve.settle()
        act.wait(dve.last())
        pe.wait(dve.last())
        sq = self.arena[:, 4:8, :]
        for n in range(4):
            a = act.mark(nc.scalar.activation(sq[:, n, :], self.arena[:, n, :], ACT.Square))
        self.fill(2)
        pe.wait(a)
        for c in range(BT):
            for n in range(4):
                p = nc.tensor.matmul(self.M[0][:, c:c + 1], sq[:, n, c * P:(c + 1) * P], self.ones, start=(n == 0), stop=(n == 3))
        p = pe.mark(p)
        m = self.rsqrt(self.hy_rs[:], self.M[0][:, 0:BT], p, self.zero)
        s, d = self.arena[:, 8:10, :], self.arena[:, 10:12, :]
        dve.mark(v.tensor_tensor(s, f, b, ALU.add))
        dve.mark(v.tensor_tensor(d, f, b, ALU.subtract))
        self.fill(2)
        pe.wait(dve.last(), m)
        for part, src, dst in ((0, s, self.kre), (1, d, self.kim)):
            for ft in range(2):
                bank = self.M[(2 * part + ft) % 4]
                for t in range(2):
                    p = nc.tensor.matmul(bank[:, :], dft[:, t, part * TOK + ft * P:part * TOK + (ft + 1) * P], src[:, t, :], start=(t == 0), stop=(t == 1))
                p = pe.mark(p)
                act.wait(p)
                act.mark(nc.scalar.activation(dst[:, ft, :], bank[:, :], ACT.Copy))
        return act.last(), dve.last()

    def hyena_conv(self, l, seqs, marks):
        nc, v, dve, act, pe = self.nc, self.nc.vector, self.dve, self.act, self.pe
        n = seqs * TOK
        hy = self.arena[:, 0:12, :]
        for line in (dve, act, pe):
            line.wait(*marks)
        self.need(dve, f"hy_bias{l}")
        self.need(pe, "idft", "ident")
        idft, dft = self.loads["idft"][0], self.loads["dft"][0]
        for c in range(BT):
            dve.mark(v.tensor_tensor(hy[:, 4 + c, 0:n], hy[:, 4 + c, 0:n], hy[:, 8 + c, 0:n], ALU.mult))
        pe.wait(dve.last())
        ut = self.arena[:, 12:16, :]
        for s in range(seqs):
            for t in range(2):
                b = self.M[(2 * s + t) % 4]
                for c in range(BT):
                    o = s * TOK + t * P
                    p = nc.tensor.transpose(b[:, c * P:(c + 1) * P], hy[:, 4 + c, o:o + P], self.ident)
                p = pe.mark(p)
                act.wait(p)
                act.mark(nc.scalar.activation(ut[:, 2 * s + t, :], b[:, :], ACT.Copy))
        uts = act.last()
        self.fill()
        pe.wait(uts)
        for s in range(seqs):
            spec = hy[:, 8:12, :]
            inv_done = None if s == 0 else pe.last()
            dve.wait(inv_done)
            for ft in range(2):
                re, im = self.M[2 * ft], self.M[2 * ft + 1]
                for part, b in ((0, re), (1, im)):
                    for t in range(2):
                        p = nc.tensor.matmul(b[:, :], dft[:, t, part * TOK + ft * P:part * TOK + (ft + 1) * P], ut[:, 2 * s + t, :], start=(t == 0), stop=(t == 1))
                    p = pe.mark(p)
                dve.wait(p)
                t0, t1 = self.tmp[:, 0, :], self.tmp[:, 1, :]
                dve.mark(v.tensor_tensor(t0, im[:, :], self.kim[:, ft, :], ALU.mult))
                dve.mark(v.tensor_tensor(spec[:, ft, :], re[:, :], self.kre[:, ft, :], ALU.mult))
                dve.mark(v.tensor_tensor(t1, im[:, :], self.kre[:, ft, :], ALU.mult))
                dve.mark(v.tensor_tensor(spec[:, 2 + ft, :], re[:, :], self.kim[:, ft, :], ALU.mult))
                dve.settle()
                dve.mark(v.tensor_tensor(spec[:, ft, :], spec[:, ft, :], t0, ALU.subtract))
                dve.mark(v.tensor_tensor(spec[:, 2 + ft, :], spec[:, 2 + ft, :], t1, ALU.add))
                dve.settle()
            specs = dve.last()
            self.fill(1 if s == 0 and seqs > 1 else 2)
            pe.wait(specs)
            o = slice(s * TOK, (s + 1) * TOK)
            for c in range(BT):
                b = self.M[c]
                for k in range(4):
                    p = nc.tensor.matmul(b[:, 0:TOK], spec[:, k, c * P:(c + 1) * P], idft[:, k, :], start=(k == 0), stop=(k == 3))
                p = pe.mark(p)
                dve.wait(p)
                yb = self.y[:, 4 + c, o]
                dve.mark(v.tensor_scalar(yb, b[:, 0:TOK], self.hy_rs[:, c:c + 1], None, ALU.mult))
                dve.settle()
                dve.mark(v.scalar_tensor_tensor(yb, hy[:, 4 + c, o], self.loads[f"hy_bias{l}"][0][:, c:c + 1], yb, ALU.mult, ALU.add))
                dve.settle()
                dve.mark(v.tensor_tensor(yb, yb, hy[:, c, o], ALU.mult))
            ybs = dve.last()
            self.fill()
            pe.wait(ybs)
        return dve.last()

    def gmlp(self, l, ntt, marks):
        nc, v, dve, act, pe = self.nc, self.nc.vector, self.dve, self.act, self.pe
        self.need(dve, f"ln_g{l}", f"ln_b{l}", f"gm_bs{l}")
        self.need(pe, f"gm_ws{l}")
        g, b_, ws, bs = (self.loads[f"{n}{l}"][0] for n in ("ln_g", "ln_b", "gm_ws", "gm_bs"))
        dve.wait(*marks)
        u, vt = self.arena[:, 16:20, :], self.arena[:, 20:24, :]
        for t in range(ntt):
            x = vt[:, t, :]
            st = self.stat
            dve.mark(v.bn_stats(st[:, 8:14], x))
            dve.settle()
            dve.mark(v.bn_aggr(st[:, 14:16], st[:, 8:14]))
            m = self.rsqrt(st[:, 16:17], st[:, 15:16], dve.last())
            dve.wait(m)
            dve.mark(v.tensor_scalar(x, x, st[:, 14:15], st[:, 16:17], ALU.subtract, ALU.mult))
            dve.settle()
            dve.mark(v.tensor_tensor(x, x, g, ALU.mult))
            dve.settle()
            dve.mark(v.tensor_tensor(x, x, b_, ALU.add))
            dve.settle()
            self.fill(2)
        pe.wait(dve.last())
        freed = [None] * 4
        tm_read = [None] * 4
        for t in range(ntt):
            for j in range(BT):
                b = self.M[j]
                pe.wait(freed[j])
                p = pe.mark(nc.tensor.matmul(b[:, 0:2 * P], vt[:, t, j * P:(j + 1) * P], ws[:, 2 * j:2 * j + 2, :], start=True, stop=True))
                dve.wait(p)
                tm = self.tmp[:, 0, j * P:(j + 1) * P]
                dve.wait(tm_read[j])
                dve.mark(v.tensor_tensor(tm[0:64, :], b[0:64, 0:P], bs[0:64, j, :], ALU.add))
                freed[j] = dve.mark(v.tensor_tensor(tm[64:P, :], b[64:P, P:2 * P], bs[64:P, j, :], ALU.add))
                dve.settle()
                if j == 3:
                    self.fill(2)
                tm_read[j] = dve.mark(v.tensor_tensor(self.y[:, 8 + j, t * P:(t + 1) * P], tm, u[:, j, t * P:(t + 1) * P], ALU.mult))
        return dve.last()

    def merge(self, branches, n, gated):
        nc, v, dve, act = self.nc, self.nc.vector, self.dve, self.act
        dve.mark(v.memset(self.y[:, 0:KT, 0:n], 0.0))
        dve.settle()
        with self.roll(branches, tile=12, bank=8, act=8, dve=8) as i:
            rhs = gated(i)
            for pair in range(4):
                def terms(hi, lo):
                    for o in range(2):
                        nc.tensor.wait_ge(self.free.sem, self.free.value(o - 3))
                        b = self.G[(self.free.off + o) % 4]
                        for k in range(BT):
                            c = slice((o * BT + k) * P, (o * BT + k + 1) * P)
                            m = self.three(b[:, 0:n], hi[:, c], lo[:, c], rhs[0](k), rhs[1](k), k == 0, k == BT - 1)
                    return m
                self.tile(terms)
                for o in range(2):
                    e = self.free.off % 4
                    sel = self.M[e]
                    u = self.tile(self.feature_tile(n, bank=sel))
                    act.wait(u)
                    th = self.tmp[:, e % 2, 0:n]
                    act.eng.wait_ge(self.free.sem, self.free.value(-1))
                    a = act.mark(nc.scalar.activation(th, sel[:, 0:n], ACT.Tanh, scale=0.5))
                    dve.wait(a)
                    dve.mark(v.scalar_tensor_tensor(th, th, 1.0, self.G[e][:, 0:n], ALU.add, ALU.mult))
                    dve.settle()
                    acc = self.y[:, 2 * pair + o, 0:n]
                    self.release(v.tensor_tensor(acc, acc, th, ALU.add))
        return (self.free, self.free.value())


def short_conv(p, l, n):
    nc, v, dve, act = p.nc, p.nc.vector, p.dve, p.act
    sw, seqs = p.loads[f"hy_sw{l}"][0], n // TOK

    def evacuate(m, b, u):
        act.wait(u)
        o = p.arena[:, m, 0:n]
        a = act.mark(nc.scalar.activation(o, b[:, 0:n], ACT.Identity, bias=sw[:, m, 3:4], scale=sw[:, m, 1:2]))
        dve.wait(a)
        o3 = o.rearrange("p (s t) -> p s t", s=seqs)
        b3 = b[:, 0:n].rearrange("p (s t) -> p s t", s=seqs)
        dve.mark(v.scalar_tensor_tensor(o3[:, :, 1:TOK], b3[:, :, 0:TOK - 1], sw[:, m, 0:1], o3[:, :, 1:TOK], ALU.mult, ALU.add))
        dve.settle()
        return v.scalar_tensor_tensor(o3[:, :, 0:TOK - 1], b3[:, :, 1:TOK], sw[:, m, 2:3], o3[:, :, 0:TOK - 1], ALU.mult, ALU.add)
    return evacuate


def gate_tile(p, n, slot, yt, j):
    nc, v, dve, act = p.nc, p.nc.vector, p.dve, p.act
    b = p.bank()
    u = p.tile(p.feature_tile(n, bank=b))
    act.wait(u)
    th = p.tmp[:, 3 + j % 2, 0:n]
    act.eng.wait_ge(p.free.sem, p.free.value(-1))
    a = act.mark(nc.scalar.activation(th, b[:, 0:n], ACT.Tanh, scale=0.5))
    dve.wait(a)
    dve.mark(v.scalar_tensor_tensor(th, th, 1.0, b[:, 0:n], ALU.add, ALU.mult))
    dve.settle()
    d = dve.mark(v.tensor_tensor(th, th, yt, ALU.mult))
    act.wait(d)
    hi, lo = p.arena_r[:, slot, 0:n], p.arena_r[:, slot + 4, 0:n]
    a = act.mark(nc.scalar.activation(hi, th, ACT.Copy, scale=0.5))
    dve.wait(a)
    p.release(v.scalar_tensor_tensor(lo, th, 0.5, hi.bitcast(F32), ALU.mult, ALU.subtract))


def block1_layer(p, l, x_mark):
    nc, v, dve, act, pe = p.nc, p.nc.vector, p.dve, p.act, p.pe
    last = l == DEPTH - 1
    n = TOK if last else ALL
    mod_mark = p.modulation(l)
    neg_lam = p.lam(l)
    h_mark = p.pre_norm(mod_mark, x_mark)
    pe.wait(h_mark)

    K, Q, V = p.arena[:, 12:16, :], p.arena[:, 16:20, :], p.arena[:, 20:24, :]

    def copy_to(dst, width):
        def evacuate(j, b, u):
            act.wait(u)
            return nc.scalar.activation(dst[:, j, 0:width], b[:, 0:width], ACT.Copy)
        return evacuate
    p.fillers += p.feature_gemm(4, ALL, copy_to(K, ALL)) + p.feature_gemm(4, n, copy_to(Q, n))
    p.fillers += p.token_gemm(4, lambda j, b: nc.scalar.activation(V[:, j, :], b[:, :], ACT.Copy))
    nc.gpsimd.wait_ge(x_mark[0].sem, x_mark[1])
    p.fill()
    filter_marks = p.hyena_filter(l)
    p.fill(12)
    kqv = (p.free, p.free.value())
    p.need(dve, "rope")
    p.need(pe, "rope", "perm1", "ident")
    dve.wait(kqv)
    pe.wait(kqv, *filter_marks)
    act.wait(*filter_marks)

    p.need(act, f"hy_sw{l}")
    p.need(dve, f"hy_sw{l}")
    p.fillers += p.feature_gemm(12, n, short_conv(p, l, n))
    rope = p.loads["rope"][0]
    bank_read = [None] * 4
    for j in range(8):
        T = (K, Q)[j // 4]
        pe.wait(bank_read[j % 4])
        m = bank_read[j % 4] = p.rope(T[:, j % 4, 0:TOK], TOK, rope[:, 0, :], rope[:, 1, :], p.loads["perm1"][0], kqv, p.M[j % 4], p.tmp[:, j % 2, :])
    parts = [(0, 0, ALL)] if last else [(0, 0, ALL), (TOK, TOK, TOK)]
    a = p.diff_attention(l, parts, K, Q, V, neg_lam, (m,))
    p.fill(12)
    hy_mark = (p.free, p.free.value())

    gu, vt = p.arena[:, 16:20, :], p.arena[:, 20:24, :]
    ntt = n // P

    def gelu_to(j, b, u):
        act.wait(u)
        return nc.scalar.activation(gu[:, j, 0:n], b[:, 0:n], ACT.Gelu)
    p.fillers += p.feature_gemm(4, n, gelu_to)
    p.fillers += p.token_gemm(ntt, lambda j, b: nc.scalar.activation(vt[:, j, :], b[:, :], ACT.Gelu))
    b_mark = p.hyena_conv(l, seqs=n // TOK, marks=(a, hy_mark) + filter_marks)
    nc.gpsimd.wait_ge(b_mark[0].sem, b_mark[1])
    p.load(f"ln_g{l}", p.arena[:, 8, :], eng=nc.gpsimd)
    p.load(f"ln_b{l}", p.arena[:, 9, :], eng=nc.gpsimd)
    p.load(f"gm_ws{l}", p.arena[:, 10:12, :].rearrange("p a (g q) -> p (a g) q", q=P), eng=nc.gpsimd)
    p.load(f"gm_bs{l}", p.arena[:, 12, :].rearrange("p (j q) -> p j q", q=P), eng=nc.gpsimd)
    p.fill(8)
    gm = (p.free, p.free.value())
    act.wait(b_mark)
    dve.wait(b_mark)

    p.fillers += [(lambda j=j: gate_tile(p, n, j, p.y[:, j, 0:n], j)) for j in range(4)]
    if not last:
        p.fillers += p.modulation_gemm(l + 1, p.arena[0:2, 13:15, :])
    c_mark = p.gmlp(l, ntt, (gm, b_mark))
    p.fill(4 + 24)
    for line in (pe, act, dve):
        line.wait(c_mark)

    arenaR = p.arena_r
    with p.roll(2, tile=4, bank=4, act=8, dve=8) as i:
        for j in range(4):
            gate_tile(p, n, i * 8 + (8 + j), p.y[:, i * 4 + (4 + j), 0:n], j)
    pe.wait((p.free, p.free.value()))

    def gated(i):
        return (lambda k: arenaR[:, i * 8 + k, 0:n]), (lambda k: arenaR[:, i * 8 + (4 + k), 0:n])
    return gated, n


def block1_out(p, n, m_mark, x_mark):
    nc, v, dve, act, pe = p.nc, p.nc.vector, p.dve, p.act, p.pe
    act.wait(m_mark)
    dve.wait(m_mark)
    pe.wait(m_mark)
    for k in range(KT):
        m = p.halves(p.hhi[:, k, 0:n], p.hlo[:, k, 0:n], p.y[:, k, 0:n], 0.5)
    pe.wait(m)
    for o in range(KT):
        b = p.bank()
        u = p.tile(p.feature_tile(n, bank=b))
        act.wait(u)
        p.release(nc.scalar.activation(p.arena[:, o, 0:n], b[:, 0:n], ACT.Copy))
    m = p.rms(p.arena[:], n, KT, p.tmp[:, 2, :], ((p.free, p.free.value()),))
    dve.wait(m, (p.free, p.free.value()))
    dve.settle()
    for k in range(KT):
        o = p.arena[:, k, 0:n]
        dve.mark(v.tensor_tensor(o, o, p.tmp[:, 2, 0:n], ALU.mult))
        dve.settle()
        for s in range(n // TOK):
            c = slice(s * TOK, (s + 1) * TOK)
            dve.mark(v.scalar_tensor_tensor(p.x[:, k, c], p.arena[:, k, c], p.mod[:, 16 + k, s:s + 1], p.x[:, k, c], ALU.mult, ALU.add))
    return dve.last()


def second_norm(p, gain, x_mark):
    nc, v, dve = p.nc, p.nc.vector, p.dve
    m = p.rms(p.x, TOK, KT, p.tmp[:, 2, :], (x_mark,))
    p.need(dve, gain)
    g = p.loads[gain][0]
    dve.wait(m)
    dve.settle()
    done = [None, None]
    for k in range(KT):
        t = p.tmp[:, 3 + k % 2, 0:TOK]
        dve.wait(done[k % 2])
        d = dve.mark(v.scalar_tensor_tensor(t, p.x[:, k, 0:TOK], g[:, k:k + 1], p.tmp[:, 2, 0:TOK], ALU.mult, ALU.mult))
        done[k % 2] = p.halves(p.hhi[:, k, 0:TOK], p.hlo[:, k, 0:TOK], t, 1.0, (d,))
    return dve.last()


def compress(p, z, which, X, xh, xl, hid):
    nc, v, dve, act, pe = p.nc, p.nc.vector, p.dve, p.act, p.pe
    pe_t = p.loads[f"pe_{which}"][0]
    p.need(dve, f"pe_{which}")
    pair = p.tmp[:, 0, :].rearrange("p (g t) -> p g t", g=2)[:, :, 0:P]
    for g in range(2):
        for par in range(2):
            a = act.mark(nc.scalar.activation(pair[par * 64:par * 64 + 64, g, :], z[g * 64:g * 64 + 64, par::2], ACT.Copy))
    dve.wait(a)
    for g in range(2):
        for jj in range(16):
            dve.mark(v.tensor_scalar(X[:, jj, g * NCMP:(g + 1) * NCMP], pair[:, g, jj:jj + 8 * (NCMP - 1) + 1:8], pe_t[:, jj:jj + 1], None, ALU.add))
    dve.settle()
    m = p.halves(xh[:], xl[:], X, 1.0, (dve.last(),))
    pe.wait(m)
    banks = [p.M[1], p.M[2]]
    for g in range(4):
        def products(hi, lo):
            for q in range(4):
                jj = 4 * g + q
                for o in range(2):
                    c = slice(q * 256 + o * P, q * 256 + (o + 1) * P)
                    r = p.three(banks[o][:, 0:2 * NCMP], hi[:, c], lo[:, c], xh[:, jj, :], xl[:, jj, :], jj == 0, jj == 15)
            return r
        u = p.tile(products)
    act.wait(u)
    dve.wait(u)
    th = p.tmp[:, 1, 0:4 * NCMP].rearrange("p (o n) -> p o n", o=2)
    for o in range(2):
        a = act.mark(nc.scalar.activation(th[:, o, :], banks[o][:, 0:2 * NCMP], ACT.Tanh, scale=0.5))
        dve.wait(a)
        dve.mark(v.scalar_tensor_tensor(th[:, o, :], th[:, o, :], 1.0, banks[o][:, 0:2 * NCMP], ALU.add, ALU.mult))
    dve.settle()
    return dve.mark(v.tensor_scalar(hid, th, 0.5, None, ALU.mult))


def block2(p, x_mark):
    nc, v, dve, act, pe = p.nc, p.nc.vector, p.dve, p.act, p.pe
    pool = nc.gpsimd
    pool.wait_ge(x_mark[0].sem, x_mark[1])
    p.load("head_spread", p.shared[0:32, 0:1792].rearrange("p (a n) -> p a n", a=14), eng=pool)
    p.load("ck_w2", p.shared[:, 1792:1920].rearrange("p (a n) -> p a n", a=2), eng=pool)
    p.load("cv_w2", p.shared[:, 1920:2048].rearrange("p (a n) -> p a n", a=2), eng=pool)
    p.load("ple", p.y[:, 8, :], eng=pool)
    L = {k: m[0] for k, m in p.loads.items()}

    p.need(dve, "pos", "inv_freq", "head_gain", "causal", "cmp_add", "cmp_keep")
    p.need(pe, "perm2", "head_sum", "head_spread", "block_mean", "ck_w2", "cv_w2")
    dve.wait(x_mark)
    act.wait(x_mark)
    pe.wait(x_mark)
    trig = p.y[:, 9, :].rearrange("p (s t) -> p s t", s=2)
    posf = p.tmp[:, 0, 0:TOK]
    for s, shift in ((0, math.pi / 2), (1, 0.0)):
        act.wait(dve.last())
        dve.mark(v.tensor_copy(posf, L["pos"]))
        dve.settle()
        dve.mark(v.tensor_scalar(p.tmp[:, 1, 0:TOK], posf, L["inv_freq"], None, ALU.mult))
        dve.settle()
        m = p.sine(trig[:, s, :], p.tmp[:, 1, 0:TOK], p.tmp[:, 0, 0:TOK], dve.last(), P, big=True, shift=shift)
        dve.wait(m)
    cos, sin = trig[:, 0, :], trig[:, 1, :]

    h = second_norm(p, "g_mix", dve.last())
    pe.wait(h)
    Z = p.arena[:, 0:8, :].rearrange("p a (b t) -> p (a b) t", t=TOK)
    with p.roll(4, tile=4, bank=4) as i:
        for j in range(4):
            b = p.bank()
            u = p.tile(p.feature_tile(TOK, bank=b))
            act.wait(u)
            p.release(nc.scalar.activation(Z[:, i * 4 + j, :], b[:, 0:TOK], ACT.Copy))
    z_mark = (p.free, p.free.value())
    VM, VS = p.arena[:, 8:10, :], p.arena[:, 10:12, :]
    gate = p.sb("gate2", [P, 2, 24])[:]

    def values_gates(j, b):
        act.mark(nc.scalar.activation(VS[:, j, 0:256], b[:, 0:256], ACT.Copy))
        return nc.scalar.activation(gate[:, j, :], b[:, 256:280], ACT.Tanh, scale=0.5)
    p.fillers += p.token_gemm(2, lambda j, b: nc.scalar.activation(VM[:, j, :], b[:, :], ACT.Copy))
    p.fillers += p.token_gemm(2, values_gates, 280)
    p.fill(8)
    a = (p.free, p.free.value())
    dve.wait(a)
    dve.mark(v.tensor_scalar(gate, gate, 1.0, 0.5, ALU.add, ALU.mult))

    X = p.y[:, 10, 0:32 * NCMP].rearrange("p (a n) -> p a n", a=16)
    xh, xl = p.sb("cmp_xh", [P, 16, 2 * NCMP], F32R), p.sb("cmp_xl", [P, 16, 2 * NCMP], F32R)
    hid = p.sb("cmp_hid", [P, 2, 2 * NCMP])[:]
    act.wait(z_mark)
    act.settle()
    pe.wait(a)
    m = compress(p, Z[:, 4, :], "k", X, xh, xl, hid)
    pe.wait(m)
    kcT = p.sb("kc_t", [P, 2, 16])[:]
    b = p.M[0]
    for g in range(2):
        for o in range(2):
            q = nc.tensor.matmul(b[g * 64:g * 64 + 64, 0:NCMP], L["ck_w2"][:, o, :], hid[:, o, g * NCMP:(g + 1) * NCMP], start=(o == 0), stop=(o == 1))
        q = pe.mark(q)
    act.wait(q)
    a = act.mark(nc.scalar.activation(kcT[:, 0, 0:NCMP], b[:, 0:NCMP], ACT.Copy))
    a = act.mark(nc.scalar.activation(kcT[:, 1, 0:NCMP], b[:, 0:NCMP], ACT.Square))
    pe.wait(a)
    q = pe.mark(nc.tensor.matmul(b[:, 0:NCMP], L["block_mean"], kcT[:, 1, 0:NCMP], start=True, stop=True))
    m = p.rsqrt(kcT[:, 1, 0:NCMP], b[:, 0:NCMP], q)
    dve.settle()
    dve.mark(v.scalar_tensor_tensor(kcT[:, 0, 0:NCMP], kcT[:, 0, 0:NCMP], L["head_gain"][:, 14:15], kcT[:, 1, 0:NCMP], ALU.mult, ALU.mult))
    p.rope(kcT[:, 0, 0:NCMP], NCMP, cos[:, 31::16], sin[:, 31::16], L["perm2"], dve.last(), b, p.tmp[:, 3, :])
    act.wait(dve.last())
    m = compress(p, Z[:, 5, :], "v", X, xh, xl, hid)
    pe.wait(m)
    vc = p.sb("vc", [16, P])[:]
    for g in range(2):
        for o in range(2):
            q = nc.tensor.matmul(b[0:NCMP, g * 64:g * 64 + 64], hid[:, o, g * NCMP:(g + 1) * NCMP], L["cv_w2"][:, o, :], start=(o == 0), stop=(o == 1))
    q = pe.mark(q)
    act.wait(q)
    act.mark(nc.scalar.activation(vc[0:NCMP, :], b[0:NCMP, 0:P], ACT.Copy))

    tiles = [0, 1, 2, 3, 6, 7] + list(range(8, 16))
    pe.wait(act.last())
    done = [None, None]
    for n, zt in enumerate(tiles):
        act.wait(done[n % 2])
        a = act.mark(nc.scalar.activation(p.tmp[:, n % 2, 0:TOK], Z[:, zt, :], ACT.Square))
        pe.wait(a)
        done[n % 2] = pe.mark(nc.tensor.matmul(b[0:32, 0:TOK], L["head_sum"][:, n, :], p.tmp[:, n % 2, 0:TOK], start=(n == 0), stop=(n == 13)))
    hr = p.tmp[0:32, 2, 0:TOK]
    m = p.rsqrt(hr, b[0:32, 0:TOK], done[1])
    pe.wait(m)
    dve.settle()
    last_use = [None] * 4
    for n, zt in enumerate(tiles):
        s, r = p.M[1 + n % 2], p.M[0 if n % 2 else 3]
        pe.wait(last_use[n % 2])
        q = pe.mark(nc.tensor.matmul(s[:, 0:TOK], L["head_spread"][:, n, :], hr, start=True, stop=True))
        dve.wait(q)
        d = dve.mark(v.scalar_tensor_tensor(Z[:, zt, :], Z[:, zt, :], L["head_gain"][:, n:n + 1], s[:, 0:TOK], ALU.mult, ALU.mult))
        dve.settle()
        last_use[n % 2] = p.rope(Z[:, zt, :], TOK, cos, sin, L["perm2"], d, r, p.tmp[:, 3 + n % 2, :])
    qk = dve.last()

    Sm = p.arena[:, 12:15, :].rearrange("p a (b t) -> p (a b) t", t=TOK)
    PT = p.arena[:, 15:18, :].rearrange("p a (b k q) -> p a b k q", b=2, k=2)
    Sc = p.sb("s_cmp", [P, 2, 16])[:]
    PTc = p.y[0:16, 11, 0:2 * P].rearrange("p (b q) -> p b q", b=2)
    YN = p.y[:, 0:2, :].rearrange("p a (b t) -> p (a b) t", t=TOK)
    YM = p.y[:, 2:4, :].rearrange("p a (b t) -> p (a b) t", t=TOK)
    st = p.stat
    banks_read = None
    for i in range(2):
        nk = P * (i + 1)
        q_ = slice(i * P, (i + 1) * P)
        for j in range(4):
            pe.wait(qk, banks_read)
            for ab in range(2):
                r = slice(ab * 64, ab * 64 + 64)
                for kind, (qt, kt) in enumerate(((j, 6), (j, 7), (8 + j, 12 + j))):
                    c = (kind % 2) * nk
                    nc.tensor.matmul(p.M[2 * ab + kind // 2][:, c:c + nk], Z[r, qt, q_], Z[r, kt, 0:nk], start=True, stop=True)
                q = nc.tensor.matmul(p.M[2 * ab + 1][:, TOK:TOK + NCMP], Z[r, j, q_], kcT[r, 0, 0:NCMP], start=True, stop=True)
                q = pe.mark(q)
            dve.wait(q)
            mask = L["causal"][:, TOK - nk:TOK].unsqueeze(1).broadcast_to([P, 2, nk])
            for ab in range(2):
                two, one = p.M[2 * ab], p.M[2 * ab + 1]
                dve.mark(v.scalar_tensor_tensor(Sm[:, 3 * ab:3 * ab + 2, 0:nk], two[:, 0:2 * nk].rearrange("p (b n) -> p b n", b=2), 0.125, mask, ALU.mult, ALU.add))
                dve.mark(v.scalar_tensor_tensor(Sm[:, 3 * ab + 2, 0:nk], one[:, 0:nk], 0.125, L["causal"][:, TOK - nk:TOK], ALU.mult, ALU.add))
                dve.mark(v.scalar_tensor_tensor(Sc[:, ab, 0:NCMP], one[:, TOK:TOK + NCMP], 0.125, L["cmp_add"][:, i, :], ALU.mult, ALU.add))
            ckeep = L["cmp_keep"][:, i:i + 1, :].broadcast_to([P, 2, NCMP])
            dve.settle()
            dve.mark(v.tensor_reduce(st[:, 0:6], Sm[:, :, 0:nk], AXX, ALU.max, negate=True))
            d = dve.mark(v.tensor_reduce(st[:, 6:8], Sc[:, :, 0:NCMP], AXX, ALU.max, negate=True))
            act.wait(d)
            for r in range(6):
                act.mark(nc.scalar.activation(Sm[:, r, 0:nk], Sm[:, r, 0:nk], ACT.Exp, bias=st[:, r:r + 1], accum_out=st[:, 8 + r:9 + r]))
            for ab in range(2):
                a = act.mark(nc.scalar.activation(Sc[:, ab, 0:NCMP], Sc[:, ab, 0:NCMP], ACT.Exp, bias=st[:, 6 + ab:7 + ab]))
            dve.wait(a)
            dve.mark(v.tensor_tensor(Sc[:, :, 0:NCMP], Sc[:, :, 0:NCMP], ckeep, ALU.mult))
            dve.settle()
            dve.mark(v.tensor_reduce(st[:, 14:16], Sc[:, :, 0:NCMP], AXX, ALU.add))
            dve.settle()
            dve.mark(v.tensor_scalar(st[:, 8:16], st[:, 8:16], 1e-30, None, ALU.max))
            dve.settle()
            dve.mark(v.reciprocal(st[:, 16:24], st[:, 8:16]))
            dve.settle()
            for kind, cols in ((1, slice(16, 20, 3)), (2, slice(17, 21, 3)), (0, slice(22, 24))):
                c0 = j * 3 + kind
                dve.mark(v.tensor_tensor(st[:, cols], st[:, cols], gate[:, i, c0:c0 + 13:12], ALU.mult))
            dve.settle()
            dve.mark(v.tensor_tensor(Sm[:, :, 0:nk], Sm[:, :, 0:nk], st[:, 16:22].unsqueeze(2).broadcast_to([P, 6, nk]), ALU.mult))
            d = dve.mark(v.tensor_tensor(Sc[:, :, 0:NCMP], Sc[:, :, 0:NCMP], st[:, 22:24].unsqueeze(2).broadcast_to([P, 2, NCMP]), ALU.mult))
            pe.wait(d)
            for kind in range(3):
                for ab in range(2):
                    for kt in range(i + 1):
                        c = (ab * 2 + kt) * P
                        nc.tensor.transpose(p.M[kind][:, c:c + P], Sm[:, 3 * ab + kind, kt * P:(kt + 1) * P], p.ident)
            for ab in range(2):
                q = nc.tensor.transpose(p.M[3][0:NCMP, ab * P:(ab + 1) * P], Sc[:, ab, 0:NCMP], p.ident)
            q = pe.mark(q)
            act.wait(q)
            dve.wait(q)
            for kind in range(3):
                a = act.mark(nc.scalar.activation(PT[:, kind, :, 0:i + 1, :], p.M[kind][:, :].rearrange("p (b k q) -> p b k q", b=2, k=2)[:, :, 0:i + 1, :], ACT.Copy))
            d = dve.mark(v.tensor_copy(PTc[0:NCMP, :, :], p.M[3][0:NCMP, 0:2 * P].rearrange("p (b q) -> p b q", b=2)))
            pe.wait(a, d)
            for ab in range(2):
                o = slice(ab * 64, ab * 64 + 64)
                for kind in range(2):
                    for kt in range(i + 1):
                        nc.tensor.matmul(p.M[0][o, 0:P], VS[:, kt, kind * P + ab * 64:kind * P + ab * 64 + 64], PT[:, kind, ab, kt, :], start=(kind == 0 and kt == 0), stop=False)
                nc.tensor.matmul(p.M[0][o, 0:P], vc[0:NCMP, o], PTc[0:NCMP, ab, :], start=False, stop=True)
                for kt in range(i + 1):
                    hd = 2 * j + ab
                    q = nc.tensor.matmul(p.M[1][o, 0:P], VM[:, kt, hd * 64:hd * 64 + 64], PT[:, 2, ab, kt, :], start=(kt == 0), stop=(kt == i))
            q = pe.mark(q)
            dve.wait(q)
            dve.mark(v.tensor_copy(YN[:, j, q_], p.M[0][:, 0:P]))
            banks_read = dve.mark(v.tensor_copy(YM[:, j, q_], p.M[1][:, 0:P]))
    act.wait(banks_read)
    dve.settle()

    R = p.arena_r
    for br, Y in enumerate((YN, YM)):
        for k in range(BT):
            m = p.halves(R[:, br * 8 + k, 0:TOK], R[:, br * 8 + 4 + k, 0:TOK], Y[:, k, :])
    pe.wait(m)
    dve.wait(m)

    def gated(i):
        return (lambda k: R[:, i * 8 + k, 0:TOK]), (lambda k: R[:, i * 8 + (4 + k), 0:TOK])
    m = p.merge(2, TOK, gated)
    act.wait(m)
    dve.wait(m)
    for k in range(KT):
        m = p.halves(p.hhi[:, k, 0:TOK], p.hlo[:, k, 0:TOK], p.y[:, k, 0:TOK], 0.5)
    pe.wait(m)
    for o in range(KT):
        b = p.bank()
        u = p.tile(p.feature_tile(TOK, bank=b))
        dve.wait(u)
        p.release(v.tensor_tensor(p.x[:, o, 0:TOK], p.x[:, o, 0:TOK], b[:, 0:TOK], ALU.add))

    h = second_norm(p, "g_ffn", (p.free, p.free.value()))
    pe.wait(h)
    ah = R[:, 0:11, :].rearrange("p a (b t) -> p (a b) t", t=TOK)
    al = R[:, 11:22, :].rearrange("p a (b t) -> p (a b) t", t=TOK)

    def ffn_pair(f):
        e = p.free.off % 4
        up, gt = p.bank(), p.M[e]
        ug = p.tile(p.feature_tile(TOK, bank=gt))
        uu = p.tile(p.feature_tile(TOK, bank=up))
        act.wait(ug)
        act.eng.wait_ge(p.free.sem, p.free.value(-1))
        th = p.tmp[:, e % 2, 0:TOK]
        a = act.mark(nc.scalar.activation(th, gt[:, 0:TOK], ACT.Tanh, scale=0.5))
        dve.wait(a)
        dve.mark(v.scalar_tensor_tensor(th, th, 1.0, gt[:, 0:TOK], ALU.add, ALU.mult))
        dve.wait(uu)
        dve.settle()
        d = dve.mark(v.tensor_tensor(th, th, up[:, 0:TOK], ALU.mult))
        act.wait(d)
        a = act.mark(nc.scalar.activation(ah[:, f, :], th, ACT.Copy, scale=0.5))
        dve.wait(a)
        p.release(v.scalar_tensor_tensor(al[:, f, :], th, 0.5, ah[:, f, :].bitcast(F32), ALU.mult, ALU.subtract))
    with p.roll(5, tile=8, bank=4, act=8, dve=8) as i:
        for j in range(4):
            ffn_pair(i * 4 + j)
    for f in range(20, FT):
        ffn_pair(f)
    last = (p.free, p.free.value())
    pe.wait(last)
    out_banks = p.G + p.M

    def down(k, first, final):
        def products(hi, lo):
            for o in range(KT):
                c = slice(o * P, (o + 1) * P)
                m = p.three(out_banks[o][:, 0:TOK], hi[:, c], lo[:, c], ah[:, k, :], al[:, k, :], first, final)
            return m
        return p.tile(products)
    for k in range(2):
        down(k, k == 0, False)
    with p.roll(4, tile=4) as i:
        for j in range(4):
            down(i * 4 + (2 + j), False, False)
    for k in range(18, FT):
        u = down(k, False, k == FT - 1)
    dve.wait(u)
    for o in range(KT):
        d = dve.mark(v.tensor_tensor(p.x[:, o, 0:TOK], p.x[:, o, 0:TOK], out_banks[o][:, 0:TOK], ALU.add))
    pe.wait(d)
    dve.settle()

    h = second_norm(p, "g_ple", d)
    p.need(act, "ple")
    p.need(dve, "ple")
    ph, pl = R[:, 22, :], R[:, 23, :]
    m = p.halves(ph, pl, L["ple"])
    pe.wait(h, m)
    for o in range(KT):
        b = p.bank()
        u = p.tile(p.feature_tile(TOK, bank=b))
        act.wait(u)
        p.release(nc.scalar.activation(p.y[:, o, 0:TOK], b[:, 0:TOK], ACT.Tanh, scale=0.5))
    dve.wait((p.free, p.free.value()))
    outs = []
    for g in range(2):
        def products(hi, lo):
            for o in range(4):
                for k in range(2):
                    c = slice((o * 2 + k) * P, (o * 2 + k + 1) * P)
                    t = slice(k * TOK, (k + 1) * TOK)
                    m = p.three(p.M[o][:, 0:TOK], hi[:, c], lo[:, c], ph[:, t], pl[:, t], k == 0, k == 1)
            return m
        u = p.tile(products)
        dve.wait(u)
        for o in range(4):
            k = 4 * g + o
            yk, xk = p.y[:, k, 0:TOK], p.x[:, k, 0:TOK]
            d = dve.mark(v.scalar_tensor_tensor(yk, yk, 1.0, p.M[o][:, 0:TOK], ALU.add, ALU.mult))
            dve.settle()
            outs.append(dve.mark(v.scalar_tensor_tensor(xk, yk, 0.5, xk, ALU.mult, ALU.add)))
        pe.wait(d)
        nc.sync.wait_ge(outs[-1][0].sem, outs[-1][1])
        nc.sync.dma_start(p.out[:, 4 * g:4 * g + 4, :], p.x[:, 4 * g:4 * g + 4, 0:TOK]).then_inc(p.stored, 16)
    nc.sync.wait_ge(p.stored, 32)


SMALL = ["cond", "ident", "norm_pre0", "norm_post0", "ada_b0", "norm_pre1", "norm_post1", "ada_b1", "lambda",
         "rope", "perm1", "subln0", "subln1", "hy_z"] + \
    [f"hy_{n}{l}" for l in range(2) for n in ("w1", "b1", "w2", "b2", "freq", "sw", "bias")] + \
    ["inv_freq", "head_gain", "causal", "cmp_add", "cmp_keep", "perm2", "head_sum",
     "block_mean", "pe_k", "pe_v", "g_mix", "g_ffn", "g_ple"]


def program(nc, ins, out):
    with ExitStack() as ctx:
        p = Program(nc, ctx, ins, out)
        p.stored = p.sem("stored")
        for s in range(2):
            n = ("x", "ctx")[s]
            p.load(n, p.x[:, :, s * TOK:(s + 1) * TOK])
        for n in SMALL:
            p.load(n)
        p.load("pos", dt=I32)
        p.shared = p.sb("shared", [P, 2048])
        p.load("dft", p.shared[:, 0:1024].rearrange("p (a n) -> p a n", a=2))
        p.load("idft", p.shared[:, 1024:2048].rearrange("p (a n) -> p a n", a=4))
        p.stream()
        p.constants()
        for line in (p.act, p.dve, p.pe):
            p.need(line, "x", "ctx")
        p.condition()
        for _ in range(AHEAD):
            p.split()
        p.fillers += p.modulation_gemm(0, p.arena[0:2, 13:15, :])
        p.fill(24)
        x_mark = p.const
        for l in range(DEPTH):
            gated, n = block1_layer(p, l, x_mark)
            m = p.merge(3, n, gated)
            x_mark = block1_out(p, n, m, x_mark)
            for line in (p.act, p.dve, p.pe):
                line.wait(x_mark)
        block2(p, x_mark)
        assert p.used.off == TILES, (p.used.off, TILES)


def _columns(w):
    k, n = w.shape
    return w.reshape(k // P, P, n // P, P).transpose(2, 1, 0, 3).reshape(n // P, P, k)


def _rows(w):
    return w.reshape(4, 2, P, 512).transpose(0, 2, 1, 3).reshape(4, P, 1024)


def _feat(a):
    t, f = a.shape
    return a.T.reshape(f // P, P, t).transpose(1, 0, 2)


def _vec(a):
    return a.reshape(-1, P).T


def _layout(i):
    tiles = []

    def merged(ws, gates):
        for w, g in zip(ws, gates):
            b, s = _columns(w), _columns(g)
            for pair in range(4):
                tiles.append(np.concatenate([b[2 * pair], b[2 * pair + 1]], axis=1)[None])
                tiles.append(s[2 * pair:2 * pair + 2])

    def ada(l):
        tiles.append(i["ada_w"][l].reshape(KT, P, 3, 1024).transpose(2, 0, 1, 3).reshape(24, P, 1024))
    for l in range(DEPTH):
        w = i["w_in"][l]
        if l == 0:
            ada(0)
        tiles.append(_columns(w[:, 0:512]))
        tiles.append(_columns(w[:, 1024:1536]))
        tiles.append(_rows(w[:, 512:1024]))
        tiles.append(_columns(w[:, 2048:3584]))
        tiles.append(_columns(w[:, 4096:4608]))
        tiles.append(_rows(w[:, 4608:5120]))
        tiles.append(_columns(w[:, 1536:2048]))
        if l == 0:
            ada(1)
        for g in (3584, 5120):
            tiles.append(_columns(w[:, g:g + 512]))
        merged(list(i["w_branch"][l]), [w[:, 5632 + b * D:5632 + (b + 1) * D] for b in range(3)])
        tiles.append(_columns(i["w_out"][l]))
    w = i["w_in_2"][0]
    order = [h for j in range(4) for h in (j, 4 + j)]
    heads = np.concatenate([np.arange(h * 64, h * 64 + 64) for h in order])
    tiles.append(_columns(w[:, heads]))
    for c in (512, 640, 768, 1024):
        tiles.append(_columns(w[:, c:c + P]))
    tiles.append(_columns(w[:, 1304:1816]))
    tiles.append(_columns(w[:, 1816:2328]))
    tiles.append(_rows(w[:, 2328:2840]))
    vsg = np.zeros((D, 512), w.dtype)
    vsg[:, 0:128], vsg[:, 128:256], vsg[:, 256:280] = w[:, 896:1024], w[:, 1152:1280], w[:, 1280:1304]
    tiles.append(_rows(vsg))
    for n in ("nsa_ck_w1_2", "nsa_cv_w1_2"):
        tiles.append(i[n][0].reshape(4, 4, P, 256).transpose(0, 2, 1, 3).reshape(4, P, 1024))
    merged([i["w_up_nsa_2"][0][heads], i["w_up_moba_2"][0]], [w[:, 2840:3864], w[:, 3864:4888]])
    tiles.append(_columns(i["w_out_2"][0]))
    f = i["w_ffn_in_2"][0]
    g, u = _columns(f[:, :D_FF]), _columns(f[:, D_FF:])
    tiles.append(np.stack([g, u], axis=1).reshape(2 * FT, P, D))
    tiles.append(i["w_ffn_out_2"][0].reshape(FT, P, D))
    tiles.append(_columns(i["w_ple_gate_2"][0]))
    tiles.append(i["w_ple_proj_2"][0].reshape(2, P, 2, 4, P).transpose(2, 1, 3, 0, 4).reshape(2, P, 1024))
    a = {"stream": np.concatenate(tiles)}
    assert a["stream"].shape == (TILES, P, 1024), a["stream"].shape

    a["x"], a["ctx"] = _feat(i["x"][0]), _feat(i["ctx"][0])
    a["cond"] = np.stack([_vec(i["c"][0]), _vec(i["c_ctx"])], axis=2)
    a["lambda"] = np.broadcast_to(i["da_lambda"], (P,) + i["da_lambda"].shape)
    for l in range(DEPTH):
        a[f"ada_b{l}"], a[f"norm_pre{l}"], a[f"norm_post{l}"] = _vec(i["ada_b"][l]), _vec(i["norm_pre"][l]), _vec(i["norm_post"][l])
        a[f"subln{l}"] = i["da_subln"][l][:, None]
        a[f"hy_w1{l}"], a[f"hy_w2{l}"], a[f"hy_w3{l}"] = i["hy_f_w1"][l], i["hy_f_w2"][l], i["hy_f_w3"][l]
        a[f"hy_b1{l}"], a[f"hy_b2{l}"] = i["hy_f_b1"][l][:, None], i["hy_f_b2"][l][:, None]
        a[f"hy_freq{l}"] = i["hy_f_freq"][l].T
        a[f"hy_sw{l}"] = np.stack([_vec(r) for r in (*i["hy_short_w"][l], i["hy_short_b"][l])], axis=2)
        a[f"hy_bias{l}"] = _vec(i["hy_bias"][l])
        a[f"ln_g{l}"], a[f"ln_b{l}"] = (np.broadcast_to(i[n][l], (P, BR)) for n in ("gm_ln_g", "gm_ln_b"))
        a[f"gm_ws{l}"] = i["gm_ws"][l].transpose(2, 0, 1)
        a[f"gm_bs{l}"] = np.repeat(i["gm_bs"][l], 64, axis=0).reshape(4, P, P).transpose(1, 0, 2)
    a["pos"] = np.broadcast_to(i["positions_2"], (P, TOK))
    a["ple"] = _feat(i["p_2"][0, 0]).reshape(P, 2 * TOK)
    for n in ("g_mix", "g_ffn", "g_ple"):
        a[n] = _vec(i[n + "_2"][0])
    a["ck_w2"], a["cv_w2"] = (i[n][0].reshape(2, P, 64).transpose(1, 0, 2) for n in ("nsa_ck_w2_2", "nsa_cv_w2_2"))
    a["pe_k"], a["pe_v"] = (i[n][0].reshape(16, P).T for n in ("nsa_pe_k_2", "nsa_pe_v_2"))
    gains = ["nsa_q_gain_2"] * 4 + ["nsa_ks_gain_2", "nsa_kw_gain_2"] + ["moba_q_gain_2"] * 4 + ["moba_k_gain_2"] * 4 + ["nsa_kc_gain_2"]
    a["head_gain"] = np.stack([np.tile(i[n][0], 2) for n in gains], axis=1)

    f = np.float32
    a["ident"] = np.eye(P, dtype=f)
    d = np.arange(P)
    inv = (f(10000.0) ** (-np.arange(16, dtype=f) / f(16))).astype(f)
    t = np.arange(TOK)
    coord = np.where((d[:, None] % 64) < 32, t[None, :] // 64, t[None, :] % 64).astype(f)
    ang = (coord * inv[d % 16][:, None]).astype(f).astype(np.float64)
    a["rope"] = np.stack([np.cos(ang), np.sin(ang)], axis=1).astype(f)

    def rotation(half, width, rotated):
        m = np.zeros((P, P), f)
        for x in range(P):
            if x % 64 < rotated:
                if x % width < half:
                    m[x + half, x] = -1.0
                else:
                    m[x - half, x] = 1.0
        return m
    a["perm1"], a["perm2"] = rotation(16, 32, 64), rotation(8, 16, 16)
    inv2 = (f(500000.0) ** (-np.arange(8, dtype=f) / f(8))).astype(f)
    a["inv_freq"] = np.where(d % 64 < 16, inv2[d % 8], f(0.0)).astype(f)[:, None]
    lt = np.linspace(0.0, 1.0, TOK, dtype=f)[:, None]
    wpos = (f(2.0 * math.pi / TOK) * np.arange(TOK, dtype=f))[:, None]
    bands = np.linspace(1e-4, 15, 16, dtype=f)[None, :]
    bw = (bands * wpos).astype(np.float64)
    a["hy_z"] = np.concatenate([lt, np.cos(bw), -np.sin(bw)], axis=1).astype(f).T
    deltas = np.abs(np.linspace(math.log(1e-2) / 1.5, math.log(1e-2) / 0.3, BR, dtype=f))
    a["hy_decay"] = np.exp((-lt * deltas).astype(np.float64)).astype(f).reshape(2, P, BR).transpose(1, 0, 2)
    w = 2.0 * math.pi * (np.arange(TOK) + 0.5) / 512.0
    c, s = np.cos(w[None, :] * t[:, None]), -np.sin(w[None, :] * t[:, None])
    a["dft"] = np.concatenate([c, s], axis=1).astype(f).reshape(2, P, 512).transpose(1, 0, 2)
    a["idft"] = (np.concatenate([c.T, s.T], axis=0) / TOK).astype(f).reshape(4, P, TOK).transpose(1, 0, 2)
    q, k = np.arange(P)[:, None], np.arange(P)[None, :]
    a["causal"] = np.concatenate([np.zeros((P, P), f), np.where(k <= q, 0.0, NEG).astype(f)], axis=1)
    end = np.arange(NCMP) * 16 + 31
    keep = (end[None, None, :] <= (np.arange(P)[:, None, None] + P * np.arange(2)[None, :, None]))
    a["cmp_keep"], a["cmp_add"] = keep.astype(f), np.where(keep, 0.0, NEG).astype(f)
    hs = np.zeros((P, 14, 32), f)
    sp = np.zeros((32, 14, P), f)
    for n in range(14):
        for half in range(2):
            hs[half * 64:half * 64 + 64, n, 2 * n + half] = 1.0 / 64
            sp[2 * n + half, n, half * 64:half * 64 + 64] = 1.0
    a["head_sum"], a["head_spread"] = hs, sp
    a["block_mean"] = np.kron(np.eye(2, dtype=f), np.full((64, 64), 1.0 / 64, f))
    return {n: np.ascontiguousarray(x) for n, x in a.items()}


def kernel(**inputs):
    import concourse.bacc as bacc
    from concourse.bass_utils import run_bass_kernel_spmd

    arrays = _layout({n: np.asarray(x) for n, x in inputs.items()})
    nc = bacc.Bacc("TRN2", target_bir_lowering=False, num_devices=1)
    ins = {n: nc.dram_tensor(f"in_{n}", x.shape, mybir.dt.from_np(x.dtype), kind="ExternalInput").ap() for n, x in arrays.items()}
    out = nc.dram_tensor("out", (P, KT, TOK), F32, kind="ExternalOutput").ap()
    program(nc, ins, out)
    r = run_bass_kernel_spmd(nc, [{f"in_{n}": x for n, x in arrays.items()}], core_ids=[0])
    y = r.results[0]["out"]
    return y.transpose(2, 1, 0).reshape(1, TOK, D)
```

```python
import math
from contextlib import ExitStack, contextmanager

import numpy as np

import concourse.bass as bass
from concourse import mybir

F32 = mybir.dt.float32
F32R = mybir.dt.float32r
I32 = mybir.dt.int32
ACT = mybir.ActivationFunctionType
ALU = mybir.AluOpType
AXX = mybir.AxisListType.X

P = 128
D = 1024
KT = D // P
TOK = 256
ALL = 2 * TOK
BR = 512
BT = BR // P
HEADS = 4
DEPTH = 2
EPS = 1e-6
RAW = 4
SPLIT = 4
AHEAD = 2
D_FF = 2816
FT = D_FF // P
NCMP = 15
NEG = -1e30
TWO_PI = 2.0 * math.pi
MAGIC = 1.5 * 2.0 ** 23
LAYER_TILES = 24 + 4 + 4 + 4 + 12 + 4 + 4 + 12 + 36 + 8
TILES = DEPTH * LAYER_TILES + 8 + 8 + 4 + 4 + 4 + 4 + 24 + 8 + 2 * FT + FT + 8 + 2


def pi_parts():
    parts, rest = [], TWO_PI
    for _ in range(3):
        scale = 2.0 ** (8 - math.ceil(math.log2(rest)))
        part = math.floor(rest * scale) / scale
        parts.append(part)
        rest -= part
    return parts + [float(np.float32(rest))]


class Count:

    def __init__(self, sem):
        self.sem, self.off, self.sym = sem, 0, None

    def value(self, k=0):
        v = self.off + k
        return v if self.sym is None else self.sym + v


class Line:

    def __init__(self, eng, sem):
        self.eng, self.count = eng, Count(sem)

    def mark(self, ins):
        ins.then_inc(self.count.sem, 1)
        self.count.off += 1
        return (self.count, self.count.value())

    def wait(self, *marks):
        for m in marks:
            if m is not None:
                self.eng.wait_ge(m[0].sem, m[1])

    def last(self):
        return (self.count, self.count.value())

    def settle(self):
        self.eng.wait_ge(self.count.sem, self.count.value())


class SquareSum:

    def __init__(self, p, n, tiles=KT):
        self.p, self.n, self.tiles, self.k = p, n, tiles, 0
        self.late, self.read, self.factor = None, [None, None], None

    def add(self, src, *waits, mark=None):
        p, k = self.p, self.k
        p.act.wait(self.read[k % 2], *waits)
        a = (mark or p.act.mark)(p.nc.scalar.activation(p.tmp[:, k % 2, 0:self.n], src, ACT.Square))
        self.flush()
        self.late = (k, a)
        self.k += 1

    def flush(self):
        if self.late:
            p, (k, a) = self.p, self.late
            p.pe.wait(a)
            self.read[k % 2] = p.pe.mark(p.nc.tensor.matmul(p.M[0][:, 0:self.n], p.mean_all, p.tmp[:, k % 2, 0:self.n], start=(k == 0), stop=(k == self.tiles - 1)))
            self.late = None

    def finish(self):
        if self.factor is None:
            self.flush()
            p = self.p
            self.factor = p.rsqrt(p.tmp[:, 2, 0:self.n], p.M[0][:, 0:self.n], self.read[(self.tiles - 1) % 2])
        return self.factor


class Program:
    def __init__(self, nc, ctx, ins, out):
        self.nc, self.ctx, self.ins, self.out = nc, ctx, ins, out
        self.act = Line(nc.scalar, self.sem("act"))
        self.dve = Line(nc.vector, self.sem("dve"))
        self.pe = Line(nc.tensor, self.sem("pe"))
        self.hi = Count(self.sem("tile_hi"))
        self.lo = Count(self.sem("tile_lo"))
        self.used = Count(self.sem("tile_used"))
        self.free = Count(self.sem("bank_free"))
        self.arrived = [self.sem(f"tile_arrived{r}") for r in range(RAW)]
        self.split_at = 0
        self.early = 0
        self.sym_tile = None
        self.loads = {}
        self.fillers = []
        self.ready = None
        self.G = [ctx.enter_context(nc.psum_tensor(f"gemm_bank{i}", [P, 512], F32)) for i in range(4)]
        self.M = [ctx.enter_context(nc.psum_tensor(f"misc_bank{i}", [P, 512], F32)) for i in range(4)]
        sb = self.sb
        self.raw = sb("raw", [P, RAW, 1024])
        self.whi = sb("whi", [P, SPLIT, 1024], F32R)
        self.wlo = sb("wlo", [P, SPLIT, 1024], F32R)
        self.x = sb("x", [P, KT, ALL])
        self.hhi = sb("hhi", [P, KT, ALL], F32R)
        self.hlo = sb("hlo", [P, KT, ALL], F32R)
        at = nc.sbuf_base
        self.arena = sb("arena", [P, 24, ALL])
        self.arena_r = nc.alloc_sbuf_tensor_at("arena_r", [P, 24, ALL], F32R, offset=at)
        at = nc.sbuf_base
        self.y = sb("y", [P, 12, ALL])
        self.y_r = nc.alloc_sbuf_tensor_at("y_r", [P, 12, ALL], F32R, offset=at)
        self.tmp = sb("tmp", [P, 5, ALL])
        self.kre, self.kim = self.y[:, 8:10, :], self.y[:, 10:12, :]
        self.wt = self.y[:, 4:6, :].rearrange("p a (b q) -> p (a b) q", q=TOK)
        self.stat = sb("stat", [P, 40])
        self.hy_rs = sb("hy_rs", [P, BT])

    def sem(self, name):
        return self.ctx.enter_context(self.nc.semaphore(name))

    def sb(self, name, shape, dt=F32):
        return self.ctx.enter_context(self.nc.sbuf_tensor(name, shape, dt))

    def load(self, name, dst=None, src=None, dt=F32, eng=None):
        src = self.ins[name] if src is None else src
        if dst is None:
            dst = self.sb(name + "_sb", list(src.shape), dt)[:]
        s = self.sem("in_" + name)
        (eng or self.nc.scalar).dma_start(dst, src).then_inc(s, 16)
        self.loads[name] = (dst, s)
        return dst

    def need(self, line, *names):
        for n in names:
            line.eng.wait_ge(self.loads[n][1], 16)

    @contextmanager
    def roll(self, n, **step):
        counts = {"act": self.act.count, "dve": self.dve.count, "pe": self.pe.count, "tile": self.used, "bank": self.free}
        start = {k: c.off for k, c in counts.items()}
        split0, early = self.split_at, self.early
        assert step["tile"] % SPLIT == 0 and step.get("bank", 0) % 4 == 0
        eng = (mybir.EngineType.PE, mybir.EngineType.Activation, mybir.EngineType.DVE)
        with self.nc.Fori(0, n, 1, engines=eng) as i:
            for k, c in counts.items():
                c.sym = i * step.get(k, 0) if step.get(k, 0) else None
            self.sym_tile = i * step["tile"]
            yield i
        for k, c in counts.items():
            assert c.off == start[k] + step.get(k, 0), (k, c.off - start[k], step.get(k, 0))
            c.off = start[k] + n * step.get(k, 0)
            c.sym = None
        assert self.early == early
        self.split_at = split0 + n * step["tile"]
        self.sym_tile = None

    def plus(self, v):
        return v if self.sym_tile is None else self.sym_tile + v

    def fill(self, n=1):
        while n and self.fillers:
            self.fillers.pop(0)()
            n -= 1

    def stream(self):
        sp, w, s_lo = self.nc.sync, self.ins["stream"], self.lo.sem
        for r in range(RAW):
            sp.dma_start(self.raw[:, r, :], w[r]).then_inc(self.arrived[r], 16)
        turns, rest = divmod(TILES - RAW, RAW)
        with sp.Fori(0, turns, 1) as i:
            for r in range(RAW):
                sp.wait_ge(s_lo, i * RAW + (r + 1))
                sp.dma_start(self.raw[:, r, :], w[i * RAW + (RAW + r)]).then_inc(self.arrived[r], 16)
        for r in range(rest):
            sp.wait_ge(s_lo, turns * RAW + r + 1)
            sp.dma_start(self.raw[:, r, :], w[turns * RAW + RAW + r]).then_inc(self.arrived[r], 16)

    def split_hi(self):
        t, act = self.split_at, self.nc.scalar
        if self.sym_tile is None and t >= TILES:
            return
        r, s = t % RAW, t % SPLIT
        act.wait_ge(self.arrived[r], self.plus(t - r) * (16 // RAW) + 16)
        if t >= SPLIT:
            act.wait_ge(self.used.sem, self.plus(t - SPLIT + 1))
        act.activation(self.whi[:, s, :], self.raw[:, r, :], ACT.Copy).then_inc(self.hi.sem, 1)

    def split_lo(self):
        t, dve = self.split_at, self.nc.vector
        if self.sym_tile is None and t >= TILES:
            return
        r, s = t % RAW, t % SPLIT
        dve.wait_ge(self.hi.sem, self.plus(t + 1))
        dve.tensor_tensor(self.wlo[:, s, :], self.raw[:, r, :], self.whi[:, s, :].bitcast(F32), ALU.subtract).then_inc(self.lo.sem, 1)
        self.split_at += 1
        self.early += 1

    def split(self):
        self.split_hi()
        self.split_lo()

    def tile(self, products):
        if self.early <= AHEAD:
            self.split()
        self.early -= 1
        t = self.used.off
        self.nc.tensor.wait_ge(self.lo.sem, self.plus(t + 1))
        s = t % SPLIT
        last = products(self.whi[:, s, :], self.wlo[:, s, :])
        last.then_inc(self.used.sem, 1)
        self.used.off += 1
        return (self.used, self.used.value())

    def bank(self):
        e = self.free.off
        if e >= 4:
            self.nc.tensor.wait_ge(self.free.sem, self.free.value(-3))
        return self.G[e % 4]

    def release(self, ins):
        ins.then_inc(self.free.sem, 1)
        self.free.off += 1
        return (self.free, self.free.value())

    def three(self, out, w_hi, w_lo, r_hi, r_lo, first, last):
        mm = self.nc.tensor.matmul
        mm(out, w_lo, r_hi, start=first, stop=False)
        mm(out, w_hi, r_lo, start=False, stop=False)
        return mm(out, w_hi, r_hi, start=False, stop=last)

    def feature_tile(self, n, rhs=None, col=0, nk=KT, bank=None):
        r_hi, r_lo = rhs or (self.hhi, self.hlo)

        def products(hi, lo):
            for k in range(nk):
                if self.ready:
                    self.pe.wait(self.ready[k])
                c = slice(col + k * P, col + (k + 1) * P)
                m = self.three(bank[:, 0:n], hi[:, c], lo[:, c], r_hi[:, k, 0:n], r_lo[:, k, 0:n], k == 0, k == nk - 1)
            self.ready = None
            return m
        return products

    def token_gemm(self, ntt, evacuate, width=512):
        banks = []

        def one(g):
            def run():
                if g == 0:
                    for j in range(ntt):
                        self.nc.tensor.wait_ge(self.free.sem, self.free.value(j - 3))
                        banks.append(self.G[(self.free.off + j) % 4])

                def products(hi, lo):
                    for kk in range(2):
                        k = 2 * g + kk
                        c = slice(kk * 512, kk * 512 + width)
                        for j in range(ntt):
                            tk = slice(j * P, (j + 1) * P)
                            m = self.three(banks[j][:, 0:width], self.hhi[:, k, tk], self.hlo[:, k, tk], hi[:, c], lo[:, c], k == 0, k == KT - 1)
                    return m
                u = self.tile(products)
                if g == 3:
                    self.act.wait(u)
                    for j in range(ntt):
                        self.release(evacuate(j, banks[j]))
            return run
        return [one(g) for g in range(4)]

    def feature_gemm(self, tiles, n, evacuate):
        def one(j):
            def run():
                b = self.bank()
                u = self.tile(self.feature_tile(n, bank=b))
                self.release(evacuate(j, b, u))
            return run
        return [one(j) for j in range(tiles)]

    def halves(self, hi, lo, src, scale=1.0, waits=()):
        self.act.wait(*waits)
        a = self.act.mark(self.nc.scalar.activation(hi, src, ACT.Copy, scale=scale))
        self.dve.wait(a)
        return self.dve.mark(self.nc.vector.scalar_tensor_tensor(lo, src, scale, hi.bitcast(F32), ALU.mult, ALU.subtract))

    def rsqrt(self, dst, src, mark, bias=None):
        p = dst.shape[0]
        self.act.wait(mark)
        a = self.act.mark(self.nc.scalar.activation(dst, src, ACT.Sqrt, bias=(self.eps if bias is None else bias)[0:p, :]))
        self.dve.wait(a)
        return self.dve.mark(self.nc.vector.reciprocal(dst, dst))

    def sine(self, dst, arg, tmp, mark, p, big=False, shift=0.0):
        v, dve = self.nc.vector, self.dve
        k = tmp
        parts = pi_parts()
        dve.wait(mark)

        def go(ins):
            dve.mark(ins)
            dve.settle()
        for stage in ([4096.0] if big else []) + [1.0]:
            sh = shift if stage == 1.0 else 0.0
            go(v.tensor_scalar(k, arg, 1.0 / (TWO_PI * stage), sh / TWO_PI, ALU.mult, ALU.add))
            go(v.tensor_scalar(k, k, MAGIC, None, ALU.add))
            go(v.tensor_scalar(k, k, MAGIC, None, ALU.subtract))
            for c in parts:
                go(v.scalar_tensor_tensor(arg, k, -c * stage, arg, ALU.mult, ALU.add))
        if shift:
            go(v.tensor_scalar(arg, arg, shift, None, ALU.add))
        go(v.tensor_scalar(arg, arg, 3.1415925, -3.1415925, ALU.min, ALU.max))
        self.act.wait(dve.last())
        return self.act.mark(self.nc.scalar.activation(dst, arg, ACT.Sin))

    def constants(self):
        nc, dve = self.nc, self.nc.vector
        self.mean_all = self.sb("mean_all", [P, P])[:]
        self.ident = self.loads["ident"][0]
        self.ones = self.sb("ones", [P, 1])[:]
        self.eps = self.sb("eps", [P, 1])[:]
        self.zero = self.sb("zero", [P, 1])[:]
        for ap, v in ((self.mean_all, 1.0 / D), (self.ones, 1.0), (self.eps, EPS), (self.zero, 0.0)):
            self.dve.mark(dve.memset(ap, v))
        self.mean_col = self.sb("mean_col", [P, 31])[:]
        self.dve.mark(dve.memset(self.mean_col, 0.0))
        self.dve.settle()
        self.dve.mark(dve.memset(self.mean_col[:, 15:16], 1.0 / P))
        self.const = self.dve.last()
        self.need(self.pe, "ident")
        for line in (self.act, self.pe, self.dve):
            line.wait(self.const)

    def condition(self):
        nc = self.nc
        self.chi = self.sb("chi", [P, KT, 2], F32R)
        self.clo = self.sb("clo", [P, KT, 2], F32R)
        c = self.loads["cond"][0]
        th = self.sb("c_tanh", [P, KT, 2])[:]
        self.need(self.act, "cond")
        self.need(self.dve, "cond")
        a = self.act.mark(nc.scalar.activation(th, c, ACT.Tanh, scale=0.5))
        self.dve.wait(a)
        d = self.dve.mark(nc.vector.scalar_tensor_tensor(th, th, 1.0, c, ALU.add, ALU.mult))
        self.dve.settle()
        self.cond_mark = self.halves(self.chi[:], self.clo[:], th, 0.5, (d,))
        self.mods = [self.sb(f"mod{l}", [P, 24, 2]) for l in range(DEPTH)]
        self.A = self.sb("modA", [P, KT, 2])

    def modulation_gemm(self, l, rows):
        nc, act, pe, dve = self.nc, self.act, self.pe, self.dve
        banks = []

        def one(c, k):
            def run():
                if k == 0:
                    if c == 0:
                        pe.wait(self.cond_mark)
                    banks.clear()
                    for j in range(2):
                        if self.free.off + j >= 4:
                            nc.tensor.wait_ge(self.free.sem, self.free.value(j - 3))
                        banks.append(self.G[(self.free.off + j) % 4])

                def products(hi, lo):
                    for j in range(2):
                        m = self.three(banks[j][0:2, :], self.chi[:, k, :], self.clo[:, k, :], hi[:, j * 512:(j + 1) * 512], lo[:, j * 512:(j + 1) * 512], k == 0, k == KT - 1)
                    return m
                u = self.tile(products)
                if k == KT - 1:
                    act.wait(u)
                    if c:
                        act.wait(self.turned)
                    for j in range(2):
                        done = self.release(nc.scalar.activation(rows[:, j, :], banks[j][0:2, :], ACT.Copy))
                    b = self.bank()
                    pe.wait(done)
                    for m in range(8):
                        t = nc.tensor.transpose(b[:, 2 * m:2 * m + 2], rows[:, m // 4, (m % 4) * P:(m % 4 + 1) * P], self.ident[0:2, 0:2])
                    self.turned = pe.mark(t)
                    dve.wait(self.turned)
                    self.release(nc.vector.tensor_copy(self.mods[l][:, 8 * c:8 * c + 8, :], b[:, 0:16].rearrange("p (m s) -> p m s", s=2)))
            return run
        return [one(c, k) for c in range(3) for k in range(KT)]

    def modulation(self, l):
        nc = self.nc
        self.mod = self.mods[l]
        self.need(self.dve, f"ada_b{l}", f"norm_pre{l}", f"norm_post{l}")
        v, dve = nc.vector, self.dve
        self.dve.wait((self.free, self.free.value()))

        def bc(name, n):
            return self.loads[name][0].unsqueeze(2).broadcast_to([P, n, 2])
        dve.mark(v.tensor_tensor(self.mod[:], self.mod[:], bc(f"ada_b{l}", 24), ALU.add))
        dve.settle()
        dve.mark(v.scalar_tensor_tensor(self.A[:], self.mod[:, 8:16, :], 1.0, bc(f"norm_pre{l}", 8), ALU.add, ALU.mult))
        dve.mark(v.tensor_tensor(self.mod[:, 16:24, :], self.mod[:, 16:24, :], bc(f"norm_post{l}", 8), ALU.mult))
        self.need(dve, f"subln{l}")
        self.subg = self.sb(f"sub_gain{l}", [P, 1])[:]
        dve.mark(v.tensor_scalar(self.subg, self.loads[f"subln{l}"][0], 0.2 + 0.6 * math.exp(-0.3 * l), None, ALU.mult))
        return dve.last()

    def make_h(self, n, scaled, shift, r_mark):
        nc, v, act, dve = self.nc, self.nc.vector, self.act, self.dve
        dve.wait(r_mark)
        dve.settle()
        act.settle()
        slots = (0, 1, 3, 4)
        marks, ready = [None] * KT, []
        for k in range(KT + 1):
            if k < KT:
                t = self.tmp[:, slots[k % 4], 0:n]
                if k >= 4:
                    dve.wait(ready[k - 4])
                scaled(k, t)
                marks[k] = dve.last()
                act.wait(marks[k])
                for s in range(n // TOK):
                    c = slice(s * TOK, (s + 1) * TOK)
                    if shift:
                        a = act.mark(nc.scalar.activation(self.hhi[:, k, c], t[:, c], ACT.Identity, bias=shift(k, s)))
                if not shift:
                    a = act.mark(nc.scalar.activation(self.hhi[:, k, 0:n], t, ACT.Copy))
                marks[k] = a
            if k:
                q = k - 1
                t = self.tmp[:, slots[q % 4], 0:n]
                dve.wait(marks[q])
                if shift:
                    for s in range(n // TOK):
                        c = slice(s * TOK, (s + 1) * TOK)
                        m = dve.mark(v.scalar_tensor_tensor(self.hlo[:, q, c], t[:, c], shift(q, s), self.hhi[:, q, c].bitcast(F32), ALU.add, ALU.subtract))
                else:
                    m = dve.mark(v.tensor_tensor(self.hlo[:, q, 0:n], t, self.hhi[:, q, 0:n].bitcast(F32), ALU.subtract))
                ready.append(m)
        self.ready = ready
        return ready[-1]

    def pre_norm(self, mod_mark, sums, normed):
        v = self.nc.vector
        m = sums.finish()
        self.act.wait(mod_mark)

        def scaled(k, t):
            for s in range(2):
                c = slice(s * TOK, (s + 1) * TOK)
                self.dve.mark(v.scalar_tensor_tensor(t[:, c], self.x[:, k, c], self.A[:, k, s:s + 1], self.tmp[:, 2, c], ALU.mult, ALU.mult))

        def shifted(k, t):
            for s in range(2):
                c = slice(s * TOK, (s + 1) * TOK)
                self.dve.mark(v.tensor_scalar(t[:, c], normed[:, k, c], self.A[:, k, s:s + 1], self.mod[:, k, s:s + 1], ALU.mult, ALU.add))
        if normed is not None:
            return self.make_h(ALL, shifted, None, m)
        return self.make_h(ALL, scaled, lambda k, s: self.mod[:, k, s:s + 1], m)

    def lam(self, l):
        nc, v, dve = self.nc, self.nc.vector, self.dve
        src = self.loads["lambda"][0]
        self.need(dve, "lambda")
        t = self.sb(f"lam_t{l}", [P, 2, 64])[:]
        e = self.sb(f"lam_e{l}", [P, 4])[:]
        for j in range(2):
            dve.mark(v.tensor_tensor(t[:, j, :], src[:, l, 2 * j, :], src[:, l, 2 * j + 1, :], ALU.mult))
        dve.settle()
        d = dve.mark(v.tensor_reduce(e[:, 0:2], t, AXX, ALU.add))
        self.act.wait(d)
        a = self.act.mark(nc.scalar.activation(e[:, 0:2], e[:, 0:2], ACT.Exp))
        dve.wait(a)
        dve.mark(v.tensor_tensor(e[:, 2:3], e[:, 1:2], e[:, 0:1], ALU.subtract))
        dve.settle()
        dve.mark(v.tensor_scalar(e[:, 3:4], e[:, 2:3], -(0.8 - 0.6 * math.exp(-0.3 * l)), None, ALU.add))
        dve.settle()
        return e[:, 3:4]

    def rope(self, ap, n, cos, sin, perm, mark, bank, tmp):
        nc, v, dve = self.nc, self.nc.vector, self.dve
        self.pe.wait(mark)
        p = self.pe.mark(nc.tensor.matmul(bank[:, 0:n], perm, ap, start=True, stop=True))
        dve.wait(p)
        dve.mark(v.tensor_tensor(tmp[:, 0:n], bank[:, 0:n], sin, ALU.mult))
        dve.mark(v.tensor_tensor(ap, ap, cos, ALU.mult))
        dve.settle()
        return dve.mark(v.tensor_tensor(ap, ap, tmp[:, 0:n], ALU.add))

    def diff_attention(self, l, parts, Kt, Qt, V, neg_lam, marks):
        nc, v, dve, act, pe = self.nc, self.nc.vector, self.dve, self.act, self.pe
        st = self.stat
        S = (self.M[0], self.M[1])
        units = [(part, h, i) for part in parts for h in range(HEADS) for i in range(2)]
        pe.wait(*marks)
        dve.wait(*marks)
        w_read = [None, None]
        wt_copied, pv_done, out_done, exp_done = [], [None], [None], [None]

        def scores(u):
            (q_off, k_off, nkeys), h, i = units[u]
            q = slice(q_off + i * P, q_off + (i + 1) * P)
            pe.wait(exp_done[0])
            for m in range(2):
                r = slice(m * 64, (m + 1) * 64)
                p = pe.mark(nc.tensor.matmul(S[m][:, 0:nkeys], Qt[r, h, q], Kt[r, h, k_off:k_off + nkeys], start=True, stop=True))
            return p

        def softmax(u, s_mark):
            nkeys = units[u][0][2]
            c = 10 * (u % 2)
            dve.wait(s_mark)
            for m in range(2):
                dve.mark(v.tensor_reduce(st[:, c + m:c + m + 1], S[m][:, 0:nkeys], AXX, ALU.max, negate=True))
            dve.settle()
            act.wait(dve.mark(v.tensor_scalar(st[:, c + 2:c + 4], st[:, c:c + 2], 0.125, None, ALU.mult)))
            for m in range(2):
                exp_done[0] = act.mark(nc.scalar.activation(self.tmp[:, m, 0:nkeys], S[m][:, 0:nkeys], ACT.Exp, bias=st[:, c + 2 + m:c + 3 + m], scale=0.125, accum_out=st[:, c + 4 + m:c + 5 + m]))

        def weights(u):
            nkeys = units[u][0][2]
            c = 10 * (u % 2)
            dve.wait(exp_done[0])
            dve.mark(v.reciprocal(st[:, c + 6:c + 8], st[:, c + 4:c + 6]))
            dve.settle()
            dve.mark(v.tensor_tensor(st[:, c + 7:c + 8], st[:, c + 7:c + 8], neg_lam, ALU.mult))
            dve.mark(v.tensor_scalar(self.tmp[:, 0, 0:nkeys], self.tmp[:, 0, 0:nkeys], st[:, c + 6:c + 7], None, ALU.mult))
            dve.settle()
            dve.wait(w_read[0])
            return dve.mark(v.scalar_tensor_tensor(self.tmp[:, 2, 0:nkeys], self.tmp[:, 1, 0:nkeys], st[:, c + 7:c + 8], self.tmp[:, 0, 0:nkeys], ALU.mult, ALU.add))

        def turn(u, w_mark):
            nkt = units[u][0][2] // P
            pe.wait(w_mark, *wt_copied[-1:])
            for kt in range(nkt):
                p = nc.tensor.transpose(self.M[2][:, kt * P:(kt + 1) * P], self.tmp[:, 2, kt * P:(kt + 1) * P], self.ident)
            w_read[0] = pe.mark(p)
            act.wait(w_read[0], pv_done[0])
            i = units[u][2]
            wt_copied.append(act.mark(nc.scalar.activation(
                self.wt[:, 0:nkt, i * P:(i + 1) * P], self.M[2][:, 0:nkt * P].rearrange("p (k q) -> p k q", k=nkt), ACT.Copy)))

        def values(u):
            (q_off, k_off, nkeys), h, i = units[u]
            if i == 0:
                return
            nkt = nkeys // P
            pe.wait(wt_copied[-1], out_done[0])
            for kt in range(nkt):
                p = nc.tensor.matmul(self.M[3][:, 0:TOK], V[:, k_off // P + kt, h * P:(h + 1) * P], self.wt[:, kt, :], start=(kt == 0), stop=(kt == nkt - 1))
            pv_done[0] = pe.mark(p)
            act.wait(pv_done[0])
            out_done[0] = act.mark(nc.scalar.activation(self.y[:, h, q_off:q_off + TOK], self.M[3][:, 0:TOK], ACT.Copy))

        softmax(0, scores(0))
        for u in range(len(units)):
            w = weights(u)
            self.fill()
            s = scores(u + 1) if u + 1 < len(units) else None
            turn(u, w)
            if s:
                softmax(u + 1, s)
            if u % 2 and len(parts) == 1:
                self.fill()
            values(u)
        self.fill(12)
        self.need(dve, f"subln{l}")
        n = len(parts) * TOK
        nq = n // P
        act.settle()
        act.wait(dve.last())
        pe.wait(dve.last(), act.last())
        sq_read = [None, None]
        for h in range(HEADS):
            sq = self.tmp[:, h % 2, 0:n]
            act.wait(sq_read[h % 2])
            a = act.mark(nc.scalar.activation(sq, self.y[:, h, 0:n], ACT.Square))
            pe.wait(a)
            for q in range(nq):
                e = h * nq + q
                p = nc.tensor.matmul(self.M[0][0:16, 0:P], self.mean_col[:, 15 - e:31 - e], sq[:, q * P:(q + 1) * P], start=(e == 0), stop=(e == HEADS * nq - 1))
            sq_read[h % 2] = pe.mark(p)
        r = self.tmp[0:16, 2, 0:P]
        pe.wait(self.rsqrt(r, self.M[0][0:16, 0:P], sq_read[1]))
        act.settle()
        scaled = {}
        for h in range(HEADS):
            b = self.M[1 + h % 2]
            if h >= 2:
                pe.wait(scaled[h - 2])
            for q in range(nq):
                e = h * nq + q
                p = nc.tensor.matmul(b[:, q * P:(q + 1) * P], self.ident[0:16, e:e + 1].broadcast_to([16, P]), r, start=True, stop=True)
            dve.wait(pe.mark(p))
            yh = self.y[:, h, 0:n]
            scaled[h] = dve.mark(v.scalar_tensor_tensor(yh, yh, self.subg, b[:, 0:n], ALU.mult, ALU.mult))
        return dve.last()

    def hyena_filter(self, l):
        nc, v, dve, act, pe = self.nc, self.nc.vector, self.dve, self.act, self.pe
        names = [f"hy_{n}{l}" for n in ("w1", "b1", "w2", "b2", "w3", "freq")]
        w3_at = self.y[0:64, 4:6, :].rearrange("p a n -> p (a n)")
        self.load(f"hy_w3{l}", w3_at, eng=nc.gpsimd)
        self.load(f"hy_decay{l}", self.y[:, 6:8, :], self.ins["hy_decay"], eng=nc.gpsimd)
        for line in (pe, dve):
            self.need(line, *names, "hy_z", f"hy_decay{l}", "dft")
        w1, b1, w2, b2, w3, fr = (self.loads[n][0] for n in names)
        z, decay, dft = (self.loads[n][0] for n in ("hy_z", f"hy_decay{l}", "dft"))
        hid = self.tmp[0:64, 0, 0:TOK]
        arg = self.tmp[0:64, 0, TOK:ALL]
        k = self.tmp[0:64, 1, 0:TOK]
        src = z
        m = None
        for s, (w, b, kk) in enumerate(((w1, b1, 33), (w2, b2, 64))):
            pe.wait(m)
            p = pe.mark(nc.tensor.matmul(self.M[0][0:64, 0:TOK], w, src, start=True, stop=True))
            dve.wait(p)
            dve.mark(v.tensor_scalar(arg, self.M[0][0:64, 0:TOK], b, fr[:, s:s + 1], ALU.add, ALU.mult))
            m = self.sine(hid, arg, k, dve.last(), 64)
            self.fill(2)
            src = hid
        pe.wait(m)
        f, b = self.arena[:, 0:2, :], self.arena[:, 2:4, :]
        for c, dst in ((0, f), (1, b)):
            for t in range(2):
                p = pe.mark(nc.tensor.matmul(self.M[2 * c + t][:, :], hid[:, t * P:(t + 1) * P], w3[:, c * BR:(c + 1) * BR], start=True, stop=True))
                dve.wait(p)
                dve.mark(v.tensor_tensor(dst[:, t, :], self.M[2 * c + t][:, :], decay[:, t, :], ALU.mult))
        self.fill(2)
        dve.settle()
        dve.mark(v.memset(b[0:1, 0, :], 0.0))
        dve.settle()
        act.wait(dve.last())
        pe.wait(dve.last())
        sq = self.arena[:, 4:8, :]
        for n in range(4):
            a = act.mark(nc.scalar.activation(sq[:, n, :], self.arena[:, n, :], ACT.Square))
        self.fill(2)
        pe.wait(a)
        for c in range(BT):
            for n in range(4):
                p = nc.tensor.matmul(self.M[0][:, c:c + 1], sq[:, n, c * P:(c + 1) * P], self.ones, start=(n == 0), stop=(n == 3))
        p = pe.mark(p)
        m = self.rsqrt(self.hy_rs[:], self.M[0][:, 0:BT], p, self.zero)
        s, d = self.arena[:, 8:10, :], self.arena[:, 10:12, :]
        dve.mark(v.tensor_tensor(s, f, b, ALU.add))
        dve.mark(v.tensor_tensor(d, f, b, ALU.subtract))
        self.fill(2)
        pe.wait(dve.last(), m)
        for part, src, dst in ((0, s, self.kre), (1, d, self.kim)):
            for ft in range(2):
                bank = self.M[(2 * part + ft) % 4]
                for t in range(2):
                    p = nc.tensor.matmul(bank[:, :], dft[:, t, part * TOK + ft * P:part * TOK + (ft + 1) * P], src[:, t, :], start=(t == 0), stop=(t == 1))
                p = pe.mark(p)
                act.wait(p)
                act.mark(nc.scalar.activation(dst[:, ft, :], bank[:, :], ACT.Copy))
        return act.last(), dve.last()

    def hyena_conv(self, l, seqs, marks):
        nc, v, dve, act, pe = self.nc, self.nc.vector, self.dve, self.act, self.pe
        n = seqs * TOK
        hy = self.arena[:, 0:12, :]
        for line in (dve, act, pe):
            line.wait(*marks)
        self.need(dve, f"hy_bias{l}")
        self.need(pe, "idft", "ident")
        idft, dft = self.loads["idft"][0], self.loads["dft"][0]
        for c in range(BT):
            dve.mark(v.tensor_tensor(hy[:, 4 + c, 0:n], hy[:, 4 + c, 0:n], hy[:, 8 + c, 0:n], ALU.mult))
        pe.wait(dve.last())
        ut = self.arena[:, 12:16, :]
        for s in range(seqs):
            for t in range(2):
                b = self.M[(2 * s + t) % 4]
                for c in range(BT):
                    o = s * TOK + t * P
                    p = nc.tensor.transpose(b[:, c * P:(c + 1) * P], hy[:, 4 + c, o:o + P], self.ident)
                p = pe.mark(p)
                act.wait(p)
                act.mark(nc.scalar.activation(ut[:, 2 * s + t, :], b[:, :], ACT.Copy))
        uts = act.last()
        self.fill()
        pe.wait(uts)
        for s in range(seqs):
            spec = hy[:, 8:12, :]
            inv_done = None if s == 0 else pe.last()
            dve.wait(inv_done)
            for ft in range(2):
                re, im = self.M[2 * ft], self.M[2 * ft + 1]
                for part, b in ((0, re), (1, im)):
                    for t in range(2):
                        p = nc.tensor.matmul(b[:, :], dft[:, t, part * TOK + ft * P:part * TOK + (ft + 1) * P], ut[:, 2 * s + t, :], start=(t == 0), stop=(t == 1))
                    p = pe.mark(p)
                dve.wait(p)
                t0, t1 = self.tmp[:, 0, :], self.tmp[:, 1, :]
                dve.mark(v.tensor_tensor(t0, im[:, :], self.kim[:, ft, :], ALU.mult))
                dve.mark(v.tensor_tensor(spec[:, ft, :], re[:, :], self.kre[:, ft, :], ALU.mult))
                dve.mark(v.tensor_tensor(t1, im[:, :], self.kre[:, ft, :], ALU.mult))
                dve.mark(v.tensor_tensor(spec[:, 2 + ft, :], re[:, :], self.kim[:, ft, :], ALU.mult))
                dve.settle()
                dve.mark(v.tensor_tensor(spec[:, ft, :], spec[:, ft, :], t0, ALU.subtract))
                dve.mark(v.tensor_tensor(spec[:, 2 + ft, :], spec[:, 2 + ft, :], t1, ALU.add))
                dve.settle()
            specs = dve.last()
            self.fill(1 if s == 0 and seqs > 1 else 2)
            pe.wait(specs)
            o = slice(s * TOK, (s + 1) * TOK)
            for c in range(BT):
                b = self.M[c]
                for k in range(4):
                    p = nc.tensor.matmul(b[:, 0:TOK], spec[:, k, c * P:(c + 1) * P], idft[:, k, :], start=(k == 0), stop=(k == 3))
                p = pe.mark(p)
                dve.wait(p)
                yb = self.y[:, 4 + c, o]
                dve.mark(v.tensor_scalar(yb, b[:, 0:TOK], self.hy_rs[:, c:c + 1], None, ALU.mult))
                dve.settle()
                dve.mark(v.scalar_tensor_tensor(yb, hy[:, 4 + c, o], self.loads[f"hy_bias{l}"][0][:, c:c + 1], yb, ALU.mult, ALU.add))
                dve.settle()
                dve.mark(v.tensor_tensor(yb, yb, hy[:, c, o], ALU.mult))
            ybs = dve.last()
            self.fill()
            pe.wait(ybs)
        return dve.last()

    def gmlp(self, l, ntt, marks):
        nc, v, dve, act, pe = self.nc, self.nc.vector, self.dve, self.act, self.pe
        self.need(dve, f"ln_g{l}", f"ln_b{l}", f"gm_bs{l}")
        self.need(pe, f"gm_ws{l}")
        g, b_, ws, bs = (self.loads[f"{n}{l}"][0] for n in ("ln_g", "ln_b", "gm_ws", "gm_bs"))
        dve.wait(*marks)
        u, vt = self.arena[:, 16:20, :], self.arena[:, 20:24, :]
        for t in range(ntt):
            x = vt[:, t, :]
            st = self.stat
            dve.mark(v.bn_stats(st[:, 8:14], x))
            dve.settle()
            dve.mark(v.bn_aggr(st[:, 14:16], st[:, 8:14]))
            m = self.rsqrt(st[:, 16:17], st[:, 15:16], dve.last())
            dve.wait(m)
            dve.mark(v.tensor_scalar(x, x, st[:, 14:15], st[:, 16:17], ALU.subtract, ALU.mult))
            dve.settle()
            dve.mark(v.tensor_tensor(x, x, g, ALU.mult))
            dve.settle()
            dve.mark(v.tensor_tensor(x, x, b_, ALU.add))
            dve.settle()
            self.fill(2)
        pe.wait(dve.last())
        freed = [None] * 4
        tm_read = [None] * 4
        for t in range(ntt):
            for j in range(BT):
                b = self.M[j]
                pe.wait(freed[j])
                p = pe.mark(nc.tensor.matmul(b[:, 0:2 * P], vt[:, t, j * P:(j + 1) * P], ws[:, 2 * j:2 * j + 2, :], start=True, stop=True))
                dve.wait(p)
                tm = self.tmp[:, 0, j * P:(j + 1) * P]
                dve.wait(tm_read[j])
                dve.mark(v.tensor_tensor(tm[0:64, :], b[0:64, 0:P], bs[0:64, j, :], ALU.add))
                freed[j] = dve.mark(v.tensor_tensor(tm[64:P, :], b[64:P, P:2 * P], bs[64:P, j, :], ALU.add))
                dve.settle()
                if j == 3:
                    self.fill(2)
                tm_read[j] = dve.mark(v.tensor_tensor(self.y[:, 8 + j, t * P:(t + 1) * P], tm, u[:, j, t * P:(t + 1) * P], ALU.mult))
        return dve.last()

    def merge(self, branches, n, gated):
        nc, v, dve, act = self.nc, self.nc.vector, self.dve, self.act
        dve.mark(v.memset(self.y[:, 0:KT, 0:n], 0.0))
        dve.settle()
        with self.roll(branches, tile=12, bank=8, act=8, dve=8) as i:
            rhs = gated(i)
            for pair in range(4):
                def terms(hi, lo):
                    for o in range(2):
                        nc.tensor.wait_ge(self.free.sem, self.free.value(o - 3))
                        b = self.G[(self.free.off + o) % 4]
                        for k in range(BT):
                            c = slice((o * BT + k) * P, (o * BT + k + 1) * P)
                            m = self.three(b[:, 0:n], hi[:, c], lo[:, c], rhs[0](k), rhs[1](k), k == 0, k == BT - 1)
                    return m
                self.tile(terms)
                for o in range(2):
                    e = self.free.off % 4
                    sel = self.M[e]
                    u = self.tile(self.feature_tile(n, bank=sel))
                    act.wait(u)
                    th = self.tmp[:, e % 2, 0:n]
                    act.eng.wait_ge(self.free.sem, self.free.value(-1))
                    a = act.mark(nc.scalar.activation(th, sel[:, 0:n], ACT.Tanh, scale=0.5))
                    dve.wait(a)
                    dve.mark(v.scalar_tensor_tensor(th, th, 1.0, self.G[e][:, 0:n], ALU.add, ALU.mult))
                    dve.settle()
                    acc = self.y[:, 2 * pair + o, 0:n]
                    self.release(v.tensor_tensor(acc, acc, th, ALU.add))
        return (self.free, self.free.value())


def short_conv(p, l, n):
    nc, v, dve, act = p.nc, p.nc.vector, p.dve, p.act
    sw, seqs = p.loads[f"hy_sw{l}"][0], n // TOK

    def evacuate(m, b, u):
        act.wait(u)
        o = p.arena[:, m, 0:n]
        a = act.mark(nc.scalar.activation(o, b[:, 0:n], ACT.Identity, bias=sw[:, m, 3:4], scale=sw[:, m, 1:2]))
        dve.wait(a)
        o3 = o.rearrange("p (s t) -> p s t", s=seqs)
        b3 = b[:, 0:n].rearrange("p (s t) -> p s t", s=seqs)
        dve.mark(v.scalar_tensor_tensor(o3[:, :, 1:TOK], b3[:, :, 0:TOK - 1], sw[:, m, 0:1], o3[:, :, 1:TOK], ALU.mult, ALU.add))
        dve.settle()
        return v.scalar_tensor_tensor(o3[:, :, 0:TOK - 1], b3[:, :, 1:TOK], sw[:, m, 2:3], o3[:, :, 0:TOK - 1], ALU.mult, ALU.add)
    return evacuate


def gate_tile(p, n, slot, yt, j):
    nc, v, dve, act = p.nc, p.nc.vector, p.dve, p.act
    b = p.bank()
    u = p.tile(p.feature_tile(n, bank=b))
    act.wait(u)
    th = p.tmp[:, 3 + j % 2, 0:n]
    act.eng.wait_ge(p.free.sem, p.free.value(-1))
    a = act.mark(nc.scalar.activation(th, b[:, 0:n], ACT.Tanh, scale=0.5))
    dve.wait(a)
    dve.mark(v.scalar_tensor_tensor(th, th, 1.0, b[:, 0:n], ALU.add, ALU.mult))
    dve.settle()
    d = dve.mark(v.tensor_tensor(th, th, yt, ALU.mult))
    act.wait(d)
    hi, lo = p.arena_r[:, slot, 0:n], p.arena_r[:, slot + 4, 0:n]
    a = act.mark(nc.scalar.activation(hi, th, ACT.Copy, scale=0.5))
    dve.wait(a)
    p.release(v.scalar_tensor_tensor(lo, th, 0.5, hi.bitcast(F32), ALU.mult, ALU.subtract))


def rotary_tables(p, mark):
    nc, v, dve, act = p.nc, p.nc.vector, p.dve, p.act
    p.need(dve, "pos", "inv_freq")
    dve.wait(mark)
    dve.settle()
    act.wait(mark)
    out = []
    for slot, shift in ((6, math.pi / 2), (7, 0.0)):
        arg, k, dst = p.tmp[:, 1, 0:TOK], p.tmp[:, 0, 0:TOK], p.x[:, slot, TOK:ALL]
        dve.mark(v.tensor_copy(k, p.loads["pos"][0]))
        dve.settle()
        dve.mark(v.tensor_scalar(arg, k, p.loads["inv_freq"][0], None, ALU.mult))
        dve.settle()
        m = p.sine(dst, arg, k, dve.last(), P, big=True, shift=shift)
        p.fill()
        dve.wait(m)
        out.append(dst)
    return out[0], out[1], m


def block1_layer(p, l, x_mark, sums, normed):
    nc, v, dve, act, pe = p.nc, p.nc.vector, p.dve, p.act, p.pe
    last = l == DEPTH - 1
    n = TOK if last else ALL
    mod_mark = p.modulation(l)
    neg_lam = p.lam(l)
    h_mark = p.pre_norm(mod_mark, sums, normed)

    K, Q, V = p.arena[:, 12:16, :], p.arena[:, 16:20, :], p.arena[:, 20:24, :]

    def copy_to(dst, width):
        def evacuate(j, b, u):
            act.wait(u)
            return nc.scalar.activation(dst[:, j, 0:width], b[:, 0:width], ACT.Copy)
        return evacuate
    p.fillers += p.feature_gemm(4, ALL, copy_to(K, ALL)) + p.feature_gemm(4, n, copy_to(Q, n))
    p.fillers += p.token_gemm(4, lambda j, b: nc.scalar.activation(V[:, j, :], b[:, :], ACT.Copy))
    nc.gpsimd.wait_ge(x_mark[0].sem, x_mark[1])
    p.fill()
    filter_marks = p.hyena_filter(l)
    if last:
        p.trig = rotary_tables(p, h_mark)
    p.fill(12)
    kqv = (p.free, p.free.value())
    p.need(dve, "rope")
    p.need(pe, "rope", "perm1", "ident")
    dve.wait(kqv)
    pe.wait(kqv, *filter_marks)
    act.wait(*filter_marks)

    p.need(act, f"hy_sw{l}")
    p.need(dve, f"hy_sw{l}")
    p.fillers += p.feature_gemm(12, n, short_conv(p, l, n))
    rope = p.loads["rope"][0]
    bank_read = [None] * 4
    for j in range(8):
        T = (K, Q)[j // 4]
        pe.wait(bank_read[j % 4])
        if j == 4:
            p.fill()
        m = bank_read[j % 4] = p.rope(T[:, j % 4, 0:TOK], TOK, rope[:, 0, :], rope[:, 1, :], p.loads["perm1"][0], kqv, p.M[j % 4], p.tmp[:, j % 2, :])
    parts = [(0, 0, ALL)] if last else [(0, 0, ALL), (TOK, TOK, TOK)]
    a = p.diff_attention(l, parts, K, Q, V, neg_lam, (m,))
    p.fill(12)
    hy_mark = (p.free, p.free.value())

    gu, vt = p.arena[:, 16:20, :], p.arena[:, 20:24, :]
    ntt = n // P

    def gelu_to(j, b, u):
        act.wait(u)
        return nc.scalar.activation(gu[:, j, 0:n], b[:, 0:n], ACT.Gelu)
    p.fillers += p.feature_gemm(4, n, gelu_to)
    p.fillers += p.token_gemm(ntt, lambda j, b: nc.scalar.activation(vt[:, j, :], b[:, :], ACT.Gelu))
    b_mark = p.hyena_conv(l, seqs=n // TOK, marks=(a, hy_mark) + filter_marks)
    nc.gpsimd.wait_ge(b_mark[0].sem, b_mark[1])
    p.load(f"ln_g{l}", p.arena[:, 8, :], eng=nc.gpsimd)
    p.load(f"ln_b{l}", p.arena[:, 9, :], eng=nc.gpsimd)
    p.load(f"gm_ws{l}", p.arena[:, 10:12, :].rearrange("p a (g q) -> p (a g) q", q=P), eng=nc.gpsimd)
    p.load(f"gm_bs{l}", p.arena[:, 12, :].rearrange("p (j q) -> p j q", q=P), eng=nc.gpsimd)
    p.fill(8)
    gm = (p.free, p.free.value())
    act.wait(b_mark)
    dve.wait(b_mark)

    p.fillers += [(lambda j=j: gate_tile(p, n, j, p.y[:, j, 0:n], j)) for j in range(4)]
    if not last:
        p.fillers += p.modulation_gemm(l + 1, p.arena[0:2, 13:15, :])
    c_mark = p.gmlp(l, ntt, (gm, b_mark))
    p.fill(4 + 24)
    for line in (pe, act, dve):
        line.wait(c_mark)

    arenaR = p.arena_r
    with p.roll(2, tile=4, bank=4, act=8, dve=8) as i:
        for j in range(4):
            gate_tile(p, n, i * 8 + (8 + j), p.y[:, i * 4 + (4 + j), 0:n], j)

    def gated(i):
        return (lambda k: arenaR[:, i * 8 + k, 0:n]), (lambda k: arenaR[:, i * 8 + (4 + k), 0:n])
    return gated, n


def block1_out(p, n, m_mark):
    nc, v, dve, act, pe = p.nc, p.nc.vector, p.dve, p.act, p.pe
    act.wait(m_mark)
    dve.wait(m_mark)
    pe.wait(m_mark)
    p.ready = [p.halves(p.hhi[:, k, 0:n], p.hlo[:, k, 0:n], p.y[:, k, 0:n], 0.5) for k in range(KT)]
    sums = SquareSum(p, n)
    for o in range(KT):
        b = p.bank()
        u = p.tile(p.feature_tile(n, bank=b))
        act.wait(u)
        for s in range(n // TOK):
            c = slice(s * TOK, (s + 1) * TOK)
            act.mark(nc.scalar.activation(p.arena[:, o, c], b[:, c], ACT.Identity, bias=p.zero, scale=p.mod[:, 16 + o, s:s + 1]))
        sums.add(b[:, 0:n], mark=p.release)
    m = sums.finish()
    dve.wait(m, act.last())
    dve.settle()
    sums = SquareSum(p, n)
    act.wait(m)
    pe.wait(m)
    for k in range(KT):
        dve.mark(v.tensor_tensor(p.arena[:, k, 0:n], p.arena[:, k, 0:n], p.tmp[:, 2, 0:n], ALU.mult))
        dve.settle()
        sums.add(p.x[:, k, 0:n], dve.mark(v.tensor_tensor(p.x[:, k, 0:n], p.x[:, k, 0:n], p.arena[:, k, 0:n], ALU.add)))
    return dve.last(), sums


def second_norm(p, gain, sums):
    v = p.nc.vector
    p.need(p.dve, gain)
    g = p.loads[gain][0]
    m = sums.finish()
    return p.make_h(TOK, lambda k, t: p.dve.mark(v.scalar_tensor_tensor(t, p.x[:, k, 0:TOK], g[:, k:k + 1], p.tmp[:, 2, 0:TOK], ALU.mult, ALU.mult)), None, m)


class Compress:

    def __init__(self, p, z, which, X, xh, xl):
        self.p, self.z, self.which, self.X, self.xh, self.xl = p, z, which, X, xh, xl

    def prepare(self, *waits):
        p = self.p
        nc, v, dve, act = p.nc, p.nc.vector, p.dve, p.act
        pe_t = p.loads[f"pe_{self.which}"][0]
        p.need(dve, f"pe_{self.which}")
        act.wait(*waits)
        pair = p.tmp[:, 2, 0:2 * P].rearrange("p (g t) -> p g t", g=2)
        for g in range(2):
            for par in range(2):
                a = act.mark(nc.scalar.activation(pair[par * 64:par * 64 + 64, g, :], self.z[g * 64:g * 64 + 64, par::2], ACT.Copy))
        dve.wait(a, *waits)
        for g in range(2):
            for half in range(2):
                jj = slice(8 * half, 8 * half + 8)
                blocks = pair[:, g, 8 * half:8 * half + 8 * NCMP].rearrange("p (n b) -> p b n", b=8)
                dve.mark(v.tensor_tensor(self.X[:, jj, g * NCMP:(g + 1) * NCMP], blocks, pe_t[:, jj].unsqueeze(2).broadcast_to([P, 8, NCMP]), ALU.add))
        dve.settle()
        self.ready = p.halves(self.xh[:], self.xl[:], self.X, 1.0, (dve.last(),))

    def products(self):
        p = self.p
        b = p.bank()
        p.pe.wait(self.ready)
        for g in range(4):
            def products(hi, lo):
                for q in range(4):
                    jj, c = 4 * g + q, slice(q * 256, (q + 1) * 256)
                    r = p.three(b[0:2 * NCMP, 0:256], self.xh[:, jj, :], self.xl[:, jj, :], hi[:, c], lo[:, c], jj == 0, jj == 15)
                return r
            u = p.tile(products)
        self.used = u
        self.rows = p.tmp[0:2 * NCMP, 3, 0:256]
        p.act.wait(u)
        linear = p.tmp[0:2 * NCMP, 3, 256:512]
        p.act.mark(p.nc.scalar.activation(self.rows, b[0:2 * NCMP, 0:256], ACT.Tanh, scale=0.5))
        a = p.release(p.nc.scalar.activation(linear, b[0:2 * NCMP, 0:256], ACT.Copy))
        p.dve.wait(a, p.act.last())
        self.silu = p.dve.mark(p.nc.vector.scalar_tensor_tensor(self.rows, self.rows, 1.0, linear, ALU.add, ALU.mult))

    def turn(self, hid):
        p = self.p
        b = p.bank()
        p.pe.wait(self.silu)
        for o in range(2):
            t = p.nc.tensor.transpose(b[:, o * 2 * NCMP:(o + 1) * 2 * NCMP], self.rows[:, o * P:(o + 1) * P], p.ident[0:2 * NCMP, 0:2 * NCMP])
        self.turned = p.pe.mark(t)
        p.act.wait(self.turned)
        return p.release(p.nc.scalar.activation(hid, b[:, 0:4 * NCMP].rearrange("p (o n) -> p o n", o=2), ACT.Copy, scale=0.5))


class HeadTiles:
    SLOTS = [0, 1, 2, 3, 6, 7] + list(range(8, 16))

    def __init__(self, p, Z, cos, sin):
        self.p, self.Z, self.cos, self.sin = p, Z, cos, sin
        self.late, self.n, self.read = None, 0, [None, None]
        self.sq = p.tmp[:, 0, :].rearrange("p (b t) -> p b t", b=2)
        self.rot = p.tmp[:, 1, :].rearrange("p (b t) -> p b t", b=2)
        self.done = {}

    def tile(self):
        p, n = self.p, self.n
        act, L = p.nc.scalar, p.loads
        b = p.bank()
        u = p.tile(p.feature_tile(TOK, bank=b))
        z = self.Z[:, self.SLOTS[n], :]
        p.act.wait(u, self.read[n % 2])
        a = p.act.mark(act.activation(z, b[:, 0:TOK], ACT.Identity, bias=p.zero, scale=L["head_gain"][0][:, n:n + 1]))
        r = p.release(act.activation(self.sq[:, n % 2, :], b[:, 0:TOK], ACT.Square))
        self.flush()
        self.late = (n, z, a, r)
        self.n += 1

    def flush(self):
        if not self.late:
            return
        p, (n, z, a, r) = self.p, self.late
        nc, v, L = p.nc, p.nc.vector, p.loads
        self.late = None
        turned = p.M[2 + n % 2]
        p.pe.wait(a, r, self.done.get(n - 2))
        self.read[n % 2] = p.pe.mark(nc.tensor.matmul(p.M[0][0:32, 0:TOK], L["head_sum"][0][:, n, :], self.sq[:, n % 2, :], start=(n == 0), stop=(n == 13)))
        q = p.pe.mark(nc.tensor.matmul(turned[:, 0:TOK], L["perm2"][0], z, start=True, stop=True))
        p.dve.wait(q)
        p.dve.mark(v.tensor_tensor(self.rot[:, n % 2, :], turned[:, 0:TOK], self.sin, ALU.mult))
        p.dve.mark(v.tensor_tensor(z, z, self.cos, ALU.mult))
        p.dve.settle()
        self.done[n] = p.dve.mark(v.tensor_tensor(z, z, self.rot[:, n % 2, :], ALU.add))

    def spread(self, hr, start, stop):
        p = self.p
        for m in range(start, stop):
            n = (4, 5, 10, 11, 12, 13)[m]
            z = self.Z[:, self.SLOTS[n], :]
            s = p.M[2 + m % 2]
            p.pe.wait(self.done[n - 2] if m < 2 else self.done[("k", m - 2)])
            q = p.pe.mark(p.nc.tensor.matmul(s[:, 0:TOK], p.loads["head_spread"][0][:, n, :], hr, start=True, stop=True))
            p.dve.wait(q)
            p.dve.settle()
            self.done[("k", m)] = p.dve.mark(p.nc.vector.tensor_tensor(z, z, s[:, 0:TOK], ALU.mult))
            p.fill()


class Attention:

    def __init__(self, p, Z, kcT, vc, VM, VS, factor, gates, cmp_add, YN, YM, ident_r, tri_r):
        self.p, self.Z, self.kcT, self.vc, self.VM, self.VS = p, Z, kcT, vc, VM, VS
        self.factor, self.gates, self.cmp_add, self.YN, self.YM = factor, gates, cmp_add, YN, YM
        self.ident_r, self.tri_r = ident_r, tri_r
        self.steps = [(i, j, ab) for i in range(2) for j in range(4) for ab in range(2)]
        a = p.arena
        self.E = [a[:, 12 + ab, :].rearrange("p (b t) -> p b t", t=TOK) for ab in range(2)]
        self.E2 = a[:, 14, :].rearrange("p (b t) -> p b t", t=TOK)
        self.PT = [a[:, 15 + ab, :].rearrange("p (b k q) -> p b k q", b=2, k=2) for ab in range(2)]
        self.PT2 = a[:, 17, :].rearrange("p (b k q) -> p b k q", b=2, k=2)
        self.PTc = p.y[0:NCMP, 11, 0:2 * P].rearrange("p (b q) -> p b q", b=2)
        self.Ec = p.y[:, 11, 2 * P:2 * P + 32].rearrange("p (b n) -> p b n", b=2)
        self.diag = [p.x[:, 0:3, TOK + ab * P:TOK + ab * P + P] for ab in range(2)]
        self.stat = [p.stat[:, 12 * ab:12 * ab + 12] for ab in range(2)]
        self.ready = {}
        self.scored, self.exped, self.scaled, self.turned, self.copied, self.out, self.freed = ({} for _ in range(7))

    def scores(self, s):
        i, j, ab = self.steps[s]
        p, mm = self.p, self.p.nc.tensor.matmul
        A, B = p.M[2 * ab], p.M[2 * ab + 1]
        nk = P * (i + 1)
        r, q_ = slice(ab * 64, ab * 64 + 64), slice(i * P, (i + 1) * P)
        p.pe.wait(self.freed.get(s - 2))
        for kind, (qt, kt) in enumerate(((j, 6), (j, 7), (8 + j, 12 + j))):
            bank, c = (A, kind * nk) if kind < 2 else (B, 0)
            mm(bank[:, c:c + nk], self.Z[r, qt, q_], self.Z[r, kt, 0:nk], start=True, stop=False)
            mm(bank[:, c + i * P:c + nk], self.ident_r, self.tri_r, start=False, stop=True)
        mm(B[:, TOK:TOK + NCMP], self.Z[r, j, q_], self.kcT[r, 0, 0:NCMP], start=True, stop=False)
        self.scored[s] = p.pe.mark(mm(B[:, TOK:TOK + NCMP], p.ident, self.cmp_add[:, i, :], start=False, stop=True))

    def maxima(self, s):
        i, j, ab = self.steps[s]
        p, v, dve = self.p, self.p.nc.vector, self.p.dve
        A, B, st, nk = p.M[2 * ab], p.M[2 * ab + 1], self.stat[ab], P * (i + 1)
        dve.wait(self.scored[s])
        dve.settle()
        dve.mark(v.tensor_reduce(st[:, 0:2], A[:, 0:2 * nk].rearrange("p (b n) -> p b n", b=2), AXX, ALU.max, negate=True))
        dve.mark(v.tensor_reduce(st[:, 2:3], B[:, 0:nk], AXX, ALU.max, negate=True))
        dve.mark(v.tensor_reduce(st[:, 3:4], B[:, TOK:TOK + NCMP], AXX, ALU.max, negate=True))
        dve.settle()
        self.scored[s] = dve.mark(v.tensor_tensor(st[:, 0:4], st[:, 0:4], self.factor[:, i, j, ab, :], ALU.mult))

    def exponentials(self, s):
        i, j, ab = self.steps[s]
        p, act = self.p, self.p.act
        A, B, st, nk = p.M[2 * ab], p.M[2 * ab + 1], self.stat[ab], P * (i + 1)
        act.wait(self.scored[s], self.turned.get(s - 2))
        for c, (dst, src) in enumerate(((self.E[ab][:, 0, 0:nk], A[:, 0:nk]), (self.E[ab][:, 1, 0:nk], A[:, nk:2 * nk]),
                                        (self.E2[:, ab, 0:nk], B[:, 0:nk]), (self.Ec[:, ab, 0:NCMP], B[:, TOK:TOK + NCMP]))):
            self.exped[s] = act.mark(p.nc.scalar.activation(dst, src, ACT.Exp, bias=st[:, c:c + 1], scale=self.factor[:, i, j, ab, c:c + 1], accum_out=st[:, 4 + c:5 + c]))

    def weights(self, s):
        i, j, ab = self.steps[s]
        p, v, dve, st = self.p, self.p.nc.vector, self.p.dve, self.stat[ab]
        dve.wait(self.exped[s])
        dve.mark(v.tensor_scalar(st[:, 4:8], st[:, 4:8], 1e-30, None, ALU.max))
        dve.settle()
        dve.mark(v.reciprocal(st[:, 8:12], st[:, 4:8]))
        dve.settle()
        dve.mark(v.tensor_tensor(st[:, 8:12], st[:, 8:12], self.gates[:, i, j, ab, :], ALU.mult))
        dve.settle()
        dve.mark(v.tensor_tensor(self.diag[ab], p.ident.unsqueeze(1).broadcast_to([P, 3, P]), st[:, 8:11].unsqueeze(2).broadcast_to([P, 3, P]), ALU.mult))
        self.scaled[s] = dve.mark(v.tensor_scalar(self.Ec[:, ab, 0:NCMP], self.Ec[:, ab, 0:NCMP], st[:, 11:12], None, ALU.mult))

    def turn(self, s):
        i, j, ab = self.steps[s]
        p, mm = self.p, self.p.nc.tensor.matmul
        A, B = p.M[2 * ab], p.M[2 * ab + 1]
        p.pe.wait(self.scaled[s])
        for kind, (bank, src) in enumerate(((A, self.E[ab][:, 0, :]), (A, self.E[ab][:, 1, :]), (B, self.E2[:, ab, :]))):
            for kt in range(i + 1):
                c = (kind % 2) * TOK + kt * P
                mm(bank[:, c:c + P], src[:, kt * P:(kt + 1) * P], self.diag[ab][:, kind, :], start=True, stop=True)
        self.turned[s] = p.pe.mark(p.nc.tensor.transpose(B[0:NCMP, TOK:TOK + P], self.Ec[:, ab, 0:NCMP], p.ident))
        p.act.wait(self.turned[s], self.out.get(s - 2))
        act = p.nc.scalar.activation
        n = i + 1
        p.act.mark(act(self.PT[ab][:, :, 0:n, :], A[:, :].rearrange("p (b k q) -> p b k q", b=2, k=2)[:, :, 0:n, :], ACT.Copy))
        p.act.mark(act(self.PT2[:, ab, 0:n, :], B[:, 0:TOK].rearrange("p (k q) -> p k q", k=2)[:, 0:n, :], ACT.Copy))
        self.copied[s] = p.act.mark(act(self.PTc[:, ab, :], B[0:NCMP, TOK:TOK + P], ACT.Copy))

    def values(self, s):
        i, j, ab = self.steps[s]
        p, mm = self.p, self.p.nc.tensor.matmul
        A, B, o, q_ = p.M[2 * ab], p.M[2 * ab + 1], slice(ab * 64, ab * 64 + 64), slice(i * P, (i + 1) * P)
        hd = (2 * j + ab) * 64
        p.pe.wait(self.copied[s])
        mm(A[o, 0:P], self.vc[0:NCMP, o], self.PTc[:, ab, :], start=True, stop=False)
        for kind in range(2):
            for kt in range(i + 1):
                mm(A[o, 0:P], self.VS[:, kt, kind * P + ab * 64:kind * P + ab * 64 + 64], self.PT[ab][:, kind, kt, :], start=False, stop=(kind == 1 and kt == i))
        for kt in range(i + 1):
            m = mm(B[o, 0:P], self.VM[:, kt, hd:hd + 64], self.PT2[:, ab, kt, :], start=(kt == 0), stop=(kt == i))
        self.out[s] = p.pe.mark(m)
        p.dve.wait(self.out[s])
        p.dve.mark(p.nc.vector.tensor_copy(self.YN[o, j, q_], A[o, 0:P]))
        self.freed[s] = p.dve.mark(p.nc.vector.tensor_copy(self.YM[o, j, q_], B[o, 0:P]))
        if i and ab:
            p.dve.settle()
            self.ready[j] = [p.halves(self.half(p.hhi, br, j), self.half(p.hlo, br, j), Y[:, j, :], 1.0, (self.freed[s],)) for br, Y in enumerate((self.YN, self.YM))]

    @staticmethod
    def half(h, br, k):
        return h[:, br * BT + k, TOK:ALL]

    def run(self):
        n = len(self.steps)
        for s in range(n + 1):
            if s < n:
                self.scores(s)
                self.p.split_hi()
            if s:
                self.weights(s - 1)
                self.turn(s - 1)
            if s < n:
                self.maxima(s)
                self.p.split_lo()
                self.exponentials(s)
            self.p.fill()
            if s:
                self.values(s - 1)


def block2(p, x_mark, sums):
    nc, v, dve, act, pe = p.nc, p.nc.vector, p.dve, p.act, p.pe
    pool = nc.gpsimd
    pool.wait_ge(x_mark[0].sem, x_mark[1])
    p.load("head_spread", p.shared[0:32, 0:1792].rearrange("p (a n) -> p a n", a=14), eng=pool)
    p.load("ck_w2", p.shared[:, 1792:1920].rearrange("p (a n) -> p a n", a=2), eng=pool)
    p.load("cv_w2", p.shared[:, 1920:2048].rearrange("p (a n) -> p a n", a=2), eng=pool)
    p.load("ple", p.y[:, 8, :], eng=pool)
    L = {k: m[0] for k, m in p.loads.items()}

    p.need(act, "head_gain", "causal")
    p.need(dve, "head_gain", "cmp_any")
    p.need(pe, "perm2", "head_sum", "head_spread", "block_mean", "ck_w2", "cv_w2", "cmp_add")
    cos, sin, trig_mark = p.trig
    dve.wait(x_mark, trig_mark)
    act.wait(x_mark)
    h = second_norm(p, "g_mix", sums)
    ident_r, tri_r = p.y_r[:, 9, 0:P], p.y_r[:, 9, P:2 * P]
    act.mark(nc.scalar.activation(ident_r, p.ident, ACT.Copy))
    act.mark(nc.scalar.activation(tri_r, L["causal"], ACT.Copy))
    Z = p.arena[:, 0:8, :].rearrange("p a (b t) -> p (a b) t", t=TOK)
    for z in (4, 5):
        b = p.bank()
        u = p.tile(p.feature_tile(TOK, bank=b))
        act.wait(u)
        p.release(nc.scalar.activation(Z[:, z, :], b[:, 0:TOK], ACT.Copy))
        z_mark = (p.free, p.free.value())
    X = p.y[:, 10, 0:32 * NCMP].rearrange("p (a n) -> p a n", a=16)
    xh, xl = p.sb("cmp_xh", [P, 16, 2 * NCMP], F32R), p.sb("cmp_xl", [P, 16, 2 * NCMP], F32R)
    hid = p.sb("cmp_hid", [P, 2, 2 * NCMP])[:]
    heads = HeadTiles(p, Z, cos, sin)
    ck, cv = Compress(p, Z[:, 4, :], "k", X, xh, xl), Compress(p, Z[:, 5, :], "v", X, xh, xl)
    b = p.M[1]
    ck.prepare(z_mark)
    for _ in range(3):
        heads.tile()
    ck.products()
    cv.prepare(ck.used)
    for _ in range(2):
        heads.tile()
    m = ck.turn(hid)
    heads.tile()
    pe.wait(m)
    kcT = p.sb("kc_t", [P, 2, 16])[:]
    kc, kc_r = kcT[:, 0, 0:NCMP], kcT[:, 1, 0:NCMP]
    for g in range(2):
        for o in range(2):
            q = nc.tensor.matmul(b[g * 64:g * 64 + 64, 0:NCMP], L["ck_w2"][:, o, :], hid[:, o, g * NCMP:(g + 1) * NCMP], start=(o == 0), stop=(o == 1))
        q = pe.mark(q)
    act.wait(q)
    act.mark(nc.scalar.activation(kc, b[:, 0:NCMP], ACT.Copy))
    kc_sq = act.mark(nc.scalar.activation(kc_r, b[:, 0:NCMP], ACT.Square))
    cv.products()
    for _ in range(2):
        heads.tile()
    pe.wait(kc_sq)
    kc_sum = pe.mark(nc.tensor.matmul(b[:, 0:NCMP], L["block_mean"], kc_r, start=True, stop=True))
    m = cv.turn(hid)
    heads.tile()
    pe.wait(m)
    vc = p.sb("vc", [16, P])[:]
    for g in range(2):
        for o in range(2):
            q = nc.tensor.matmul(b[0:NCMP, P + g * 64:P + g * 64 + 64], hid[:, o, g * NCMP:(g + 1) * NCMP], L["cv_w2"][:, o, :], start=(o == 0), stop=(o == 1))
    q = pe.mark(q)
    act.wait(q)
    vc_mark = act.mark(nc.scalar.activation(vc[0:NCMP, :], b[0:NCMP, P:2 * P], ACT.Copy))
    for _ in range(5):
        heads.tile()
    heads.flush()

    VM, VS = p.arena[:, 8:10, :], p.arena[:, 10:12, :]
    gate = p.sb("gate2", [P, 2, 24])[:]

    def values_gates(j, b):
        act.mark(nc.scalar.activation(VS[:, j, 0:256], b[:, 0:256], ACT.Copy))
        return nc.scalar.activation(gate[:, j, :], b[:, 256:280], ACT.Tanh, scale=0.5)
    p.fillers += p.token_gemm(2, lambda j, b: nc.scalar.activation(VM[:, j, :], b[:, :], ACT.Copy))
    p.fillers += p.token_gemm(2, values_gates, 280)
    sel = [p.arena[:, 18 + n // 2, (n % 2) * TOK:(n % 2) * TOK + TOK] for n in range(12)] + [p.y[:, n, TOK:ALL] for n in range(4, 8)]

    def branch_gate(n, b, u):
        act.wait(u)
        return nc.scalar.activation(sel[n], b[:, 0:TOK], ACT.Tanh, scale=0.5)
    p.fillers += p.feature_gemm(16, TOK, branch_gate)
    hr = p.tmp[0:32, 4, 0:TOK]
    act.wait(heads.read[1], kc_sum)
    act.mark(nc.scalar.activation(hr, p.M[0][0:32, 0:TOK], ACT.Sqrt, bias=p.eps[0:32, :]))
    a = act.mark(nc.scalar.activation(kc_r, b[:, 0:NCMP], ACT.Sqrt, bias=p.eps))
    dve.wait(a)
    m = dve.mark(v.reciprocal(hr, hr))
    dve.mark(v.reciprocal(kc_r, kc_r))
    dve.settle()
    kc_done = dve.mark(v.scalar_tensor_tensor(kc, kc, L["head_gain"][:, 14:15], kc_r, ALU.mult, ALU.mult))
    p.fill()
    pe.wait(m, vc_mark)
    heads.spread(hr, 0, 3)
    p.rope(kc, NCMP, cos[:, 31::16], sin[:, 31::16], L["perm2"], kc_done, p.M[0], p.tmp[:, 3, :])
    for i in range(2):
        t = pe.mark(nc.tensor.transpose(b[:, 2 * P + 32 * i:2 * P + 32 * i + 32], hr[:, i * P:(i + 1) * P], p.ident[0:32, 0:32]))
    p.fill()
    factor = p.x[:, 3, TOK:TOK + 64].rearrange("p (i j a c) -> p i j a c", i=2, j=4, a=2)
    gates = p.x[:, 3, TOK + 64:TOK + 128].rearrange("p (i j a c) -> p i j a c", i=2, j=4, a=2)
    dve.wait(t)
    for i in range(2):
        for c, row in ((0, 0), (1, 0), (2, 12), (3, 0)):
            rows = b[:, 2 * P + 32 * i + row:2 * P + 32 * i + row + 8].rearrange("p (j a) -> p j a", a=2)
            f = dve.mark(v.tensor_scalar(factor[:, i, :, :, c], rows, 0.125, None, ALU.mult))
    heads.spread(hr, 3, 6)
    g_mark = (p.free, p.free.value())
    dve.wait(g_mark)
    dve.mark(v.tensor_scalar(gate, gate, 1.0, 0.5, ALU.add, ALU.mult))
    dve.mark(v.memset(gates[:, :, :, :, 2], 1.0))
    dve.settle()
    by_head = gate.rearrange("p i (a j k) -> p i j a k", a=2, j=4)
    for i in range(2):
        for c, k in ((0, 1), (1, 2)):
            dve.mark(v.tensor_copy(gates[:, i, :, :, c], by_head[:, i, :, :, k]))
        dve.mark(v.tensor_scalar(gates[:, i, :, :, 3], by_head[:, i, :, :, 0], L["cmp_any"][:, i:i + 1], None, ALU.mult))
    qk = dve.last()
    pe.wait(qk)
    act.wait(qk)
    YN = p.y[:, 0:2, :].rearrange("p a (b t) -> p (a b) t", t=TOK)
    YM = p.y[:, 2:4, :].rearrange("p a (b t) -> p (a b) t", t=TOK)
    att = Attention(p, Z, kcT, vc, VM, VS, factor, gates, L["cmp_add"], YN, YM, ident_r, tri_r)
    att.run()
    assert not p.fillers

    last = att.freed[15]
    act.wait(last)
    dve.settle()
    R = p.arena_r
    dve.wait((p.free, p.free.value()))
    acc = p.arena[:, 0:8, TOK:ALL]
    ready = []
    for pair in range(4):
        for br in range(2):
            banks = [p.bank()]
            p.nc.tensor.wait_ge(p.free.sem, p.free.value(-2))
            banks.append(p.G[(p.free.off + 1) % 4])

            def terms(hi, lo):
                for o in range(2):
                    for k in range(BT):
                        if pair == 0:
                            pe.wait(att.ready[k][br])
                        c = slice((o * BT + k) * P, (o * BT + k + 1) * P)
                        m = p.three(banks[o][:, 0:TOK], hi[:, c], lo[:, c], att.half(p.hhi, br, k), att.half(p.hlo, br, k), k == 0, k == BT - 1)
                return m
            u = p.tile(terms)
            dve.wait(u)
            for o in range(2):
                n = 2 * pair + o
                dst = p.tmp[:, o, 0:TOK] if br else acc[:, n, :]
                p.release(v.scalar_tensor_tensor(dst, sel[br * 8 + n], 1.0, banks[o][:, 0:TOK], ALU.add, ALU.mult))
        dve.wait((p.free, p.free.value()))
        for o in range(2):
            n = 2 * pair + o
            d = dve.mark(v.tensor_tensor(acc[:, n, :], acc[:, n, :], p.tmp[:, o, 0:TOK], ALU.add))
            dve.settle()
            ready.append(p.halves(p.hhi[:, n, 0:TOK], p.hlo[:, n, 0:TOK], acc[:, n, :], 0.5, (d,)))
    p.ready = ready
    sums = SquareSum(p, TOK)
    for o in range(KT):
        b = p.bank()
        u = p.tile(p.feature_tile(TOK, bank=b))
        dve.wait(u)
        sums.add(p.x[:, o, 0:TOK], p.release(v.tensor_tensor(p.x[:, o, 0:TOK], p.x[:, o, 0:TOK], b[:, 0:TOK], ALU.add)))

    h = second_norm(p, "g_ffn", sums)
    ah = R[:, 0:11, :].rearrange("p a (b t) -> p (a b) t", t=TOK)
    al = R[:, 11:22, :].rearrange("p a (b t) -> p (a b) t", t=TOK)

    def ffn_pair(f):
        e = p.free.off % 4
        up, gt = p.bank(), p.M[e]
        ug = p.tile(p.feature_tile(TOK, bank=gt))
        uu = p.tile(p.feature_tile(TOK, bank=up))
        act.wait(ug)
        act.eng.wait_ge(p.free.sem, p.free.value(-1))
        th = p.tmp[:, e % 2, 0:TOK]
        a = act.mark(nc.scalar.activation(th, gt[:, 0:TOK], ACT.Tanh, scale=0.5))
        dve.wait(a)
        dve.mark(v.scalar_tensor_tensor(th, th, 1.0, gt[:, 0:TOK], ALU.add, ALU.mult))
        dve.wait(uu)
        dve.settle()
        d = dve.mark(v.tensor_tensor(th, th, up[:, 0:TOK], ALU.mult))
        act.wait(d)
        a = act.mark(nc.scalar.activation(ah[:, f, :], th, ACT.Copy, scale=0.5))
        dve.wait(a)
        p.release(v.scalar_tensor_tensor(al[:, f, :], th, 0.5, ah[:, f, :].bitcast(F32), ALU.mult, ALU.subtract))
    for f in range(2):
        ffn_pair(f)
    pe.wait(h)
    with p.roll(5, tile=8, bank=4, act=8, dve=8) as i:
        for j in range(4):
            ffn_pair(i * 4 + (2 + j))
    last = (p.free, p.free.value())
    pe.wait(last)
    out_banks = p.G + p.M

    def down(k, first, final):
        def products(hi, lo):
            for o in range(KT):
                c = slice(o * P, (o + 1) * P)
                m = p.three(out_banks[o][:, 0:TOK], hi[:, c], lo[:, c], ah[:, k, :], al[:, k, :], first, final)
            return m
        return p.tile(products)
    for k in range(2):
        down(k, k == 0, False)
    with p.roll(4, tile=4) as i:
        for j in range(4):
            down(i * 4 + (2 + j), False, False)
    for k in range(18, FT):
        u = down(k, False, k == FT - 1)
    dve.wait(u)
    act.wait((p.free, p.free.value()))
    sums = SquareSum(p, TOK)
    for o in (4, 0, 1, 2, 3, 5, 6, 7):
        d = dve.mark(v.tensor_tensor(p.x[:, o, 0:TOK], p.x[:, o, 0:TOK], out_banks[o][:, 0:TOK], ALU.add))
        sums.add(p.x[:, o, 0:TOK], d)
    pe.wait(d)

    p.need(act, "ple")
    p.need(dve, "ple")
    ph, pl = R[:, 22, :], R[:, 23, :]
    m = p.halves(ph, pl, L["ple"])
    h = second_norm(p, "g_ple", sums)
    pe.wait(m)
    for o in range(KT):
        b = p.bank()
        u = p.tile(p.feature_tile(TOK, bank=b))
        act.wait(u)
        p.release(nc.scalar.activation(p.y[:, o, 0:TOK], b[:, 0:TOK], ACT.Tanh, scale=0.5))
    pe.wait(h)
    dve.wait((p.free, p.free.value()))
    outs = []
    for g in range(2):
        def products(hi, lo):
            for o in range(4):
                for k in range(2):
                    c = slice((o * 2 + k) * P, (o * 2 + k + 1) * P)
                    t = slice(k * TOK, (k + 1) * TOK)
                    m = p.three(p.M[o][:, 0:TOK], hi[:, c], lo[:, c], ph[:, t], pl[:, t], k == 0, k == 1)
            return m
        u = p.tile(products)
        dve.wait(u)
        for o in range(4):
            k = 4 * g + o
            yk, xk = p.y[:, k, 0:TOK], p.x[:, k, 0:TOK]
            d = dve.mark(v.scalar_tensor_tensor(yk, yk, 1.0, p.M[o][:, 0:TOK], ALU.add, ALU.mult))
            dve.settle()
            outs.append(dve.mark(v.scalar_tensor_tensor(xk, yk, 0.5, xk, ALU.mult, ALU.add)))
        pe.wait(d)
        nc.sync.wait_ge(outs[-1][0].sem, outs[-1][1])
        nc.sync.dma_start(p.out[:, 4 * g:4 * g + 4, :], p.x[:, 4 * g:4 * g + 4, 0:TOK]).then_inc(p.stored, 16)
    nc.sync.wait_ge(p.stored, 32)


SMALL = ["norm_pre0", "norm_post0", "ada_b0", "norm_pre1", "norm_post1", "ada_b1", "lambda",
         "rope", "perm1", "subln0", "subln1", "hy_z"] + \
    [f"hy_{n}{l}" for l in range(2) for n in ("w1", "b1", "w2", "b2", "freq", "sw", "bias")] + \
    ["inv_freq", "head_gain", "causal", "cmp_add", "cmp_any", "perm2", "head_sum",
     "block_mean", "pe_k", "pe_v", "g_mix", "g_ffn", "g_ple"]


def program(nc, ins, out):
    with ExitStack() as ctx:
        p = Program(nc, ctx, ins, out)
        p.stored = p.sem("stored")
        p.load("cond")
        p.load("ident")
        p.stream()
        for s in range(2):
            n = ("x", "ctx")[s]
            p.load(n, p.x[:, :, s * TOK:(s + 1) * TOK])
        p.shared = p.sb("shared", [P, 2048])
        p.load("dft", p.shared[:, 0:1024].rearrange("p (a n) -> p a n", a=2))
        p.load("idft", p.shared[:, 1024:2048].rearrange("p (a n) -> p a n", a=4))
        p.condition()
        for _ in range(AHEAD):
            p.split()
        p.load("pos", dt=I32)
        for n in SMALL:
            p.load(n, eng=nc.gpsimd)
        p.constants()
        p.fillers += p.modulation_gemm(0, p.arena[0:2, 13:15, :])
        p.fill(8)
        for line in (p.act, p.dve, p.pe):
            p.need(line, "x", "ctx")
        sums = SquareSum(p, ALL)
        for k in range(KT):
            sums.add(p.x[:, k, :])
            p.fill()
        p.dve.wait(sums.finish())
        p.dve.settle()
        for k in range(KT):
            p.dve.mark(nc.vector.tensor_tensor(p.arena[:, k, :], p.x[:, k, :], p.tmp[:, 2, :], ALU.mult))
            p.fill()
        x_mark = p.const
        for l in range(DEPTH):
            gated, n = block1_layer(p, l, x_mark, sums, p.arena[:, 0:KT, :] if l == 0 else None)
            m = p.merge(3, n, gated)
            x_mark, sums = block1_out(p, n, m)
            for line in (p.act, p.dve):
                line.wait(x_mark)
        block2(p, x_mark, sums)
        assert p.used.off == TILES, (p.used.off, TILES)


def _columns(w):
    k, n = w.shape
    return w.reshape(k // P, P, n // P, P).transpose(2, 1, 0, 3).reshape(n // P, P, k)


def _rows(w):
    return w.reshape(4, 2, P, 512).transpose(0, 2, 1, 3).reshape(4, P, 1024)


def _feat(a):
    t, f = a.shape
    return a.T.reshape(f // P, P, t).transpose(1, 0, 2)


def _vec(a):
    return a.reshape(-1, P).T


def _layout(i):
    tiles = []

    def merged(ws, gates):
        for w, g in zip(ws, gates):
            b, s = _columns(w), _columns(g)
            for pair in range(4):
                tiles.append(np.concatenate([b[2 * pair], b[2 * pair + 1]], axis=1)[None])
                tiles.append(s[2 * pair:2 * pair + 2])

    def ada(l):
        tiles.append(i["ada_w"][l].reshape(KT, P, 3, 1024).transpose(2, 0, 1, 3).reshape(24, P, 1024))
    for l in range(DEPTH):
        w = i["w_in"][l]
        if l == 0:
            ada(0)
        tiles.append(_columns(w[:, 0:512]))
        tiles.append(_columns(w[:, 1024:1536]))
        tiles.append(_rows(w[:, 512:1024]))
        tiles.append(_columns(w[:, 2048:3584]))
        tiles.append(_columns(w[:, 4096:4608]))
        tiles.append(_rows(w[:, 4608:5120]))
        tiles.append(_columns(w[:, 1536:2048]))
        if l == 0:
            ada(1)
        for g in (3584, 5120):
            tiles.append(_columns(w[:, g:g + 512]))
        merged(list(i["w_branch"][l]), [w[:, 5632 + b * D:5632 + (b + 1) * D] for b in range(3)])
        tiles.append(_columns(i["w_out"][l]))
    w = i["w_in_2"][0]
    order = [h for j in range(4) for h in (j, 4 + j)]
    heads = np.concatenate([np.arange(h * 64, h * 64 + 64) for h in order])
    for c in (512, 640):
        tiles.append(_columns(w[:, c:c + P]))
    qk = np.concatenate([_columns(w[:, heads])] + [_columns(w[:, a:b]) for a, b in ((768, 896), (1024, 1152), (1304, 1816), (1816, 2328))])
    ck, cv = (i[n][0].reshape(4, 4, P, 256).transpose(0, 2, 1, 3).reshape(4, P, 1024) for n in ("nsa_ck_w1_2", "nsa_cv_w1_2"))
    tiles += [qk[0:3], ck, qk[3:6], cv, qk[6:14]]
    tiles.append(_rows(w[:, 2328:2840]))
    vsg = np.zeros((D, 512), w.dtype)
    vsg[:, 0:128], vsg[:, 128:256], vsg[:, 256:280] = w[:, 896:1024], w[:, 1152:1280], w[:, 1280:1304]
    tiles.append(_rows(vsg))
    tiles.append(_columns(w[:, 2840:4888]))
    ups = [_columns(u).reshape(4, 2, P, BR).transpose(0, 2, 1, 3).reshape(4, P, 1024) for u in (i["w_up_nsa_2"][0][heads], i["w_up_moba_2"][0])]
    tiles.append(np.stack(ups, axis=1).reshape(8, P, 1024))
    tiles.append(_columns(i["w_out_2"][0]))
    f = i["w_ffn_in_2"][0]
    g, u = _columns(f[:, :D_FF]), _columns(f[:, D_FF:])
    tiles.append(np.stack([g, u], axis=1).reshape(2 * FT, P, D))
    tiles.append(i["w_ffn_out_2"][0].reshape(FT, P, D))
    tiles.append(_columns(i["w_ple_gate_2"][0]))
    tiles.append(i["w_ple_proj_2"][0].reshape(2, P, 2, 4, P).transpose(2, 1, 3, 0, 4).reshape(2, P, 1024))
    a = {"stream": np.concatenate(tiles)}
    assert a["stream"].shape == (TILES, P, 1024), a["stream"].shape

    a["x"], a["ctx"] = _feat(i["x"][0]), _feat(i["ctx"][0])
    a["cond"] = np.stack([_vec(i["c"][0]), _vec(i["c_ctx"])], axis=2)
    a["lambda"] = np.broadcast_to(i["da_lambda"], (P,) + i["da_lambda"].shape)
    for l in range(DEPTH):
        a[f"ada_b{l}"], a[f"norm_pre{l}"], a[f"norm_post{l}"] = _vec(i["ada_b"][l]), _vec(i["norm_pre"][l]), _vec(i["norm_post"][l])
        a[f"subln{l}"] = i["da_subln"][l][:, None]
        a[f"hy_w1{l}"], a[f"hy_w2{l}"], a[f"hy_w3{l}"] = i["hy_f_w1"][l], i["hy_f_w2"][l], i["hy_f_w3"][l]
        a[f"hy_b1{l}"], a[f"hy_b2{l}"] = i["hy_f_b1"][l][:, None], i["hy_f_b2"][l][:, None]
        a[f"hy_freq{l}"] = i["hy_f_freq"][l].T
        a[f"hy_sw{l}"] = np.stack([_vec(r) for r in (*i["hy_short_w"][l], i["hy_short_b"][l])], axis=2)
        a[f"hy_bias{l}"] = _vec(i["hy_bias"][l])
        a[f"ln_g{l}"], a[f"ln_b{l}"] = (np.broadcast_to(i[n][l], (P, BR)) for n in ("gm_ln_g", "gm_ln_b"))
        a[f"gm_ws{l}"] = i["gm_ws"][l].transpose(2, 0, 1)
        a[f"gm_bs{l}"] = np.repeat(i["gm_bs"][l], 64, axis=0).reshape(4, P, P).transpose(1, 0, 2)
    a["pos"] = np.broadcast_to(i["positions_2"], (P, TOK))
    a["ple"] = _feat(i["p_2"][0, 0]).reshape(P, 2 * TOK)
    for n in ("g_mix", "g_ffn", "g_ple"):
        a[n] = _vec(i[n + "_2"][0])
    a["ck_w2"], a["cv_w2"] = (i[n][0].reshape(2, P, 64).transpose(1, 0, 2) for n in ("nsa_ck_w2_2", "nsa_cv_w2_2"))
    a["pe_k"], a["pe_v"] = (i[n][0].reshape(16, P).T for n in ("nsa_pe_k_2", "nsa_pe_v_2"))
    gains = ["nsa_q_gain_2"] * 4 + ["nsa_ks_gain_2", "nsa_kw_gain_2"] + ["moba_q_gain_2"] * 4 + ["moba_k_gain_2"] * 4 + ["nsa_kc_gain_2"]
    a["head_gain"] = np.stack([np.tile(i[n][0], 2) for n in gains], axis=1)

    f = np.float32
    a["ident"] = np.eye(P, dtype=f)
    d = np.arange(P)
    inv = (f(10000.0) ** (-np.arange(16, dtype=f) / f(16))).astype(f)
    t = np.arange(TOK)
    coord = np.where((d[:, None] % 64) < 32, t[None, :] // 64, t[None, :] % 64).astype(f)
    ang = (coord * inv[d % 16][:, None]).astype(f).astype(np.float64)
    a["rope"] = np.stack([np.cos(ang), np.sin(ang)], axis=1).astype(f)

    def rotation(half, width, rotated):
        m = np.zeros((P, P), f)
        for x in range(P):
            if x % 64 < rotated:
                if x % width < half:
                    m[x + half, x] = -1.0
                else:
                    m[x - half, x] = 1.0
        return m
    a["perm1"], a["perm2"] = rotation(16, 32, 64), rotation(8, 16, 16)
    inv2 = (f(500000.0) ** (-np.arange(8, dtype=f) / f(8))).astype(f)
    a["inv_freq"] = np.where(d % 64 < 16, inv2[d % 8], f(0.0)).astype(f)[:, None]
    lt = np.linspace(0.0, 1.0, TOK, dtype=f)[:, None]
    wpos = (f(2.0 * math.pi / TOK) * np.arange(TOK, dtype=f))[:, None]
    bands = np.linspace(1e-4, 15, 16, dtype=f)[None, :]
    bw = (bands * wpos).astype(np.float64)
    a["hy_z"] = np.concatenate([lt, np.cos(bw), -np.sin(bw)], axis=1).astype(f).T
    deltas = np.abs(np.linspace(math.log(1e-2) / 1.5, math.log(1e-2) / 0.3, BR, dtype=f))
    a["hy_decay"] = np.exp((-lt * deltas).astype(np.float64)).astype(f).reshape(2, P, BR).transpose(1, 0, 2)
    w = 2.0 * math.pi * (np.arange(TOK) + 0.5) / 512.0
    c, s = np.cos(w[None, :] * t[:, None]), -np.sin(w[None, :] * t[:, None])
    a["dft"] = np.concatenate([c, s], axis=1).astype(f).reshape(2, P, 512).transpose(1, 0, 2)
    a["idft"] = (np.concatenate([c.T, s.T], axis=0) / TOK).astype(f).reshape(4, P, TOK).transpose(1, 0, 2)
    q, k = np.arange(P)[:, None], np.arange(P)[None, :]
    a["causal"] = np.where(k <= q, 0.0, NEG).astype(f)
    end = np.arange(NCMP) * 16 + 31
    keep = (end[None, None, :] <= (np.arange(P)[:, None, None] + P * np.arange(2)[None, :, None]))
    a["cmp_any"], a["cmp_add"] = keep[:, :, 0].astype(f), np.where(keep | ~keep[:, :, 0:1], 0.0, NEG).astype(f)
    hs = np.zeros((P, 14, 32), f)
    sp = np.zeros((32, 14, P), f)
    for n in range(14):
        for half in range(2):
            hs[half * 64:half * 64 + 64, n, 2 * n + half] = 1.0 / 64
            sp[2 * n + half, n, half * 64:half * 64 + 64] = 1.0
    a["head_sum"], a["head_spread"] = hs, sp
    a["block_mean"] = np.kron(np.eye(2, dtype=f), np.full((64, 64), 1.0 / 64, f))
    return {n: np.ascontiguousarray(x) for n, x in a.items()}


def kernel(**inputs):
    import concourse.bacc as bacc
    from concourse.bass_utils import run_bass_kernel_spmd

    arrays = _layout({n: np.asarray(x) for n, x in inputs.items()})
    nc = bacc.Bacc("TRN2", target_bir_lowering=False, num_devices=1)
    ins = {n: nc.dram_tensor(f"in_{n}", x.shape, mybir.dt.from_np(x.dtype), kind="ExternalInput").ap() for n, x in arrays.items()}
    out = nc.dram_tensor("out", (P, KT, TOK), F32, kind="ExternalOutput").ap()
    program(nc, ins, out)
    r = run_bass_kernel_spmd(nc, [{f"in_{n}": x for n, x in arrays.items()}], core_ids=[0])
    y = r.results[0]["out"]
    return y.transpose(2, 1, 0).reshape(1, TOK, D)
```
